# Optimizing a Trainium2 kernel written in Bass

```python
import math
import jax, jax.numpy as jnp
from jax import lax
import numpy as np

D_MODEL = 1024
BATCH = 1
SEQ = 512
DEPTH = 2
DEC_BATCH = 8
DEC_SEQ = 4
PAST_LEN = 2048
PAGE_SIZE = 128

HEAD_DIM = 64
A_HEADS = 4
B_HEADS = 6
C_HEADS = 6
A_W = A_HEADS * HEAD_DIM
B_W = B_HEADS * HEAD_DIM
C_W = C_HEADS * HEAD_DIM
MIX_W = A_W + B_W + C_W
CHUNK = 128
PATTERNS = ((128, 1), (512, 4), (2048, 16))
MAX_WINDOW = 2048
QBLK = 128
ROT_DIM = HEAD_DIM // 4
ROPE_THETA = 500000.0
CONV_W = 4
DELTA_CHUNK = 64
N_GROUPS = 4
EXP_PER_GROUP = 8
N_EXPERTS = N_GROUPS * EXP_PER_GROUP
TOP_K = 2
D_EXPERT = 256
MOE_TOKEN_BLOCK = 1024
EPS = 1e-6
PROJ_SIZES = (A_W, A_W, B_W, B_W, B_W, C_W, C_W, C_W, C_W, C_HEADS, C_HEADS)
PROJ_W = 2 * A_W + 3 * B_W + 4 * C_W + 2 * C_HEADS

kernel_name = 'hymba_gmlp_dilated_gdn_hmoe_step'

def rmsnorm(x, g):
    xf = x.astype(jnp.float32)
    y = xf * lax.rsqrt(jnp.mean(xf * xf, axis=-1, keepdims=True) + EPS)
    return (y * g.astype(jnp.float32)).astype(x.dtype)

def layernorm(x, g):
    xf = x.astype(jnp.float32)
    xc = xf - jnp.mean(xf, axis=-1, keepdims=True)
    y = xc * lax.rsqrt(jnp.mean(xc * xc, axis=-1, keepdims=True) + EPS)
    return (y * g.astype(jnp.float32)).astype(x.dtype)

def l2norm(x):
    return x * lax.rsqrt(jnp.sum(x * x, axis=-1, keepdims=True) + EPS)

def split_cols(p):
    parts, start = [], 0
    for size in PROJ_SIZES:
        parts.append(p[..., start:start + size])
        start += size
    return parts

def partial_rope(x, pos):
    half = ROT_DIM // 2
    inv_freq = jnp.power(ROPE_THETA, -jnp.arange(0, ROT_DIM, 2, dtype=jnp.float32) / ROT_DIM)
    ang = pos.astype(jnp.float32)[:, None] * inv_freq[None, :]
    cos = jnp.cos(ang)[:, None, :].astype(x.dtype)
    sin = jnp.sin(ang)[:, None, :].astype(x.dtype)
    x1, x2 = x[..., :half], x[..., half:ROT_DIM]
    return jnp.concatenate([x1 * cos - x2 * sin, x2 * cos + x1 * sin, x[..., ROT_DIM:]], axis=-1)

def chunk_mlp(u, v, gain, ws, bs):
    bx, t, _ = v.shape
    vn = layernorm(v, gain)
    length = CHUNK if t % CHUNK == 0 else t
    n = t // length
    mask = jnp.tril(jnp.ones((length, length), dtype=bool))
    w = jnp.where(mask[None], ws[:, :length, :length], 0).astype(v.dtype)
    vc = vn.reshape(bx, n, length, A_HEADS, HEAD_DIM)
    s = jnp.einsum('hpq,bcqhd->bcphd', w, vc) + bs[:, :length].T.astype(v.dtype)[None, None, :, :, None]
    return u * s.reshape(bx, t, A_W), vn

def dilated_attention(q, k, v, q_idx):
    scale = HEAD_DIM ** -0.5
    outs, lses = [], []
    for window, dil in PATTERNS:
        offs = jnp.arange(window // dil + 1, dtype=jnp.int32) * dil
        idx = q_idx[:, None] - offs[None, :]
        valid = idx >= 0
        idx = jnp.maximum(idx, 0)
        kg = k[:, idx]
        vg = v[:, idx]
        s = jnp.einsum('bqhd,bqmhd->bhqm', q, kg).astype(jnp.float32) * scale
        s = jnp.where(valid[None, None], s, -jnp.inf)
        m = jnp.max(s, axis=-1, keepdims=True)
        e = jnp.exp(s - m)
        den = jnp.sum(e, axis=-1, keepdims=True)
        outs.append(jnp.einsum('bhqm,bqmhd->bqhd', (e / den).astype(v.dtype), vg))
        lses.append((m + jnp.log(den))[..., 0])
    wts = jax.nn.softmax(jnp.stack(lses, axis=0), axis=0)
    wts = jnp.transpose(wts, (0, 1, 3, 2))[..., None].astype(v.dtype)
    return jnp.sum(wts * jnp.stack(outs, axis=0), axis=0)

def dilated_attention_blocked(q, k, v, q_idx):
    bx, tq, h, hd = q.shape
    blk = QBLK if tq % QBLK == 0 else tq
    nb = tq // blk
    qb = jnp.transpose(q.reshape(bx, nb, blk, h, hd), (1, 0, 2, 3, 4))
    ib = q_idx.reshape(nb, blk)
    ob = lax.map(lambda a: dilated_attention(a[0], k, v, a[1]), (qb, ib))
    return jnp.transpose(ob, (1, 0, 2, 3, 4)).reshape(bx, tq, h, hd)

def short_conv(x_new, buf, w):
    t = x_new.shape[1]
    xp = jnp.concatenate([buf.astype(x_new.dtype), x_new], axis=1)
    out = xp[:, 0:t] * w[0]
    for j in range(1, CONV_W):
        out = out + xp[:, j:j + t] * w[j]
    return jax.nn.silu(out), xp[:, -(CONV_W - 1):]

def gated_delta(q, k, v, g, beta, s0, chunk):
    bx, t, h, dk = q.shape
    dv = v.shape[-1]
    n = t // chunk

    def blocks(a):
        a = a.reshape((bx, n, chunk) + a.shape[2:])
        return jnp.moveaxis(jnp.moveaxis(a, 1, 0), 2, 3)

    qb, kb, vb, gb, bb = blocks(q), blocks(k), blocks(v), blocks(g), blocks(beta)
    cg = jnp.cumsum(gb, axis=-1)
    pos = jnp.arange(chunk)
    incl = pos[:, None] >= pos[None, :]
    strict = pos[:, None] > pos[None, :]
    decay = jnp.exp(jnp.where(incl, cg[..., :, None] - cg[..., None, :], -jnp.inf))
    a_mat = jnp.where(strict, bb[..., :, None] * jnp.einsum('...id,...jd->...ij', kb, kb) * decay, 0.0)
    rhs = jnp.concatenate([bb[..., None] * vb, (bb * jnp.exp(cg))[..., None] * kb], axis=-1)
    sol = lax.linalg.triangular_solve(a_mat + jnp.eye(chunk, dtype=jnp.float32), rhs,
                                      left_side=True, lower=True, unit_diagonal=True)
    u_c, w_c = sol[..., :dv], sol[..., dv:]
    attn = jnp.einsum('...id,...jd->...ij', qb, kb) * decay
    q_dec = qb * jnp.exp(cg)[..., None]
    k_dec = kb * jnp.exp(cg[..., -1:] - cg)[..., None]
    g_tot = jnp.exp(cg[..., -1])

    def step(s, inp):
        uu, ww, aa, qd, kd, gt = inp
        u_p = uu - jnp.einsum('bhcd,bhde->bhce', ww, s)
        o = jnp.einsum('bhcd,bhde->bhce', qd, s) + jnp.einsum('bhij,bhje->bhie', aa, u_p)
        s = gt[..., None, None] * s + jnp.einsum('bhcd,bhce->bhde', kd, u_p)
        return s, o

    s_fin, o = lax.scan(step, s0, (u_c, w_c, attn, q_dec, k_dec, g_tot))
    o = jnp.moveaxis(jnp.moveaxis(o, 3, 2), 0, 1).reshape(bx, t, h, dv)
    return o, s_fin

def expert_mix(t, gates, w1, w3, w2):
    hid = jax.nn.silu(jnp.einsum('nd,edf->nef', t, w1)) * jnp.einsum('nd,edf->nef', t, w3)
    return jnp.einsum('nef,efd->nd', hid * gates[..., None], w2)

def hier_moe(x, w_group, w_router, w1, w3, w2):
    shp = x.shape
    t = x.reshape(-1, shp[-1])
    n = t.shape[0]
    g_prob = jax.nn.softmax((t @ w_group).astype(jnp.float32), axis=-1)
    g_w, g_idx = lax.top_k(g_prob, 1)
    e_logits = (t @ w_router).astype(jnp.float32).reshape(n, N_GROUPS, EXP_PER_GROUP)
    e_logits = jnp.take_along_axis(e_logits, g_idx[:, :, None], axis=1)[:, 0]
    top_p, top_i = lax.top_k(jax.nn.softmax(e_logits, axis=-1), TOP_K)
    top_p = top_p / jnp.sum(top_p, axis=-1, keepdims=True)
    gates = g_w * top_p
    eidx = g_idx * EXP_PER_GROUP + top_i
    dense = jnp.sum(jax.nn.one_hot(eidx, N_EXPERTS, dtype=jnp.float32) * gates[..., None], axis=1)
    dense = dense.astype(t.dtype)
    blk = MOE_TOKEN_BLOCK if n % MOE_TOKEN_BLOCK == 0 else n
    y = lax.map(lambda a: expert_mix(a[0], a[1], w1, w3, w2),
                (t.reshape(n // blk, blk, shp[-1]), dense.reshape(n // blk, blk, N_EXPERTS)))
    return y.reshape(shp)

def decoder_layer(x, pos0, kbuf, vbuf, conv_buf, s0, norm1_g, w_in, a_vnorm_g, a_ws, a_bs,
                  c_conv_w, c_a_log, c_dt_bias, c_norm_g, w_out, norm2_g,
                  w_group, w_router, w1, w3, w2):
    bx, t, _ = x.shape
    h = rmsnorm(x, norm1_g)
    au, av, bq, bk, bv, cq, ck, cv, cz, cb, ca = split_cols(h @ w_in)

    out_a, a_rows = chunk_mlp(au, av, a_vnorm_g, a_ws, a_bs)

    pos = pos0 + jnp.arange(t, dtype=jnp.int32)
    q = partial_rope(bq.reshape(bx, t, B_HEADS, HEAD_DIM), pos)
    k_new = partial_rope(bk.reshape(bx, t, B_HEADS, HEAD_DIM), pos)
    v_new = bv.reshape(bx, t, B_HEADS, HEAD_DIM)
    k_all = jnp.concatenate([kbuf.astype(x.dtype), k_new], axis=1)
    v_all = jnp.concatenate([vbuf.astype(x.dtype), v_new], axis=1)
    q_idx = kbuf.shape[1] + jnp.arange(t, dtype=jnp.int32)
    out_b = dilated_attention_blocked(q, k_all, v_all, q_idx).reshape(bx, t, B_W)
    keep = min(MAX_WINDOW, t)

    qkv, conv_state = short_conv(jnp.concatenate([cq, ck, cv], axis=-1), conv_buf, c_conv_w)
    qkv = qkv.astype(jnp.float32).reshape(bx, t, 3, C_HEADS, HEAD_DIM)
    qc = l2norm(qkv[:, :, 0]) * (HEAD_DIM ** -0.5)
    kc = l2norm(qkv[:, :, 1])
    vc = qkv[:, :, 2]
    beta = jax.nn.sigmoid(cb.astype(jnp.float32))
    g = -jnp.exp(c_a_log.astype(jnp.float32)) * jax.nn.softplus(ca.astype(jnp.float32) + c_dt_bias.astype(jnp.float32))
    chunk = DELTA_CHUNK if t % DELTA_CHUNK == 0 else t
    o, s_new = gated_delta(qc, kc, vc, g, beta, s0.astype(jnp.float32), chunk)
    o = o * lax.rsqrt(jnp.mean(o * o, axis=-1, keepdims=True) + EPS) * c_norm_g.astype(jnp.float32)
    o = o * jax.nn.silu(cz.astype(jnp.float32).reshape(bx, t, C_HEADS, HEAD_DIM))
    out_c = o.reshape(bx, t, C_W).astype(x.dtype)

    x = x + jnp.concatenate([out_a, out_b, out_c], axis=-1) @ w_out
    x = x + hier_moe(rmsnorm(x, norm2_g), w_group, w_router, w1, w3, w2)
    return x, (k_new[:, -keep:], v_new[:, -keep:], a_rows, conv_state, s_new.astype(s0.dtype))

def setup_inputs(seed: int = 0) -> dict:
    key = jax.random.key(seed)
    ks = jax.random.split(key, 24)
    f32 = jnp.float32
    win_rows = min(MAX_WINDOW, PAST_LEN)

    def nrm(k, shape, scale):
        return jax.random.normal(k, shape, f32) * scale

    dt = jnp.exp(jax.random.uniform(ks[13], (DEPTH, C_HEADS), f32, math.log(1e-3), math.log(1e-1)))
    return {
        'x_prompt': nrm(ks[0], (BATCH, SEQ, D_MODEL), 1.0),
        'x_sample': nrm(ks[1], (DEC_BATCH, DEC_SEQ, D_MODEL), 1.0),
        'cache_win_k': nrm(ks[2], (DEPTH, DEC_BATCH, win_rows, B_HEADS, HEAD_DIM), 1.0),
        'cache_win_v': nrm(ks[3], (DEPTH, DEC_BATCH, win_rows, B_HEADS, HEAD_DIM), 1.0),
        'state_conv': nrm(ks[4], (DEPTH, DEC_BATCH, CONV_W - 1, 3 * C_W), 1.0),
        'state_delta': nrm(ks[5], (DEPTH, DEC_BATCH, C_HEADS, HEAD_DIM, HEAD_DIM), 0.1),
        'norm1_g': 1.0 + nrm(ks[6], (DEPTH, D_MODEL), 0.1),
        'w_in': nrm(ks[7], (DEPTH, D_MODEL, PROJ_W), D_MODEL ** -0.5),
        'a_vnorm_g': 1.0 + nrm(ks[8], (DEPTH, A_W), 0.1),
        'a_ws': nrm(ks[9], (DEPTH, A_HEADS, CHUNK, CHUNK), CHUNK ** -0.5),
        'a_bs': 1.0 + nrm(ks[10], (DEPTH, A_HEADS, CHUNK), 0.1),
        'c_conv_w': nrm(ks[11], (DEPTH, CONV_W, 3 * C_W), 0.5),
        'c_a_log': jnp.log(jax.random.uniform(ks[12], (DEPTH, C_HEADS), f32, 1.0, 16.0)),
        'c_dt_bias': dt + jnp.log(-jnp.expm1(-dt)),
        'c_norm_g': 1.0 + nrm(ks[14], (DEPTH, HEAD_DIM), 0.1),
        'w_out': nrm(ks[15], (DEPTH, MIX_W, D_MODEL), MIX_W ** -0.5),
        'norm2_g': 1.0 + nrm(ks[16], (DEPTH, D_MODEL), 0.1),
        'w_group': nrm(ks[17], (DEPTH, D_MODEL, N_GROUPS), D_MODEL ** -0.5),
        'w_router': nrm(ks[18], (DEPTH, D_MODEL, N_EXPERTS), D_MODEL ** -0.5),
        'w1': nrm(ks[19], (DEPTH, N_EXPERTS, D_MODEL, D_EXPERT), D_MODEL ** -0.5),
        'w3': nrm(ks[20], (DEPTH, N_EXPERTS, D_MODEL, D_EXPERT), D_MODEL ** -0.5),
        'w2': nrm(ks[21], (DEPTH, N_EXPERTS, D_EXPERT, D_MODEL), D_EXPERT ** -0.5),
        'final_g': 1.0 + nrm(ks[22], (D_MODEL,), 0.1),
    }

def reference(x_prompt, x_sample, cache_win_k, cache_win_v, state_conv, state_delta,
              norm1_g, w_in, a_vnorm_g, a_ws, a_bs, c_conv_w, c_a_log, c_dt_bias, c_norm_g,
              w_out, norm2_g, w_group, w_router, w1, w3, w2, final_g):
    dtype = x_prompt.dtype
    bp = x_prompt.shape[0]
    kbuf_p = jnp.zeros((bp, 0, B_HEADS, HEAD_DIM), dtype)
    conv_p = jnp.zeros((bp, CONV_W - 1, 3 * C_W), dtype)
    s_p = jnp.zeros((bp, C_HEADS, HEAD_DIM, HEAD_DIM), jnp.float32)
    xp, xs = x_prompt, x_sample
    kp_l, vp_l, cp_l, dp_l = [], [], [], []
    ks_l, vs_l, as_l, cs_l, ds_l = [], [], [], [], []
    for l in range(DEPTH):
        lw = (norm1_g[l], w_in[l], a_vnorm_g[l], a_ws[l], a_bs[l], c_conv_w[l], c_a_log[l],
              c_dt_bias[l], c_norm_g[l], w_out[l], norm2_g[l], w_group[l], w_router[l],
              w1[l], w3[l], w2[l])
        xp, (kr, vr, _, cs, sn) = decoder_layer(xp, 0, kbuf_p, kbuf_p, conv_p, s_p, *lw)
        kp_l.append(kr); vp_l.append(vr); cp_l.append(cs); dp_l.append(sn)
        xs, (kr, vr, ar, cs, sn) = decoder_layer(xs, PAST_LEN, cache_win_k[l], cache_win_v[l],
                                                 state_conv[l], state_delta[l], *lw)
        ks_l.append(kr); vs_l.append(vr); as_l.append(ar); cs_l.append(cs); ds_l.append(sn)
    y_prompt = rmsnorm(xp, final_g)
    y_sample = rmsnorm(xs, final_g)
    win_k_prompt = jnp.stack(kp_l)
    win_v_prompt = jnp.stack(vp_l)
    conv_prompt = jnp.stack(cp_l)
    delta_prompt = jnp.stack(dp_l)
    win_k_sample = jnp.stack(ks_l)
    win_v_sample = jnp.stack(vs_l)
    chunk_v_sample = jnp.stack(as_l)
    conv_sample = jnp.stack(cs_l)
    delta_sample = jnp.stack(ds_l)
    return (y_prompt, y_sample, win_k_prompt, win_v_prompt, conv_prompt, delta_prompt,
            win_k_sample, win_v_sample, chunk_v_sample, conv_sample, delta_sample)


_drawn_inputs = setup_inputs


def setup_inputs(seed=0):
    import zlib

    import numpy as np

    out = dict(_drawn_inputs(seed))
    spreads = {}
    factors = {}
    for name, (base, spread) in spreads.items():
        noise = np.random.default_rng([zlib.crc32(name.encode()), seed]).standard_normal(out[name].shape)
        drawn = base * np.exp(spread * noise) if base else spread * noise
        out[name] = __import__('jax').numpy.asarray(drawn.astype(out[name].dtype))
    for name, factor in factors.items():
        out[name] = (out[name] * factor).astype(out[name].dtype)
    return out
```

```python
from contextlib import ExitStack

import numpy as np
import concourse.bass as bass
from concourse import mybir

F32 = mybir.dt.float32
U32 = mybir.dt.uint32
I32 = mybir.dt.int32
ALU = mybir.AluOpType
ACT = mybir.ActivationFunctionType
AX = mybir.AxisListType.X

DEPTH, D, SEQ, DB, DS, PAST = 2, 1024, 512, 8, 4, 2048
NP, KT = SEQ // 128, D // 128
NT = NP + 1
NS = DB * DS
NTOK = SEQ + NS
HD, AH, BH, CH = 64, 4, 6, 6
AW, BW, CW = AH * HD, BH * HD, CH * HD
PROJ = 2 * AW + 3 * BW + 4 * CW + 2 * CH
CONV0 = 2 * AW + 3 * BW
CCH = 3 * CW
NCT = CCH // 128
NE, NG, DE, CAP = 32, 4, 256, 64
EPS = 1e-6
NEG = -1e30
SCALE = HD ** -0.5
ROWS = [128] * NP + [NS]
AU, AV, BQ, BK, BV, CZ, CB = 0, AW, 2 * AW, 2 * AW + BW, 2 * AW + 2 * BW, 2 * AW + 3 * BW, 2 * AW + 3 * BW + CW
PW = CB + 2 * CH
MIXCOL = [AU, AU + 128, BQ, BQ + 128, BQ + 256, CZ, CZ + 128, CZ + 256]
SLOT = 6144
WIN = 2048
NDIL = (WIN - 512) // 16


def constants():
    t = {}
    i = np.arange(128)
    blk, loc, col = i // 64, i % 64, np.arange(64)
    f = np.float32
    same = blk[:, None] == blk[None, :]
    t["ident"] = np.eye(128)
    t["le"] = same & (i[:, None] <= i[None, :])
    t["gt"] = same & (i[:, None] > i[None, :])
    t["ch0"] = np.broadcast_to((blk == 0)[:, None], (128, 128))
    t["ch1"] = np.broadcast_to((blk == 1)[:, None], (128, 128))
    t["gtc"] = loc[:, None] > col[None, :]
    t["lec"] = loc[:, None] <= col[None, :]
    t["idc"] = loc[:, None] == col[None, :]
    b16 = loc[:, None] // 16 == col[None, :] // 16
    b32 = loc[:, None] // 32 == col[None, :] // 32
    t["nlow16"] = -1.0 * (t["gtc"] & b16)
    t["nup16"] = -1.0 * ((loc[:, None] < col[None, :]) & b16)
    t["low32"] = t["gtc"] & b32 & ~b16
    t["low64"] = t["gtc"] & ~b32
    j = np.arange(NS)
    sb = j[:, None] // DS == j[None, :] // DS
    t["le4"] = sb & (j[:, None] <= j[None, :])
    t["gt4"] = sb & (j[:, None] > j[None, :])
    t["nlow4"] = -1.0 * t["gt4"]
    t["nup4"] = -1.0 * (sb & (j[:, None] < j[None, :]))
    t["same4"] = sb
    t["rowseq"] = (np.arange(64)[:, None] % NS) // DS == np.arange(DB)[None, :]
    t["rep4"] = np.arange(DS)[:, None] == j[None, :] % DS
    t["ones"] = np.ones((128, 128))
    t["before"] = i[:, None] < i[None, :]
    t["upto"] = i[:, None] <= i[None, :]
    t["expert"] = np.broadcast_to(np.arange(NE), (128, NE))
    t["group"] = np.broadcast_to(np.arange(NE) // 8, (128, NE))
    t["spare"] = NE * CAP + i[:, None] + 128 * np.arange(2 * NT)[None, :]

    def logmult(delta, scale):
        m = ((delta >= 0) & (delta <= 128)) * 1
        m = m + ((delta >= 0) & (delta <= 512) & (delta % 4 == 0)) + ((delta >= 0) & (delta <= 2048) & (delta % 16 == 0))
        return np.where(m > 0, np.log(np.maximum(m, 1)) / scale, NEG)

    t["pmask"] = logmult(i[:, None] + 384 - np.arange(512)[None, :], SCALE)
    r = i % 32
    s = r % DS
    kd = np.concatenate([16 * np.arange(NDIL) + a for a in range(4)])
    kr = np.concatenate([WIN - 512 + 4 * np.arange(128) + a for a in range(4)])
    sm = logmult(WIN + s[:, None] - np.concatenate([kd, kr])[None, :], SCALE)
    new = []
    for g in range(2):
        own = (4 * g + i // 32)[:, None] == (j // DS)[None, :]
        m = np.where(own, logmult(s[:, None] - (j % DS)[None, :], SCALE), NEG)
        new.append(m)
    sm = np.concatenate([sm] + new, 1)
    sm[r >= BH * DS] = 0.0
    t["smask"] = sm
    inv = 500000.0 ** (-np.arange(0, 16, 2) / 16.0)
    inv = np.power(f(500000.0), (-np.arange(0, 16, 2, dtype=f) / f(16))).astype(f)
    pos = np.zeros((128, NT), f)
    for q in range(NP):
        pos[:, q] = 128 * q + i
    pos[:NS, NP] = PAST + j % DS
    ang = (pos[:, :, None] * inv[None, None, :]).astype(f)
    t["cos"] = np.cos(ang.astype(np.float64)).reshape(128, -1)
    t["sin"] = np.sin(ang.astype(np.float64)).reshape(128, -1)
    at, parts, n = {}, [], 0
    for k, v in t.items():
        v = np.asarray(v, f)
        at[k] = (n, v.shape[0], v.shape[1])
        full = np.zeros((128, v.shape[1]), f)
        full[: v.shape[0]] = v
        parts.append(full)
        n += v.shape[1]
    return np.ascontiguousarray(np.concatenate(parts, 1)), at


def schedule():
    a, v = [], []
    a.append(("tapsT",))
    for t in range(NT):
        v += [("norm1", t, 0), ("norm1", t, 1)]
    for i in range(NCT + 2):
        if i < NCT:
            a += [("convP", i), ("convS", i)]
        if i >= 2:
            v += [("qkvP", i - 2), ("qkvS", i - 2)]
    v += [("tail", i) for i in range(3)]
    for piece in "ABC":
        for t in range(NT):
            a += [(piece, t, 0), (piece, t, 1)]
    v += [("wsT",), ("rep",), ("ws4",)]
    v += [("gate", t) for t in range(NT)]
    for t in range(NT):
        a += [("cg", t), ("D", t), ("DT", t)]
        v += [("qT", t), ("kT", t), ("bT", t), ("AA", t), ("AT0", t), ("AT1", t)]
        a += [("N2", t)]
        v += [("N2T", t)]
        if t < NP:
            a += [("N4", t)]
            v += [("N4T", t)]
        v += [("M1", t)]
        if t < NP:
            a += [("N8", t)]
            v += [("M2", t), ("M3", t)]
            for s in (32, 64):
                a += [("T", t, s), ("Y", t, s)]
                v += [("X", t, s)]
        v += [("u", t)]
        a += [("wT", t, c) for c in range(2 if t < NP else 1)]
        v += [("qdT", t)]
        if t < NP:
            for c in range(2):
                v += [("wS", t, c), ("o", t, c), ("S", t, c)]
        else:
            v += [("wS4", h) for h in range(CH)] + [("oShift",), ("o4",)] + [("S4", h) for h in range(CH)]
    for g in range(3):
        a += [("bq", g), ("bqs", g), ("bk", g), ("bks", g)]
    n = BH * NP
    for i in range(n + 2):
        if i < n:
            v += [("S", i)]
        if 1 <= i <= n:
            a += [("P", i - 1)]
        if i >= 2:
            v += [("O", i - 2)]
    for G in range(2):
        for b in range(4):
            for g in range(3):
                a += [("kd", G, b, g), ("kr", G, b, g)]
        v += [("sd", G), ("sr", G), ("sn", G)]
        v += [("pd", G), ("pr", G), ("pn", G)]
        v += [("ov", G, b) for b in range(4)]
    for t in range(NT):
        a += [("mixT", t, 0), ("mixT", t, 1)]
    for c in range(2):
        for t in range(NT):
            v += [("out", c, t)]
    for t in range(NT):
        v += [("norm2", t, 0), ("norm2", t, 1)]
    v += [("logit", 0), ("rank", 0)]
    return a, v


def build(nc, ins, outs, consts_at, x_lists, y_lists):
    c_dram = ins["consts"]
    ctx = ExitStack()
    with ctx:
        def sb(name, cols, dt=F32, rows=128):
            return ctx.enter_context(nc.sbuf_tensor(name, [rows, cols], dt))

        NCONST = c_dram.shape[1]
        consts = sb("consts", NCONST)
        x = sb("x", NT * D)[:, :].rearrange("p (t d) -> p t d", t=NT)
        hT_raw = sb("hT_raw", KT * NTOK)
        proj_raw = sb("proj_raw", NT * PW)
        ring = sb("ring", 3 * SLOT)
        qkv_raw = sb("qkv_raw", NT * CCH)
        work = sb("work", 12 * CW)
        small = sb("small", 600)
        state = sb("state", CW)[:, :]
        idx = sb("idx", 8 * NT + 4 * NT + 1, U32)
        idx_top, idx_sc, idx_ga = idx[:, 0:40], idx[:, 40:50], idx[:, 50:60]
        idx_cnt = idx[:, 60:61].bitcast(I32)

        hT = hT_raw[:, :].rearrange("p (k n) -> p k n", k=KT)
        proj = proj_raw[:, :].rearrange("p (t n) -> p t n", t=NT)
        qkv = qkv_raw[:, :].rearrange("p (t n) -> p t n", t=NT)

        def const(name):
            n, r, c = consts_at[name]
            return consts[0:r, n:n + c]

        ident = const("ident")

        class Cut:
            def __init__(self, tensor, at=0):
                self.tensor, self.at = tensor, at

            def __call__(self, cols, rows=128):
                self.at += cols
                assert self.at <= self.tensor.shape[1], (self.at, self.tensor.shape)
                return self.tensor[0:rows, self.at - cols:self.at]

        cut = Cut(small)
        g1, g2 = cut(KT), cut(KT)
        c_gain = cut(HD)
        a_log, dt_bias = cut(CH), cut(CH)
        bias_p = cut(AH)
        bias_s = cut(AH)
        w_ba = cut(KT * 12).rearrange("p (k n) -> p k n", k=KT)
        ssq, rstd = cut(NT), cut(NT)
        ln_mean, ln_var = cut(NT), cut(NT)
        gates = cut(NT * 12).rearrange("p (t n) -> p t n", t=NT)
        beta, decay = (cut(NT * CH).rearrange("p (t n) -> p t n", t=NT) for _ in range(2))
        soft = cut(NT * CH).rearrange("p (t n) -> p t n", t=NT)
        ex_cg = cut(60)
        l2 = cut(NT * 12).rearrange("p (t n) -> p t n", t=NT)
        o_ss = cut(CH)
        s_max, s_sum = cut(8), cut(8)

        hst = [qkv_raw[:, D * i:D * i + D] for i in range(2)]
        cut = Cut(work)
        XW = 3 + SEQ + 7 * DB
        cin = [cut(XW + 1)[:, 0:XW] for _ in range(2)]
        acc = [cut(XW) for _ in range(2)]
        sil = [cut(NTOK) for _ in range(2)]
        taps = cut(NCT * 28).rearrange("p (c n) -> p c n", c=NCT)
        tail = cut(NCT * 27).rearrange("p (c n) -> p c n", c=NCT)
        tail_rows = proj_raw[0:27, NP * PW + BK:NP * PW + BK + CCH]
        state_rows = proj_raw[0:28, 0:CCH]
        zeros = proj_raw[:, 5 * D:6 * D]
        g_final = proj_raw[:, 0:D]
        cut = Cut(work)
        ln_sq = cut(NP * AW).rearrange("p (t n) -> p t n", t=NP)
        ws_raw = cut(AH * 128).rearrange("p (h n) -> p h n", h=AH)
        wsT = cut(AH * 128).rearrange("p (h n) -> p h n", h=AH)
        rep_w = cut(AH * NS, DS)
        ws4 = cut(AH * NS, NS).rearrange("p (h n) -> p h n", h=AH)
        v_gain = cut(AW)
        rope_t = [cut(NP * 96) for _ in range(4)]
        c1, c2 = Cut(work), Cut(hT_raw)
        N_, NT_, U_, T_, Y_, aT_, kb_, rw_, qd_, kd_, N2_, N2T_ = (c1(CW) for _ in range(12))
        Sp_ = state
        BIG_ = work[:, 3 * CW:3 * CW + DB * HD]
        A32_, A64_, N4_, N4T_ = (c2(CW) for _ in range(4))
        S4_ = hT_raw[:, 0:3 * DB * HD]
        E_, ET_ = (c2(CW) for _ in range(2))
        KZ_ = c2(CH * 128).rearrange("p (h n) -> p h n", h=CH)
        KQ_ = c2(2 * CW)
        Sg_ = c2(CW)
        gt4_ = c2(CH * DB)
        cut = Cut(hT_raw)
        qTb = [cut(NTOK) for _ in range(3)]
        kTb = [cut(NTOK) for _ in range(3)]
        cut = Cut(qkv_raw)
        prob = [cut(SEQ) for _ in range(2)]
        probT = [cut(SEQ) for _ in range(2)]
        keysT = [cut(896) for _ in range(2)]
        cut = Cut(work)
        sprob = cut(928)
        spd, spr, spn = cut(512), cut(512), cut(128)
        qblk = cut(DB * 3 * 32).rearrange("p (b g n) -> p b g n", b=DB, g=3)
        a_max, a_sum = cut(BH * NP), cut(BH * NP)
        o4T = cut(3 * NS).rearrange("p (g n) -> p g n", g=3)
        cut = Cut(proj_raw)
        h2 = cut(NT * D).rearrange("p (t d) -> p t d", t=NT)
        rows_in = [proj_raw[0:CAP, D * i:D * i + D] for i in range(3)]
        rows_out = [cut(D // 2) for _ in range(3)]
        hidT = [cut(128) for _ in range(2)]
        rowsT = [cut(KT * CAP) for _ in range(2)]
        got = [proj_raw[:, D * i:D * i + D] for i in range(4)]
        w_route = qkv_raw[:, 3840:3840 + KT * 36].rearrange("p (k n) -> p k n", k=KT)
        junk1, junk2 = qkv_raw[:, 2 * D:3 * D], qkv_raw[:, 2 * D:3 * D]
        cut = Cut(qkv_raw)
        hid = [cut(128) for _ in range(2)]
        gate_act = [cut(128) for _ in range(2)]
        logit = cut(NT * 36).rearrange("p (t n) -> p t n", t=NT)
        glog = cut(NT * 8).rearrange("p (t n) -> p t n", t=NT)
        top = cut(NT * 8).rearrange("p (t n) -> p t n", t=NT)
        el, em, rk, m0, m1, msum = (cut(NT * NE).rearrange("p (t n) -> p t n", t=NT) for _ in range(6))
        over_gate = cut(NT * NE).rearrange("p (t n) -> p t n", t=NT)
        gi, ga, gb, e0, e1, r0, r1, o0, o1, p0, p1, w0, w1_, tq = (cut(NT) for _ in range(14))
        counts = cut(NE + 2)
        assert cut.at <= 2 * D
        fb_w = proj_raw[:, 0:SLOT]
        fb_hid = proj_raw[:, SLOT:SLOT + 2 * NTOK].rearrange("p (f n) -> p f n", f=2)
        fb_act = proj_raw[:, SLOT + 2 * NTOK:SLOT + 4 * NTOK].rearrange("p (f n) -> p f n", f=2)

        psum = [ctx.enter_context(nc.psum_tensor(f"bank{i}", [128, 512], F32)) for i in range(8)]

        keep = {}

        def lasting(name):
            keep[name] = ctx.enter_context(nc.semaphore(name))
            return keep[name]

        consts_loaded = lasting("consts_loaded")
        x_loaded = lasting("x_loaded")
        zeros_ready = lasting("zeros_ready")
        slot_full = [lasting(f"slot_full{i}") for i in range(3)]
        small_set = lasting("small_set")
        pool_stored = lasting("pool_stored")
        scattered = lasting("scattered")
        gathered = [lasting(f"gathered{i}") for i in range(4)]
        rows_loaded = [lasting(f"rows_loaded{i}") for i in range(3)]
        rows_stored = [lasting(f"rows_stored{i}") for i in range(3)]
        per_buffer = [len(range(i, NE, 3)) for i in range(3)]
        layer_left = lasting("layer_left")
        layer_cleared = lasting("layer_cleared")
        aside = lasting("aside")
        y_stored = lasting("y_stored")
        fin_row = lasting("fin_row")
        fin_step = lasting("fin_step")
        fin_gain = lasting("fin_gain")
        cleared = []

        def signal(name):
            cleared.append(ctx.enter_context(nc.semaphore(name)))
            return cleared[-1]

        act_filled, act_drained = signal("act_filled"), signal("act_drained")
        vec_filled, vec_drained = signal("vec_filled"), signal("vec_drained")
        vec_step, act_step = signal("vec_step"), signal("act_step")
        params_loaded = signal("params_loaded")
        taps_loaded = signal("taps_loaded")
        squares_ready = signal("squares_ready")
        root_asked = signal("root_asked")
        root_ready = signal("root_ready")
        rows_ready = signal("rows_ready")
        conv_in = signal("conv_in")
        conv_done = signal("conv_done")
        silu_done = signal("silu_done")
        tail_copied = signal("tail_copied")
        tail_stored = signal("tail_stored")
        mlp_params = signal("mlp_params")
        vn_ready = signal("vn_ready")
        rope_done = signal("rope_done")
        z_ready = signal("z_ready")
        gate_asked, gate_got = signal("gate_asked"), signal("gate_got")
        delta_in = signal("delta_in")
        delta_w = signal("delta_w")
        delta_state = signal("delta_state")
        state_loaded = signal("state_loaded")
        state_stored = signal("state_stored")
        expand_ready = signal("expand_ready")
        keys_used = signal("keys_used")
        sprob_asked, sprob_got = signal("sprob_asked"), signal("sprob_got")
        mix_ready = signal("mix_ready")
        probs_asked, probs_ready = signal("probs_asked"), signal("probs_ready")
        qblk_ready = signal("qblk_ready")
        sprob_ready = signal("sprob_ready")
        route_loaded = signal("route_loaded")
        route_asked, route_got = signal("route_asked"), signal("route_got")
        masks_ready = signal("masks_ready")
        index_ready = signal("index_ready")
        act_gated, hid_ready = signal("act_gated"), signal("hid_ready")
        got_used = signal("got_used")
        moe_done = signal("moe_done")
        fb_loaded, fb_up, fb_silu, fb_prod, fb_down, fb_added = (
            signal(n) for n in ("fb_loaded", "fb_up", "fb_silu", "fb_prod", "fb_down", "fb_added"))
        clear_range = range(min(s.num for s in cleared), max(s.num for s in cleared) + 1)
        assert not any(s.num in clear_range for s in keep.values())

        a_jobs, v_jobs = schedule()
        A_AT = {k: i for i, k in enumerate(a_jobs)}
        V_AT = {k: i for i, k in enumerate(v_jobs)}
        assert len(A_AT) == len(a_jobs) and len(V_AT) == len(v_jobs)
        A0, V0 = len(a_jobs), len(v_jobs)
        STORES = 7
        EUN = 6
        ELOOP = NE // EUN * EUN

        def a_bank(n):
            return psum[n % 4]

        def v_bank(n):
            return psum[4 + n % 4]

        def hd(ap, n=CH):
            return ap.rearrange("p (h n) -> p h n", h=n)

        def mid(ap, n):
            return ap[:, None, :].broadcast_to([ap.shape[0], n, ap.shape[1]])

        def inner(ap, n):
            return ap[:, :, None].broadcast_to([ap.shape[0], ap.shape[1], n])

        w_in, w_out = ins["w_in"], ins["w_out"]

        def layer_of(ap, L):
            names = "abcdefg"[:len(ap.shape) - 1]
            pat = " ".join(names)
            return ap[bass.ds(L, 1)].rearrange(f"o {pat} -> (o {names[0]}) {pat[2:]}" if len(names) > 1 else "o a -> (o a)")

        def win_cols(L, slot, at, c0, n):
            src = layer_of(w_in, L).rearrange("(p k) n -> p k n", k=KT)[:, :, c0:c0 + n]
            dst = ring[:, slot * SLOT + at:slot * SLOT + at + KT * n].rearrange("p (k n) -> p k n", k=KT)
            return dst, src

        def load_list():
            out = []
            for i in range(3):
                out.append(lambda L, s, i=i: [win_cols(L, s, 0, CONV0 + 384 * i, 384)])
            out.append(lambda L, s: [win_cols(L, s, 0, 0, 512)])
            out.append(lambda L, s: [win_cols(L, s, 0, BQ, 768)])
            out.append(lambda L, s: [win_cols(L, s, 0, BV, 384), win_cols(L, s, KT * 384, CONV0 + CCH, 384)])

            def cache(which, b0):
                def go(L, s):
                    r = []
                    for i in range(2):
                        src = layer_of(ins[which], L)[b0 + i].rearrange("n h d -> n (h d)")
                        base = s * SLOT + i * 3072
                        r.append((ring[0:NDIL, base:base + 1536],
                                  src[0:WIN - 512].rearrange("(p j) n -> p (j n)", j=16)[:, 0:1536]))
                        r.append((ring[:, base + 1536:base + 3072],
                                  src[WIN - 512:WIN].rearrange("(p j) n -> p (j n)", j=4)))
                    return r
                return go
            for G in range(2):
                for which in ("cache_win_k", "cache_win_v"):
                    for i in range(2):
                        out.append(cache(which, 4 * G + 2 * i))
            for c in range(2):
                def go(L, s, c=c):
                    src = layer_of(w_out, L).rearrange("(k p) n -> p k n", p=128)[:, :, 512 * c:512 * c + 512]
                    return [(ring[:, s * SLOT:s * SLOT + 4096].rearrange("p (k n) -> p k n", k=KT), src)]
                out.append(go)
            return out

        loads = load_list()
        E_AT = len(loads)
        NLOAD = E_AT + NE
        assert NLOAD % 3 == 0 and E_AT % 3 + 0 == 1
        ndma = [1, 1, 1, 1, 1, 2] + [4] * 8 + [1, 1] + [3] * NE
        full_at = []
        per = [0, 0, 0]
        for n in range(NLOAD):
            per[n % 3] += 16 * ndma[n]
            full_at.append(per[n % 3])
        SLOT_TOTAL = per

        def expert_src(L, e):
            w1 = layer_of(ins["w1"], L)[bass.ds(e, 1)].rearrange("o (p k) f -> (o p) (k f)", k=KT)
            w3 = layer_of(ins["w3"], L)[bass.ds(e, 1)].rearrange("o (p k) f -> (o p) (k f)", k=KT)
            w2 = layer_of(ins["w2"], L)[bass.ds(e, 1)].rearrange("o (p f) d -> (o p) (f d)", f=2)
            return w1, w3, w2

        def leave_layer(eng, L, clears=False):
            eng.drain().then_inc(layer_left, 1)
            eng.wait_ge(layer_left, (L + 1) * 5)
            eng.sem_inc(aside, 1)
            if clears:
                eng.sem_clear(clear_range)
                eng.sem_inc(layer_cleared, 1)
            eng.wait_ge(layer_cleared, L + 1)
            eng.sem_inc(aside, 1)

        def state_tile(g):
            return S4_[:, DB * HD * g:DB * HD * (g + 1)].rearrange("p (b v) -> p b v", b=DB)

        def mix_tiles(t, h):
            if t < NP:
                return list(range(4 * h, 4 * h + 4))
            return [0, 1] if h == 0 else [5, 6, 7]

        def dense_loads(sp, L):
            sp.wait_ge(moe_done, 1)
            over = sp.value_load(idx_cnt[0:1, 0:1], min_val=0, max_val=NTOK)
            with sp.If(over > CAP):
                with sp.Fori(0, NE) as e:
                    sp.wait_ge(fb_added, e * NT + 1)
                    sp.sem_inc(aside, 1)
                    for i, src in enumerate(expert_src(L, e)):
                        sp.dma_start(fb_w[:, 2048 * i:2048 * (i + 1)], src).then_inc(fb_loaded, 16)
            sp.sem_inc(aside, 1)

        block = ctx.enter_context(nc.Block())

        @block.sync
        def _(sp):
            sp.wait_ge(small_set, 1)
            sp.dma_start(consts[:, :], c_dram).then_inc(consts_loaded, 16)
            sp.dma_start(x[:, 0:NP, :], ins["x_prompt"].rearrange("b (t p) d -> p (b t) d", p=128)).then_inc(x_loaded, 16)
            sp.dma_start(x[0:NS, NP, :], ins["x_sample"].rearrange("b s d -> (b s) d")).then_inc(x_loaded, 16)

            def used_up(n):
                if n < 3:
                    return act_filled, A_AT[("convS", 3 * n + 2)] + 1
                if n < 6:
                    return act_filled, A_AT[("ABC"[n - 3], NT - 1, 1)] + 1
                if n < 14:
                    G, m = (n - 6) // 4, (n - 6) % 4
                    if m < 2:
                        return act_filled, A_AT[("kr", G, 2 * m + 1, 2)] + 1
                    return vec_filled, V_AT[("ov", G, 2 * m - 3)] + 1
                if n < 16:
                    return vec_filled, V_AT[("out", n - 14, NT - 1)] + 1
                return act_filled, A0 + 2 * (n - 16) + 2

            def stream(L, n, dmas):
                if n >= 3:
                    sp.wait_ge(*used_up(n - 3))
                for dst, src in dmas:
                    sp.dma_start(dst, src).then_inc(slot_full[n % 3], 16)

            with sp.Fori(0, DEPTH) as L:
                lay = {k: layer_of(ins[k], L) for k in ("norm1_g", "norm2_g", "c_norm_g", "c_a_log", "c_dt_bias",
                                                        "state_conv", "c_conv_w", "a_bs", "w_in")}
                for dst, src in ((g1, lay["norm1_g"].rearrange("(p k) -> p k", k=KT)),
                                 (g2, lay["norm2_g"].rearrange("(p k) -> p k", k=KT)),
                                 (c_gain, lay["c_norm_g"][None, :].broadcast_to([128, HD])),
                                 (a_log, lay["c_a_log"][None, :].broadcast_to([128, CH])),
                                 (dt_bias, lay["c_dt_bias"][None, :].broadcast_to([128, CH])),
                                 (w_ba, lay["w_in"].rearrange("(p k) n -> p k n", k=KT)[:, :, PROJ - 12:PROJ])):
                    sp.dma_start(dst, src).then_inc(params_loaded, 16)
                sp.dma_start(state_rows[0:24, :], lay["state_conv"].rearrange("b r c -> (b r) c")).then_inc(taps_loaded, 16)
                sp.dma_start(state_rows[24:28, :], lay["c_conv_w"]).then_inc(taps_loaded, 16)
                for n in range(4):
                    stream(L, n, loads[n](L, n % 3))
                sp.wait_ge(vec_drained, V_AT[("tail", 2)] + 1)
                sp.dma_start(layer_of(outs["conv_prompt"], L).rearrange("b r c -> (b r) c"), tail_rows[0:3, :]).then_inc(tail_stored, 16)
                sp.dma_start(layer_of(outs["conv_sample"], L).rearrange("b r c -> (b r) c"), tail_rows[3:27, :]).then_inc(tail_stored, 16)
                sp.wait_ge(tail_stored, 32)
                sp.dma_start(ws_raw, layer_of(ins["a_ws"], L).rearrange("h p q -> p h q")).then_inc(mlp_params, 16)
                sp.dma_start(v_gain, layer_of(ins["a_vnorm_g"], L)[None, :].broadcast_to([128, AW])).then_inc(mlp_params, 16)
                sp.dma_start(bias_p, lay["a_bs"].rearrange("h p -> p h"), allow_slow_non_contiguous=True).then_inc(mlp_params, 16)
                for n in range(4, 9):
                    stream(L, n, loads[n](L, n % 3))
                sp.wait_ge(vec_drained, V_AT[("X", NP - 1, 64)] + 1)
                for g in range(3):
                    sp.dma_start(state_tile(g), layer_of(ins["state_delta"], L)[:, 2 * g:2 * g + 2].rearrange("b h k v -> (h k) b v")).then_inc(state_loaded, 16)
                sp.wait_ge(vec_drained, V_AT[("S4", CH - 1)] + 1)
                sp.dma_start(w_route[:, :, 0:NG], layer_of(ins["w_group"], L).rearrange("(p k) n -> p k n", k=KT)).then_inc(route_loaded, 16)
                sp.dma_start(w_route[:, :, NG:36], layer_of(ins["w_router"], L).rearrange("(p k) n -> p k n", k=KT)).then_inc(route_loaded, 16)
                for n in range(9, E_AT):
                    stream(L, n, loads[n](L, n % 3))

                def expert_load(e, slot):
                    base = slot * SLOT
                    for i, src in enumerate(expert_src(L, e)):
                        sp.dma_start(ring[:, base + 2048 * i:base + 2048 * (i + 1)], src).then_inc(slot_full[slot], 16)
                for e in range(3):
                    sp.wait_ge(*used_up(E_AT + e - 3))
                    expert_load(e, (E_AT + e) % 3)
                with sp.Fori(0, (NE - 3) // 3) as i:
                    for k in range(3):
                        sp.wait_ge(act_filled, i * 6 + (A0 + 2 * k + 2))
                        sp.sem_inc(aside, 1)
                        expert_load(i * 3 + (3 + k), (E_AT + k) % 3)
                for e in range(3 + (NE - 3) // 3 * 3, NE):
                    sp.wait_ge(*used_up(E_AT + e - 3))
                    expert_load(e, (E_AT + e) % 3)
                dense_loads(sp, L)
                leave_layer(sp, L)
            sp.dma_start(g_final, ins["final_g"][None, :].broadcast_to([128, D])).then_inc(fin_gain, 16)
            sp.wait_ge(fin_row, NT)
            sp.dma_start(outs["y_prompt"].rearrange("b (t p) d -> p (b t) d", p=128), x[:, 0:NP, :]).then_inc(y_stored, 16)
            sp.dma_start(outs["y_sample"].rearrange("b s d -> (b s) d"), x[0:NS, NP, :]).then_inc(y_stored, 16)
            sp.wait_ge(y_stored, 32)

        @block.gpsimd
        def _(pool):
            pool.wait_ge(zeros_ready, 1)
            for i in range(3):
                blocks = 6 if i < 2 else 4
                pool.dma_start(x_lists[768 * i:768 * i + 128 * blocks, :].rearrange("(n p) d -> p n d", p=128),
                               mid(zeros, blocks)).then_inc(rows_stored[i], 16)
            for i in range(3):
                pool.wait_ge(rows_stored[i], 16)
            with pool.Fori(0, DEPTH) as L:
                for ct in range(NCT):
                    pool.wait_ge(conv_in, ct + 1)
                    pool.tensor_copy(tail[:, ct, 0:3], cin[ct % 2][:, SEQ:SEQ + 3])
                    src = cin[ct % 2][:, 3 + SEQ:XW].rearrange("p (b n) -> p b n", b=DB)
                    pool.tensor_copy(tail[:, ct, 3:27].rearrange("p (b n) -> p b n", b=DB), src[:, :, 4:7]).then_inc(tail_copied, 1)
                pool.wait_ge(vn_ready, 1)
                pool.dma_start(layer_of(outs["chunk_v_sample"], L).rearrange("b s c -> (b s) c"),
                               proj[0:NS, NP, AV:AV + AW]).then_inc(pool_stored, 16)
                pool.wait_ge(rope_done, 1)
                for name, c in (("win_k", BK), ("win_v", BV)):
                    pool.dma_start(layer_of(outs[name + "_prompt"], L).rearrange("b (t p) h d -> p (b t) (h d)", p=128),
                                   proj[:, 0:NP, c:c + BW]).then_inc(pool_stored, 16)
                    pool.dma_start(layer_of(outs[name + "_sample"], L).rearrange("b s h d -> (b s) (h d)"),
                                   proj[0:NS, NP, c:c + BW]).then_inc(pool_stored, 16)
                pool.wait_ge(vec_drained, V_AT[("S", NP - 1, 1)] + 1)
                for hh in range(2):
                    pool.dma_start(layer_of(outs["delta_prompt"], L).rearrange("b (g h) k v -> h k (b g) v", h=2)[hh],
                                   hd(state[64 * hh:64 * hh + 64, :])[:, hh::2, :]).then_inc(pool_stored, 16)
                pool.wait_ge(index_ready, 1)
                for t in range(NT):
                    for k in range(2):
                        pool.indirect_dma_start(x_lists[:, :], bass.IndirectOffsetOnAxis(idx_sc[0:ROWS[t], NT * k + t:NT * k + t + 1], 0),
                                                h2[0:ROWS[t], t, :], None).then_inc(scattered, 16)
                pool.wait_ge(scattered, (L + 1) * (32 * NT))
                pool.sem_inc(aside, 1)

                def load_rows(e, k):
                    pool.dma_start(rows_in[k], x_lists[bass.ds(e * CAP, CAP), :]).then_inc(rows_loaded[k], 16)

                def store_rows(e, k):
                    for c in range(2):
                        pool.dma_start(y_lists[bass.ds(e * CAP, CAP), 512 * c:512 * c + 512],
                                       rows_out[k][CAP * c:CAP * c + CAP, :]).then_inc(rows_stored[k], 16)
                for e in range(3):
                    load_rows(e, e)
                for e in range(2):
                    pool.wait_ge(vec_filled, V0 + 2 * e + 1)
                    load_rows(e + 3, e)
                with pool.Fori(0, (NE - 5) // 3) as i:
                    for k in range(3):
                        pool.wait_ge(vec_filled, i * 6 + (V0 + 2 * (k + 2) + 1))
                        pool.sem_inc(aside, 1)
                        load_rows(i * 3 + (5 + k), (k + 2) % 3)
                        pool.wait_ge(act_drained, i * 6 + (A0 + 2 * k + 2))
                        pool.sem_inc(aside, 1)
                        store_rows(i * 3 + k, k)
                for e in range(NE - 5, NE):
                    pool.wait_ge(act_drained, A0 + 2 * e + 2)
                    store_rows(e, e % 3)
                for k in range(3):
                    pool.wait_ge(rows_stored[k], L * (32 * per_buffer[k]) + (32 * per_buffer[k] + 16))
                pool.sem_inc(aside, 1)
                for t in range(NT):
                    if t >= 2:
                        pool.wait_ge(got_used, t - 1)
                    for k in range(2):
                        j = (t % 2) * 2 + k
                        pool.indirect_dma_start(got[j][0:ROWS[t], :], None, y_lists[:, :],
                                                bass.IndirectOffsetOnAxis(idx_ga[0:ROWS[t], NT * k + t:NT * k + t + 1], 0)).then_inc(gathered[j], 16)
                pool.wait_ge(pool_stored, (L + 1) * (16 * STORES))
                pool.sem_inc(aside, 1)
                leave_layer(pool, L, clears=True)

        @block.scalar
        def _(act):
            steps = [0]
            roots, asked = [0], [0]

            def get(label):
                act.wait_ge(act_filled, A_AT[label] + 1)
                return a_bank(A_AT[label])

            def root(ap):
                roots[0] += 1
                act.wait_ge(root_asked, roots[0])
                act.activation(ap, ap, ACT.Sqrt).then_inc(root_ready, 1)

            act.wait_ge(consts_loaded, 16)
            act.wait_ge(x_loaded, 32)
            with act.Fori(0, DEPTH) as L:
                for t in range(NT):
                    r = ROWS[t]
                    if t:
                        act.wait_ge(squares_ready, t)
                    act.activation(junk1[0:r], x[0:r, t, :], ACT.Square, accum_out=ssq[0:r, t:t + 1]).then_inc(squares_ready, 1)
                root(rstd)
                bank = get(("tapsT",))
                act.activation(taps, bank[:, 0:NCT * 28].rearrange("p (c n) -> p c n", c=NCT), ACT.Copy).then_inc(act_drained, 1)
                for i in range(NCT + 1):
                    if i < NCT:
                        c = cin[i % 2]
                        seqs = c[:, 3 + SEQ:XW].rearrange("p (b n) -> p b n", b=DB)
                        if i >= 2:
                            act.wait_ge(conv_done, i - 1)
                            act.wait_ge(tail_copied, i - 1)
                        bank = get(("convP", i))
                        act.activation(c[:, 3:3 + SEQ], bank[:, 0:SEQ], ACT.Copy).then_inc(act_drained, 1)
                        bank = get(("convS", i))
                        act.activation(seqs[:, :, 3:7], bank[:, 0:NS].rearrange("p (b n) -> p b n", b=DB), ACT.Copy).then_inc(act_drained, 1)
                        if i == 0:
                            act.wait_ge(act_drained, A_AT[("tapsT",)] + 1)
                        act.activation(seqs[:, :, 0:3], taps[:, i, 0:24].rearrange("p (b n) -> p b n", b=DB), ACT.Copy).then_inc(conv_in, 1)
                    if i >= 1:
                        j = i - 1
                        act.wait_ge(conv_done, j + 1)
                        if j >= 2:
                            act.wait_ge(vec_filled, V_AT[("qkvS", j - 2)] + 1)
                        a = acc[j % 2]
                        act.activation(sil[j % 2][:, 0:SEQ], a[:, 0:SEQ], ACT.Silu)
                        src = a[:, 3 + SEQ:XW].rearrange("p (b n) -> p b n", b=DB)[:, :, 0:DS]
                        act.activation(sil[j % 2][:, SEQ:NTOK].rearrange("p (b n) -> p b n", b=DB), src, ACT.Silu).then_inc(silu_done, 1)
                act.wait_ge(rows_stored[0], 16)
                act.wait_ge(rows_stored[1], 16)
                act.wait_ge(rows_stored[2], 16)
                where = {"A": ((AU, 512), (CB, 12)), "B": ((BQ, BW), (BK, BW)), "C": ((BV, BW), (CZ, CW))}
                for piece in "ABC":
                    for t in range(NT):
                        for j, (c, n) in enumerate(where[piece]):
                            if (piece, t, j) == ("B", NP, 0):
                                act.wait_ge(tail_stored, 32)
                            bank = get((piece, t, j))
                            act.activation(proj[0:ROWS[t], t, c:c + n], bank[0:ROWS[t], 0:n], ACT.Copy).then_inc(act_drained, 1)
                act.wait_ge(act_drained, A_AT[("C", NT - 1, 1)] + 1)
                act.activation(proj[:, 0:NP, CZ:CZ + CW], proj[:, 0:NP, CZ:CZ + CW], ACT.Silu).then_inc(z_ready, 1)
                act.activation(proj[0:NS, NP, CZ:CZ + CW], proj[0:NS, NP, CZ:CZ + CW], ACT.Silu).then_inc(z_ready, 1)
                root(ln_var)
                act.wait_ge(gate_asked, 1)
                act.activation(beta, gates[:, :, 0:CH], ACT.Exp, scale=-1.0)
                act.wait_ge(params_loaded, 16 * 6)
                act.activation(a_log, a_log, ACT.Exp).then_inc(gate_got, 1)
                act.wait_ge(gate_asked, 2)
                act.activation(decay, decay, ACT.Exp, scale=-1.0).then_inc(act_step, 1)
                act.wait_ge(act_step, 1)
                act.activation(decay, decay, ACT.Ln, bias=1.0).then_inc(gate_got, 1)
                root(l2)
                for t in range(NT):
                    r, w = ROWS[t], (64 if t < NP else NS)
                    bank = get(("cg", t))
                    if t < NP:
                        act.activation(ex_cg[:, 0:24], bank[:, 0:24], ACT.Exp).then_inc(act_drained, 1)
                    else:
                        act.activation(ex_cg[0:r, 0:12], bank[0:r, 0:12], ACT.Exp)
                        act.activation(ex_cg[:, 12:60], bank[:, 12:60], ACT.Exp).then_inc(act_drained, 1)
                    for label, dst in (("D", E_), ("DT", ET_)):
                        bank = get((label, t))
                        act.activation(dst[0:r, 0:CH * w], bank[0:r, 0:CH * w], ACT.Exp).then_inc(act_drained, 1)

                    def out(label, dst, n=CW, rr=r):
                        bank = get(label)
                        act.activation(dst[0:rr, 0:n], bank[0:rr, 0:n], ACT.Copy).then_inc(act_drained, 1)
                    out(("N2", t), N2_, CH * w)
                    if t < NP:
                        out(("N4", t), N4_)
                        out(("N8", t), N2_)
                        for s in (32, 64):
                            out(("T", t, s), T_)
                            out(("Y", t, s), Y_)
                        for c in range(2):
                            bank = get(("wT", t, c))
                            act.activation(hd(ET_, 3)[:, :, 64 * c:64 * c + 64], hd(bank[:, 0:3 * 64], 3), ACT.Copy).then_inc(act_drained, 1)
                    else:
                        bank = get(("wT", t, 0))
                        act.activation(ET_[:, 0:192].rearrange("p (g n) -> p g n", g=3)[:, :, 0:NS],
                                       bank[:, 0:3 * NS].rearrange("p (g n) -> p g n", g=3), ACT.Copy).then_inc(act_drained, 1)
                    root(o_ss)
                act.wait_ge(vec_drained, V_AT[("S4", CH - 1)] + 1)
                for g in range(3):
                    act.dma_start(layer_of(outs["delta_sample"], L)[:, 2 * g:2 * g + 2].rearrange("b h k v -> (h k) b v"), state_tile(g)).then_inc(state_stored, 16)
                act.wait_ge(state_stored, 48)
                for g in range(3):
                    for name, dst in (("bq", qTb), ("bk", kTb)):
                        bank = get((name, g))
                        act.activation(dst[g][:, 0:SEQ], bank[:, 0:SEQ], ACT.Copy).then_inc(act_drained, 1)
                        bank = get((name + "s", g))
                        act.activation(dst[g][:, SEQ:NTOK], bank[:, 0:NS], ACT.Copy).then_inc(act_drained, 1)
                n = BH * NP
                for i in range(n + 1):
                    if i < n:
                        keys = 128 * (i % NP + 1)
                        act.wait_ge(probs_asked, i + 1)
                        act.activation(prob[i % 2][:, 0:keys], prob[i % 2][:, 0:keys], ACT.Exp, bias=a_max[:, i:i + 1],
                                       accum_out=a_sum[:, i:i + 1]).then_inc(probs_ready, 1)
                    if i >= 1:
                        j = i - 1
                        keys = 128 * (j % NP + 1)
                        bank = get(("P", j))
                        if j >= 2:
                            act.wait_ge(vec_filled, V_AT[("O", j - 2)] + 1)
                        act.activation(probT[j % 2][:, 0:keys], bank[:, 0:keys], ACT.Copy).then_inc(act_drained, 1)
                for G in range(2):
                    for q in range(12):
                        qq = 12 * G + q
                        if q >= 2:
                            act.wait_ge(keys_used, 11 * G + q - 1)
                        bank = get(("kd", G, q // 3, q % 3))
                        act.activation(keysT[qq % 2][:, 0:384], bank[:, 0:384], ACT.Copy).then_inc(act_drained, 1)
                        bank = get(("kr", G, q // 3, q % 3))
                        act.activation(keysT[qq % 2][:, 384:896], bank[:, :], ACT.Copy).then_inc(act_drained, 1)
                    act.wait_ge(sprob_asked, G + 1)
                    act.activation(sprob, sprob, ACT.Exp, bias=s_max[:, 4:5], accum_out=s_sum[:, 0:1]).then_inc(sprob_got, 1)
                for t in range(NT):
                    for h in range(2):
                        bank = get(("mixT", t, h))
                        ks = mix_tiles(t, h)
                        act.activation(hT[:, ks[0]:ks[0] + len(ks), 128 * t:128 * t + ROWS[t]],
                                       bank[:, 0:len(ks) * ROWS[t]].rearrange("p (k n) -> p k n", k=len(ks)), ACT.Copy).then_inc(act_drained, 1)
                for t in range(NT):
                    r = ROWS[t]
                    act.wait_ge(vec_drained, V_AT[("out", 1, t)] + 1)
                    act.wait_ge(squares_ready, NT + t)
                    act.activation(junk2[0:r], x[0:r, t, :], ACT.Square, accum_out=ssq[0:r, t:t + 1]).then_inc(squares_ready, 1)
                root(rstd)
                act.wait_ge(route_asked, 1)
                act.activation(top[:, :, 0:NG], top[:, :, 0:NG], ACT.Exp).then_inc(route_got, 1)
                act.wait_ge(route_asked, 2)
                act.activation(p1, p1, ACT.Exp).then_inc(route_got, 1)

                def silu(k, rnd):
                    act.wait_ge(vec_filled, rnd * (2 * EUN) + (V0 + 2 * k + 2))
                    act.activation(gate_act[k % 2], v_bank(V0 + 2 * k + 1)[:, 0:128], ACT.Silu).then_inc(act_gated, 1)

                def hidden_out(k, rnd):
                    act.wait_ge(act_filled, rnd * (2 * EUN) + (A0 + 2 * k + 1))
                    act.activation(hidT[k % 2], a_bank(A0 + 2 * k)[:, 0:128], ACT.Copy).then_inc(act_drained, 1)

                def result_out(k, rnd):
                    act.wait_ge(act_filled, rnd * (2 * EUN) + (A0 + 2 * k + 2))
                    act.wait_ge(rows_stored[k % 3], L * (32 * per_buffer[k % 3]) + rnd * (32 * EUN // 3) + 32 * (k // 3) + 16)
                    act.activation(rows_out[k % 3], a_bank(A0 + 2 * k + 1)[:, :], ACT.Copy).then_inc(act_drained, 1)
                silu(0, 0)
                hidden_out(0, 0)
                with act.Fori(0, ELOOP // EUN) as rnd:
                    for k in range(EUN):
                        silu(k + 1, rnd)
                        result_out(k, rnd)
                        hidden_out(k + 1, rnd)
                for k in range(NE - ELOOP):
                    if k + 1 < NE - ELOOP:
                        silu(k + 1, ELOOP // EUN)
                    result_out(k, ELOOP // EUN)
                    if k + 1 < NE - ELOOP:
                        hidden_out(k + 1, ELOOP // EUN)
                act.wait_ge(moe_done, 1)
                over = act.value_load(idx_cnt[0:1, 0:1], min_val=0, max_val=NTOK)
                with act.If(over > CAP):
                    with act.Fori(0, NE) as e:
                        for f in range(2):
                            act.wait_ge(fb_up, e * 2 + (f + 1))
                            act.activation(fb_act[:, f, 0:SEQ], psum[2 * f][:, :], ACT.Silu)
                            act.activation(fb_act[:, f, SEQ:NTOK], psum[4 + f][:, 0:NS], ACT.Silu).then_inc(fb_silu, 1)
                leave_layer(act, L)
            for t in range(NT):
                r = ROWS[t]
                if t:
                    act.wait_ge(fin_step, t)
                act.activation(junk1[0:r], x[0:r, t, :], ACT.Square, accum_out=ssq[0:r, t:t + 1]).then_inc(fin_step, 1)
            act.wait_ge(fin_step, NT + 1)
            act.activation(rstd, rstd, ACT.Sqrt).then_inc(fin_step, 1)

        def delta_tile(pe, L, t, job, after, tr):
            r, w = ROWS[t], (64 if t < NP else NS)
            chunks = [0, 64] if t < NP else [0]
            prompt = t < NP
            LE, GT = (const("le"), const("gt")) if prompt else (const("le4"), const("gt4"))

            def each(label, lhs, rhs, n=w, of_heads=range(CH)):
                bank, done = job(label)
                for h in of_heads:
                    for c in chunks:
                        mm = pe.matmul(bank[c:c + w, n * h:n * h + n], lhs(h, c), rhs(h, c), start=True, stop=True)
                mm.then_inc(done, 1)

            def of(buf):
                return lambda h, c: buf[c:c + w, w * h:w * h + w]

            pe.wait_ge(delta_in, 3 * t + 3)
            bank, done = job(("cg", t))
            g = decay[0:r, t, :]
            mm = pe.matmul(bank[0:r, 0:CH], LE, g, start=True, stop=True)
            pe.matmul(bank[0:r, CH:2 * CH], GT, g, start=True, stop=True)
            if prompt:
                for c in range(2):
                    mm = pe.matmul(bank[:, 12 + 6 * c:18 + 6 * c], const(f"ch{c}"), g, start=True, stop=True)
            else:
                mm = pe.matmul(bank[:, 12:60], const("ones")[0:r, :], gt4_[0:r, :], start=True, stop=True)
            mm.then_inc(done, 1)
            bank, done = job(("D", t))
            pe.matmul(bank[0:r, 0:CH * w], LE, N2_[0:r, 0:CH * w], start=True, stop=True).then_inc(done, 1)
            bank, done = job(("DT", t))
            pe.matmul(bank[0:r, 0:CH * w], GT, N2T_[0:r, 0:CH * w], start=True, stop=True).then_inc(done, 1)
            for label, src in (("qT", qkv[0:r, t, 0:CW]), ("kT", qkv[0:r, t, CW:2 * CW]), ("bT", kb_[0:r])):
                bank, done = job((label, t))
                for gg in range(3):
                    mm = tr(bank[:, r * gg:r * gg + r], src[:, 128 * gg:128 * gg + 128])
                mm.then_inc(done, 1)
            after(("bT", t))
            kq = KQ_[:, 0:6 * r].rearrange("p (g m n) -> p g m n", g=3, m=2)

            def kTc(h, c):
                return KZ_[:, h, c:c + w]

            def kqc(h, c, m):
                return kq[:, h // 2, m, c:c + w]
            each(("AA", t), lambda h, c: kqc(h, c, 0), kTc)
            for i, hs in enumerate((range(0, 4), range(4, 6))):
                bank, done = job((f"AT{i}", t))
                for h in hs:
                    for c in chunks:
                        mm = pe.matmul(bank[c:c + w, 2 * w * (h - hs[0]):2 * w * (h - hs[0] + 1)].rearrange("p (m n) -> p m n", m=2),
                                       kTc(h, c), kqc(h, c, slice(0, 2)), start=True, stop=True)
                mm.then_inc(done, 1)
            pe.wait_ge(delta_w, 2 * t + 2)
            each(("N2", t), of(NT_), of(N_))
            each(("N2T", t), of(N_), of(NT_))
            after(("N2", t))
            after(("N2T", t))
            if prompt:
                each(("N4", t), of(N2T_), of(N2_))
                each(("N4T", t), of(N2_), of(N2T_))
            each(("M1", t), of(N2_), of(U_))
            after(("M1", t))
            if prompt:
                after(("N4", t))
                each(("N8", t), of(N4T_), of(N4_))
                each(("M2", t), of(N4_), of(U_))
                after(("M2", t))
                after(("N8", t))
                each(("M3", t), of(N2_), of(U_))
                after(("M3", t))
                for s, A in ((32, A32_), (64, A64_)):
                    each(("T", t, s), of(U_), lambda h, c: ident[c:c + w, c:c + w])
                    each(("Y", t, s), of(A), of(U_))
                    after(("Y", t, s))
                    each(("X", t, s), of(T_), of(Y_))
                    after(("X", t, s))
            pe.wait_ge(delta_w, 2 * t + 2)
            each(("u", t), of(U_), lambda h, c: qkv[c:c + w, t, 2 * CW + 64 * h:2 * CW + 64 * h + 64], n=64)
            for ci, c in enumerate(chunks):
                bank, done = job(("wT", t, ci))
                for h in range(CH):
                    mm = pe.matmul(bank[64 * (h % 2):64 * (h % 2) + 64, w * (h // 2):w * (h // 2) + w],
                                   rw_[c:c + w, 64 * h:64 * h + 64], U_[c:c + w, w * h:w * h + w], start=True, stop=True)
                mm.then_inc(done, 1)
            bank, done = job(("qdT", t))
            for gg in range(3):
                mm = tr(bank[:, r * gg:r * gg + r], qd_[0:r, 128 * gg:128 * gg + 128])
            mm.then_inc(done, 1)
            after(("qdT", t))
            after(("wT", t, len(chunks) - 1))
            if prompt:
                for ci, c in enumerate(chunks):
                    def state_of(h):
                        return state[:, 64 * h:64 * h + 64]
                    bank, done = job(("wS", t, ci))
                    for h in range(CH):
                        mm = pe.matmul(bank[c:c + 64, 64 * h:64 * h + 64],
                                       ET_[:, 128 * (h // 2) + c:128 * (h // 2) + c + 64],
                                       state_of(h), start=True, stop=True)
                    mm.then_inc(done, 1)
                    after(("wS", t, ci))
                    bank, done = job(("o", t, ci))
                    for h in range(CH):
                        dst = bank[c:c + 64, 64 * h:64 * h + 64]
                        pe.matmul(dst, KQ_[:, 128 * (h // 2) + c:128 * (h // 2) + c + 64],
                                  state_of(h), start=True, stop=False)
                        mm = pe.matmul(dst, aT_[c:c + 64, 64 * h:64 * h + 64], N_[c:c + 64, 64 * h:64 * h + 64], start=False, stop=True)
                    mm.then_inc(done, 1)
                    bank, done = job(("S", t, ci))
                    for h in range(CH):
                        mm = pe.matmul(bank[64 * (h % 2):64 * (h % 2) + 64, 64 * h:64 * h + 64],
                                       kd_[c:c + 64, 64 * h:64 * h + 64], N_[c:c + 64, 64 * h:64 * h + 64], start=True, stop=True)
                    mm.then_inc(done, 1)
                    after(("S", t, ci))
                return
            pe.wait_ge(state_loaded, 48)
            for h in range(CH):
                p = 64 * (h % 2)
                bank, done = job(("wS4", h))
                pe.matmul(bank[0:64, :], ET_[p:p + 64, 64 * (h // 2):64 * (h // 2) + 64], S4_[p:p + 64, 512 * (h // 2):512 * (h // 2) + 512],
                          start=True, stop=True).then_inc(done, 1)
            pe.wait_ge(delta_state, 1)
            bank, done = job(("oShift",))
            pe.matmul(bank[0:NS, 0:CW], ident[NS:2 * NS, NS:2 * NS], KQ_[NS:2 * NS, 0:CW], start=True, stop=True).then_inc(done, 1)
            bank, done = job(("o4",))
            for h in range(CH):
                mm = pe.matmul(bank[0:NS, 64 * h:64 * h + 64], aT_[0:NS, NS * h:NS * h + NS], N_[0:NS, 64 * h:64 * h + 64], start=True, stop=True)
            mm.then_inc(done, 1)
            for h in range(CH):
                pe.wait_ge(expand_ready, h + 1)
                bank, done = job(("S4", h))
                pe.matmul(bank[64 * (h % 2):64 * (h % 2) + 64, :], kd_[0:NS, 64 * h:64 * h + 64], BIG_[0:NS, :], start=True, stop=True).then_inc(done, 1)

        @block.tensor
        def _(pe):
            def job(label):
                if label in A_AT:
                    n = A_AT[label]
                    if n >= 4:
                        pe.wait_ge(act_drained, n - 3)
                    return a_bank(n), act_filled
                n = V_AT[label]
                if n >= 4:
                    pe.wait_ge(vec_drained, n - 3)
                return v_bank(n), vec_filled

            def after(label):
                if label in A_AT:
                    pe.wait_ge(act_drained, A_AT[label] + 1)
                else:
                    pe.wait_ge(vec_drained, V_AT[label] + 1)

            def arrived(L, n):
                pe.wait_ge(slot_full[n % 3], L * SLOT_TOTAL[n % 3] + full_at[n])
                pe.sem_inc(aside, 1)

            def tr(out, in_, start=True):
                r = in_.shape[0]
                return pe.transpose(out, in_, ident[0:r, 0:r])

            def ringv(n, at, cols, k=KT):
                base = (n % 3) * SLOT + at
                return ring[:, base:base + k * cols].rearrange("p (k n) -> p k n", k=k)

            pe.wait_ge(consts_loaded, 16)
            with pe.Fori(0, DEPTH) as L:
                pe.wait_ge(taps_loaded, 32)
                bank, done = job(("tapsT",))
                for c in range(NCT):
                    mm = tr(bank[:, 28 * c:28 * c + 28], state_rows[:, 128 * c:128 * c + 128])
                mm.then_inc(done, 1)
                for t in range(NT):
                    pe.wait_ge(rows_ready, t + 1)
                    r = ROWS[t]
                    for h in range(2):
                        bank, done = job(("norm1", t, h))
                        for k in range(4):
                            mm = tr(bank[:, k * r:k * r + r], hst[t % 2][0:r, 4 * h + k::KT])
                        mm.then_inc(done, 1)
                after(("norm1", NT - 1, 1))
                for i in range(NCT + 2):
                    if i < NCT:
                        n = i // 3
                        if i % 3 == 0:
                            arrived(L, n)
                        w = ringv(n, 0, 384)[:, :, 128 * (i % 3):128 * (i % 3) + 128]
                        for label, c0, c1_ in ((("convP", i), 0, SEQ), (("convS", i), SEQ, NTOK)):
                            bank, done = job(label)
                            for k in range(KT):
                                mm = pe.matmul(bank[:, 0:c1_ - c0], w[:, k, :], hT[:, k, c0:c1_], start=k == 0, stop=k == KT - 1)
                            mm.then_inc(done, 1)
                    if i >= 2:
                        j = i - 2
                        pe.wait_ge(silu_done, j + 1)
                        bank, done = job(("qkvP", j))
                        for t in range(NP):
                            mm = tr(bank[:, 128 * t:128 * t + 128], sil[j % 2][:, 128 * t:128 * t + 128])
                        mm.then_inc(done, 1)
                        bank, done = job(("qkvS", j))
                        tr(bank[0:NS, 0:128], sil[j % 2][:, SEQ:NTOK]).then_inc(done, 1)
                pe.wait_ge(tail_copied, NCT)
                for i in range(3):
                    bank, done = job(("tail", i))
                    for c in range(3):
                        mm = tr(bank[0:27, 128 * c:128 * c + 128], tail[:, 3 * i + c, :])
                    mm.then_inc(done, 1)
                pe.wait_ge(params_loaded, 16 * 6)
                for p, piece in enumerate("ABC"):
                    n = 3 + p
                    arrived(L, n)
                    parts = {"A": (ringv(n, 0, 512), w_ba), "B": (ringv(n, 0, 768)[:, :, 0:384], ringv(n, 0, 768)[:, :, 384:768]),
                             "C": (ringv(n, 0, 384), ringv(n, KT * 384, 384))}[piece]
                    for t in range(NT):
                        for j, w in enumerate(parts):
                            bank, done = job((piece, t, j))
                            for k in range(KT):
                                mm = pe.matmul(bank[0:ROWS[t], 0:w.shape[2]], hT[:, k, 128 * t:128 * t + ROWS[t]], w[:, k, :],
                                               start=k == 0, stop=k == KT - 1)
                            mm.then_inc(done, 1)
                pe.wait_ge(mlp_params, 48)
                bank, done = job(("wsT",))
                for h in range(AH):
                    mm = tr(bank[:, 128 * h:128 * h + 128], ws_raw[:, h, :])
                mm.then_inc(done, 1)
                after(("wsT",))
                bank, done = job(("rep",))
                for h in range(AH):
                    mm = pe.matmul(bank[0:DS, NS * h:NS * h + NS], wsT[0:DS, h, 0:DS], const("rep4"), start=True, stop=True)
                mm.then_inc(done, 1)
                after(("rep",))
                bank, done = job(("ws4",))
                for h in range(AH):
                    pe.matmul(bank[0:NS, NS * h:NS * h + NS], rep_w[:, NS * h:NS * h + NS], const("rep4"), start=True, stop=True)
                pe.matmul(bank[0:NS, 128:128 + AH], const("rep4"), bias_p[0:DS, :], start=True, stop=True).then_inc(done, 1)
                after(("ws4",))
                pe.wait_ge(vn_ready, 1)
                for t in range(NT):
                    bank, done = job(("gate", t))
                    for h in range(AH):
                        w = wsT[:, h, :] if t < NP else ws4[:, h, :]
                        mm = pe.matmul(bank[0:ROWS[t], 64 * h:64 * h + 64], w, proj[0:ROWS[t], t, AV + 64 * h:AV + 64 * h + 64],
                                       start=True, stop=True)
                    mm.then_inc(done, 1)
                for t in range(NT):
                    delta_tile(pe, L, t, job, after, tr)
                pe.wait_ge(rope_done, 1)
                for g in range(3):
                    for name, c in (("bq", BQ), ("bk", BK)):
                        bank, done = job((name, g))
                        for t in range(NP):
                            mm = tr(bank[:, 128 * t:128 * t + 128], proj[:, t, c + 128 * g:c + 128 * g + 128])
                        mm.then_inc(done, 1)
                        bank, done = job((name + "s", g))
                        tr(bank[:, 0:NS], proj[0:NS, NP, c + 128 * g:c + 128 * g + 128]).then_inc(done, 1)
                after(("bks", 2))
                n = BH * NP
                for i in range(n + 2):
                    if i < n:
                        h, t = divmod(i, NP)
                        p0_, g = 64 * (h % 2), h // 2
                        bank, done = job(("S", i))
                        pe.matmul(bank[:, 0:128 * (t + 1)], qTb[g][p0_:p0_ + 64, 128 * t:128 * t + 128],
                                  kTb[g][p0_:p0_ + 64, 0:128 * (t + 1)], start=True, stop=True).then_inc(done, 1)
                    if 1 <= i <= n:
                        j = i - 1
                        pe.wait_ge(probs_ready, j + 1)
                        bank, done = job(("P", j))
                        for b in range(j % NP + 1):
                            mm = tr(bank[:, 128 * b:128 * b + 128], prob[j % 2][:, 128 * b:128 * b + 128])
                        mm.then_inc(done, 1)
                    if i >= 2:
                        j = i - 2
                        h, t = divmod(j, NP)
                        after(("P", j))
                        bank, done = job(("O", j))
                        for b in range(t + 1):
                            mm = pe.matmul(bank[:, 0:64], probT[j % 2][:, 128 * b:128 * b + 128],
                                           proj[:, b, BV + 64 * h:BV + 64 * h + 64], start=b == 0, stop=b == t)
                        mm.then_inc(done, 1)
                pe.wait_ge(qblk_ready, 1)
                for G in range(2):
                    score = {}
                    for q in range(13):
                        if q < 12:
                            b, g = divmod(q, 3)
                            n = 6 + 4 * G + b // 2
                            if q % 6 == 0:
                                arrived(L, n)
                            kk = ring[:, (n % 3) * SLOT + 3072 * (b % 2):(n % 3) * SLOT + 3072 * (b % 2) + 3072].rearrange("p (j n) -> p j n", j=8)
                            bank, done = job(("kd", G, b, g))
                            for j in range(4):
                                mm = tr(bank[:, NDIL * j:NDIL * j + NDIL], kk[0:NDIL, j, 128 * g:128 * g + 128])
                            mm.then_inc(done, 1)
                            bank, done = job(("kr", G, b, g))
                            for j in range(4):
                                mm = tr(bank[:, 128 * j:128 * j + 128], kk[:, 4 + j, 128 * g:128 * g + 128])
                            mm.then_inc(done, 1)
                        if q >= 1:
                            b, g = divmod(q - 1, 3)
                            after(("kr", G, b, g))
                            if q == 1:
                                for name in ("sd", "sr", "sn"):
                                    score[name] = job((name, G))
                            kt = keysT[(12 * G + q - 1) % 2]
                            qb = qblk[:, 4 * G + b, g, :]
                            for name, rhs in (("sd", kt[:, 0:384]), ("sr", kt[:, 384:896]), ("sn", kTb[g][:, SEQ:NTOK])):
                                bank = score[name][0]
                                mm = pe.matmul(bank[32 * b:32 * b + 32, 0:rhs.shape[1]], qb, rhs, start=g == 0, stop=g == 2)
                                if q == 12:
                                    mm.then_inc(vec_filled, 1)
                                elif name == "sn":
                                    mm.then_inc(keys_used, 1)
                    pe.wait_ge(sprob_ready, G + 1)
                    bank, done = job(("pd", G))
                    for j in range(4):
                        mm = tr(bank[0:NDIL, 128 * j:128 * j + 128], sprob[:, NDIL * j:NDIL * j + NDIL])
                    mm.then_inc(done, 1)
                    bank, done = job(("pr", G))
                    for j in range(4):
                        mm = tr(bank[:, 128 * j:128 * j + 128], sprob[:, 384 + 128 * j:384 + 128 * j + 128])
                    mm.then_inc(done, 1)
                    bank, done = job(("pn", G))
                    tr(bank[0:NS, 0:128], sprob[:, 896:928]).then_inc(done, 1)
                    after(("pn", G))
                    for b in range(4):
                        n = 8 + 4 * G + b // 2
                        if b % 2 == 0:
                            arrived(L, n)
                        vv = ring[:, (n % 3) * SLOT + 3072 * (b % 2):(n % 3) * SLOT + 3072 * (b % 2) + 3072].rearrange("p (j n) -> p j n", j=8)
                        bank, done = job(("ov", G, b))
                        for g in range(3):
                            dst = bank[:, 8 * g:8 * g + 8]
                            col = 32 * b + 8 * g
                            cs = slice(128 * g, 128 * g + 128)
                            for j in range(4):
                                pe.matmul(dst, vv[0:NDIL, j, cs], spd[0:NDIL, 128 * j + col:128 * j + col + 8], start=j == 0, stop=False)
                            for j in range(4):
                                pe.matmul(dst, vv[:, 4 + j, cs], spr[:, 128 * j + col:128 * j + col + 8], start=False, stop=False)
                            mm = pe.matmul(dst, proj[0:NS, NP, BV + 128 * g:BV + 128 * g + 128], spn[0:NS, col:col + 8], start=False, stop=True)
                        mm.then_inc(done, 1)
                pe.wait_ge(mix_ready, 1)
                for t in range(NT):
                    r = ROWS[t]
                    for h in range(2):
                        bank, done = job(("mixT", t, h))
                        for j, k in enumerate(mix_tiles(t, h)):
                            mm = tr(bank[:, j * r:j * r + r], proj[0:r, t, MIXCOL[k]:MIXCOL[k] + 128])
                        mm.then_inc(done, 1)
                after(("mixT", NT - 1, 1))
                for c in range(2):
                    arrived(L, 14 + c)
                    w = ringv(14 + c, 0, 512)
                    for t in range(NT):
                        bank, done = job(("out", c, t))
                        for k in range(KT):
                            mm = pe.matmul(bank[0:ROWS[t], :], hT[:, k, 128 * t:128 * t + ROWS[t]], w[:, k, :], start=k == 0, stop=k == KT - 1)
                        mm.then_inc(done, 1)
                for t in range(NT):
                    r = ROWS[t]
                    pe.wait_ge(rows_ready, NT + t + 1)
                    for h in range(2):
                        bank, done = job(("norm2", t, h))
                        for k in range(4):
                            mm = tr(bank[:, k * r:k * r + r], h2[0:r, t, 4 * h + k::KT])
                        mm.then_inc(done, 1)
                after(("norm2", NT - 1, 1))
                pe.wait_ge(route_loaded, 32)
                bank, done = job(("logit", 0))
                for t in range(NT):
                    for k in range(KT):
                        mm = pe.matmul(bank[0:ROWS[t], 36 * t:36 * t + 36], hT[:, k, 128 * t:128 * t + ROWS[t]], w_route[:, k, :],
                                       start=k == 0, stop=k == KT - 1)
                mm.then_inc(done, 1)
                pe.wait_ge(masks_ready, 1)
                bank, done = job(("rank", 0))
                for t in range(NT + 1):
                    dst = bank[0:ROWS[t], 32 * t:32 * t + 32] if t < NT else bank[:, 160:192]
                    for u in range(min(t + 1, NT)):
                        m = const("before") if u == t else const("ones")
                        mm = pe.matmul(dst, m[0:ROWS[u], 0:dst.shape[0]], msum[0:ROWS[u], u, :], start=u == 0, stop=u == min(t, NT - 1))
                mm.then_inc(done, 1)

                def rows_across(k, rnd):
                    pe.wait_ge(rows_loaded[k % 3], L * (16 * per_buffer[k % 3]) + rnd * (16 * EUN // 3) + 16 * (k // 3 + 1))
                    pe.wait_ge(vec_drained, rnd * (2 * EUN) + (V0 + 2 * k - 3))
                    pe.sem_inc(aside, 1)
                    bank = v_bank(V0 + 2 * k)
                    for c in range(KT):
                        mm = pe.transpose(bank[:, CAP * c:CAP * c + CAP], rows_in[k % 3][:, c::KT], ident[0:CAP, 0:CAP])
                    mm.then_inc(vec_filled, 1)

                def up(k, rnd):
                    slot = (E_AT + k) % 3
                    w13 = ring[:, slot * SLOT:slot * SLOT + 4096].rearrange("p (w k f j) -> p w k f j", w=2, k=KT, j=2)
                    pe.wait_ge(slot_full[slot], L * SLOT_TOTAL[slot] + rnd * (48 * EUN // 3) + full_at[E_AT + k])
                    pe.wait_ge(vec_drained, rnd * (2 * EUN) + (V0 + 2 * k + 1))
                    pe.sem_inc(aside, 1)
                    bank = v_bank(V0 + 2 * k + 1)
                    for c in range(KT):
                        for j in range(2):
                            mm = pe.matmul(bank[CAP * j:CAP * j + CAP, 0:256].rearrange("p (w f) -> p w f", w=2),
                                           rowsT[k % 2][:, CAP * c:CAP * c + CAP], w13[:, :, c, :, j], start=c == 0, stop=c == KT - 1)
                    mm.then_inc(vec_filled, 1)

                def hidden_across(k, rnd):
                    pe.wait_ge(vec_drained, rnd * (2 * EUN) + (V0 + 2 * k + 2))
                    pe.wait_ge(act_drained, rnd * (2 * EUN) + (A0 + 2 * k - 3))
                    pe.sem_inc(aside, 1)
                    pe.transpose(a_bank(A0 + 2 * k)[:, 0:128], hid[k % 2], ident).then_inc(act_filled, 1)

                def down(k, rnd):
                    slot = (E_AT + k) % 3
                    w2 = ring[:, slot * SLOT + 4096:slot * SLOT + 6144].rearrange("p (j d) -> p j d", j=2)
                    pe.wait_ge(act_drained, rnd * (2 * EUN) + (A0 + 2 * k + 1))
                    pe.sem_inc(aside, 1)
                    bank = a_bank(A0 + 2 * k + 1)
                    for j in range(2):
                        for c in range(2):
                            mm = pe.matmul(bank[CAP * c:CAP * c + CAP, :], hidT[k % 2][:, CAP * j:CAP * j + CAP], w2[:, j, 512 * c:512 * c + 512],
                                           start=j == 0, stop=j == 1)
                    mm.then_inc(act_filled, 1)
                rows_across(0, 0)
                up(0, 0)
                rows_across(1, 0)
                hidden_across(0, 0)
                with pe.Fori(0, ELOOP // EUN) as rnd:
                    for k in range(EUN):
                        up(k + 1, rnd)
                        rows_across(k + 2, rnd)
                        down(k, rnd)
                        hidden_across(k + 1, rnd)
                for k in range(NE - ELOOP):
                    if k + 1 < NE - ELOOP:
                        up(k + 1, ELOOP // EUN)
                    down(k, ELOOP // EUN)
                    if k + 1 < NE - ELOOP:
                        hidden_across(k + 1, ELOOP // EUN)
                pe.wait_ge(moe_done, 1)
                over = pe.value_load(idx_cnt[0:1, 0:1], min_val=0, max_val=NTOK)
                with pe.If(over > CAP):
                    fw = [fb_w[:, 2048 * i:2048 * i + 2048].rearrange("p (k f) -> p k f", k=KT) for i in range(2)]
                    fw2 = fb_w[:, 4096:6144].rearrange("p (j d) -> p j d", j=2)
                    with pe.Fori(0, NE) as e:
                        pe.wait_ge(fb_loaded, e * 48 + 48)
                        pe.sem_inc(aside, 1)
                        for f in range(2):
                            for i in range(2):
                                for dst, c0, c1_ in ((psum[2 * f + i][:, :], 0, SEQ), (psum[4 + f][:, 64 * i:64 * i + NS], SEQ, NTOK)):
                                    for c in range(KT):
                                        mm = pe.matmul(dst, fw[i][:, c, f::2], hT[:, c, c0:c1_], start=c == 0, stop=c == KT - 1)
                            mm.then_inc(fb_up, 1)
                        pe.wait_ge(fb_prod, e * 2 + 2)
                        pe.sem_inc(aside, 1)
                        for t in range(NT):
                            r = ROWS[t]
                            pe.wait_ge(fb_added, e * NT + (t + 1))
                            pe.sem_inc(aside, 1)
                            for c in range(2):
                                for j in range(2):
                                    mm = pe.matmul(psum[6 + c][0:r, :], fb_hid[:, j, 128 * t:128 * t + r], fw2[:, j, 512 * c:512 * c + 512],
                                                   start=j == 0, stop=j == 1)
                            mm.then_inc(fb_down, 1)
                leave_layer(pe, L)

        def delta_vec(dve, t, then, get, kept, inv_root):
            r, w = ROWS[t], (64 if t < NP else NS)
            prompt = t < NP
            m = ("gtc", "lec", "idc", "nlow16", "nup16") if prompt else ("gt4", "le4", "ident", "nlow4", "nup4")
            gtc, lec, idc, nlow, nup = (const(k)[0:r, 0:w] for k in m)
            q, k, v = (qkv[0:r, t, CW * i:CW * i + CW] for i in range(3))
            ew = CH * w
            then(dve.tensor_tensor(hd(qkv[0:r, t, 0:2 * CW], 12), hd(qkv[0:r, t, 0:2 * CW], 12), inner(l2[0:r, t, :], 64), ALU.mult))
            bt = inner(beta[0:r, t, :], 64)
            if not prompt:
                then(dve.tensor_tensor(gt4_[0:r, :].rearrange("p (h b) -> p h b", h=CH), mid(const("rowseq")[0:r, :], CH),
                                       inner(decay[0:r, t, :], DB), ALU.mult))
            dve.tensor_tensor(hd(kb_[0:r]), hd(k), bt, ALU.mult).then_inc(delta_in, 1)
            gb = inner(decay[0:r, t, :], w)
            dve.tensor_tensor(hd(N2_[0:r, 0:ew]), mid(gtc, CH), gb, ALU.mult).then_inc(delta_in, 1)
            dve.tensor_tensor(hd(N2T_[0:r, 0:ew]), mid(lec, CH), gb, ALU.mult).then_inc(delta_in, 1)
            dve.tensor_tensor(hd(v), hd(v), bt, ALU.mult)
            dve.wait_ge(delta_in, 3 * t + 3)
            dve.wait_ge(act_drained, A_AT[("cg", t)] + 1)
            dve.tensor_tensor(hd(rw_[0:r]), hd(kb_[0:r]), inner(ex_cg[0:r, 0:CH], 64), ALU.mult)
            dve.tensor_tensor(hd(qd_[0:r]), hd(q), inner(ex_cg[0:r, 0:CH], 64), ALU.mult)
            dve.tensor_tensor(hd(kd_[0:r]), hd(k), inner(ex_cg[0:r, CH:2 * CH], 64), ALU.mult).then_inc(delta_w, 1)
            kq = KQ_[:, 0:6 * r].rearrange("p (g m n) -> p g m n", g=3, m=2)
            bank = get(("qT", t))
            kept(dve.tensor_copy(kq[:, :, 1, :], hd(bank[:, 0:3 * r], 3)))
            bank = get(("kT", t))
            for hh in range(2):
                p = slice(64 * hh, 64 * hh + 64)
                ins = dve.tensor_copy(KZ_[p, hh::2, 0:r], hd(bank[p, 0:3 * r], 3))
            kept(ins)
            bank = get(("bT", t))
            kept(dve.tensor_copy(kq[:, :, 0, :], hd(bank[:, 0:3 * r], 3)))
            dve.wait_ge(act_drained, A_AT[("DT", t)] + 1)
            bank = get(("AA", t))
            kept(dve.tensor_tensor(T_[0:r, 0:ew], bank[0:r, 0:ew], E_[0:r, 0:ew], ALU.mult), ("AA", t))
            A = hd(T_[0:r, 0:ew])
            dve.tensor_tensor(hd(N_[0:r, 0:ew]), A, mid(nlow, CH), ALU.mult)
            if prompt:
                dve.tensor_tensor(hd(A32_), A, mid(const("low32"), CH), ALU.mult)
                dve.tensor_tensor(hd(A64_), A, mid(const("low64"), CH), ALU.mult)
            for i, (h0, h1) in enumerate(((0, 4), (4, 6))):
                bank = get((f"AT{i}", t))
                pair = bank[0:r, 0:2 * w * (h1 - h0)].rearrange("p (h m n) -> p h m n", h=h1 - h0, m=2)
                e = hd(ET_[0:r, 0:ew])[:, h0:h1, :]
                dve.tensor_tensor(hd(NT_[0:r, 0:ew])[:, h0:h1, :], pair[:, :, 0, :], e, ALU.mult)
                kept(dve.tensor_tensor(hd(aT_[0:r, 0:ew])[:, h0:h1, :], pair[:, :, 1, :], e, ALU.mult), (f"AT{i}", t))
            then(dve.tensor_tensor(hd(NT_[0:r, 0:ew]), hd(NT_[0:r, 0:ew]), mid(nup, CH), ALU.mult))
            dve.tensor_tensor(hd(aT_[0:r, 0:ew]), hd(aT_[0:r, 0:ew]), mid(lec, CH), ALU.mult)
            dve.tensor_tensor(hd(U_[0:r, 0:ew]), hd(NT_[0:r, 0:ew]), mid(idc, CH), ALU.add).then_inc(delta_w, 1)
            dve.wait_ge(delta_w, 2 * t + 2)

            def copy(label, dst):
                bank = get(label)
                kept(dve.tensor_copy(dst, bank[0:dst.shape[0], 0:dst.shape[1]]), label)

            def more(label, op=ALU.add):
                bank = get(label)
                kept(dve.tensor_tensor(U_[0:r, 0:ew], U_[0:r, 0:ew], bank[0:r, 0:ew], op), label)
            copy(("N2T", t), N2T_[0:r, 0:ew])
            if prompt:
                copy(("N4T", t), N4T_)
            more(("M1", t))
            if prompt:
                more(("M2", t))
                more(("M3", t))
                for s in (32, 64):
                    more(("X", t, s), ALU.subtract)
            copy(("u", t), E_[0:r])
            if prompt:
                copy(("qdT", t), KQ_[:, 0:CW])
                for ci in range(2):
                    c = slice(64 * ci, 64 * ci + 64)
                    bank = get(("wS", t, ci))
                    kept(dve.tensor_tensor(N_[c, :], E_[c, :], bank[c, 0:CW], ALU.subtract))
                    then(dve.tensor_tensor(hd(Sg_), hd(state), inner(ex_cg[:, 12 + 6 * ci:18 + 6 * ci], 64), ALU.mult))
                    bank = get(("o", t, ci))
                    kept(dve.tensor_copy(NT_[c, :], bank[c, 0:CW]))
                    bank = get(("S", t, ci))
                    for hh in range(2):
                        p = slice(64 * hh, 64 * hh + 64)
                        ins = dve.tensor_tensor(hd(state[p, :])[:, hh::2, :], hd(Sg_[p, :])[:, hh::2, :], hd(bank[p, 0:CW])[:, hh::2, :], ALU.add)
                    kept(ins, ("S", t, ci))
            else:
                bank = get(("qdT", t))
                kept(dve.tensor_copy(ET_[:, 0:192].rearrange("p (g n) -> p g n", g=3)[:, :, NS:2 * NS],
                                     bank[:, 0:3 * NS].rearrange("p (g n) -> p g n", g=3)))
                for h in range(CH):
                    bank = get(("wS4", h))
                    big = BIG_[0:64, :].rearrange("p (b v) -> p b v", b=DB)
                    kept(dve.tensor_tensor(big, bank[0:64, :].rearrange("p (b v) -> p b v", b=DB), inner(const("rowseq"), HD), ALU.mult), ("wS4", h))
                    then(dve.tensor_reduce(KQ_[0:64, 64 * h:64 * h + 64], BIG_[0:64, :].rearrange("p (b v) -> p v b", b=DB), AX, ALU.add))
                dve.tensor_tensor(N_[0:r, :], E_[0:r, :], KQ_[0:r, 0:CW], ALU.subtract).then_inc(delta_state, 1)
                dve.wait_ge(delta_state, 1)
                copy(("oShift",), NT_[0:r, :])
                bank = get(("o4",))
                kept(dve.tensor_tensor(NT_[0:r, :], NT_[0:r, :], bank[0:r, 0:CW], ALU.add))
                for h in range(CH):
                    p = slice(64 * (h % 2), 64 * (h % 2) + 64)
                    dve.tensor_tensor(BIG_[0:r, :].rearrange("p (b v) -> p b v", b=DB), mid(N_[0:r, 64 * h:64 * h + 64], DB),
                                      inner(const("rowseq")[0:r, :], HD), ALU.mult).then_inc(expand_ready, 1)
                    s4 = S4_[p, 512 * (h // 2):512 * (h // 2) + 512]
                    s4v = s4.rearrange("p (b v) -> p b v", b=DB)
                    then(dve.tensor_tensor(s4v, s4v, inner(ex_cg[p, 12 + DB * h:12 + DB * h + DB], HD), ALU.mult))
                    bank = get(("S4", h))
                    kept(dve.tensor_tensor(s4, s4, bank[p, :], ALU.add))
                dve.wait_ge(vec_drained, V_AT[("S4", CH - 1)] + 1)
            dve.wait_ge(z_ready, 2)
            o = NT_[0:r, :]
            then(dve.tensor_tensor(T_[0:r, :], o, o, ALU.mult))
            then(dve.tensor_reduce(o_ss[0:r, :], hd(T_[0:r, :]), AX, ALU.add))
            then(dve.tensor_scalar(o_ss, o_ss, 1.0 / HD, EPS, ALU.mult, ALU.add))
            inv_root(o_ss)
            then(dve.tensor_tensor(hd(o), hd(o), inner(o_ss[0:r, :], HD), ALU.mult))
            then(dve.tensor_tensor(hd(o), hd(o), mid(c_gain[0:r, :], CH), ALU.mult))
            z = proj[0:r, t, CZ:CZ + CW]
            then(dve.tensor_tensor(z, z, o, ALU.mult))

        def route(dve, then, get, kept):
            bank = get(("logit", 0))
            then(dve.memset(logit, 0.0))
            then(dve.memset(glog, -3e38))
            dve.tensor_copy(logit[:, 0:NP, :], bank[:, 0:36 * NP].rearrange("p (t n) -> p t n", t=NP))
            kept(dve.tensor_copy(logit[0:NS, NP, :], bank[0:NS, 36 * NP:36 * NT]), ("logit", 0))
            then(dve.tensor_copy(glog[:, :, 0:NG], logit[:, :, 0:NG]))

            def eight(src):
                for t in range(NT):
                    ins = dve.max(top[:, t, :], src[:, t, :])
                then(ins)
                for t in range(NT):
                    ins = dve.max_index(idx_top[:, 8 * t:8 * t + 8], top[:, t, :], src[:, t, :])
                then(ins)
            it = idx_top.rearrange("p (t n) -> p t n", t=NT)
            eight(glog)
            dve.tensor_copy(gi, it[:, :, 0])
            then(dve.tensor_copy(ga, top[:, :, 0]))
            dve.tensor_tensor(top[:, :, 0:NG], logit[:, :, 0:NG], inner(ga, NG), ALU.subtract).then_inc(route_asked, 1)
            then(dve.tensor_tensor(em, mid(const("group"), NT), inner(gi, NE), ALU.is_equal))
            then(dve.tensor_tensor(el, logit[:, :, NG:36], em, ALU.mult))
            then(dve.tensor_scalar(em, em, -NEG, NEG, ALU.mult, ALU.add))
            then(dve.tensor_tensor(el, el, em, ALU.add))
            dve.wait_ge(route_got, 1)
            then(dve.tensor_reduce(ga, top[:, :, 0:NG], AX, ALU.add))
            then(dve.reciprocal(ga, ga))
            eight(el)
            dve.tensor_copy(e0, it[:, :, 0])
            then(dve.tensor_copy(e1, it[:, :, 1]))
            dve.tensor_tensor(p1, top[:, :, 1], top[:, :, 0], ALU.subtract).then_inc(route_asked, 1)
            for e, m in ((e0, m0), (e1, m1)):
                then(dve.tensor_tensor(m, mid(const("expert"), NT), inner(e, NE), ALU.is_equal))
            dve.tensor_tensor(msum, m0, m1, ALU.add).then_inc(masks_ready, 1)
            dve.wait_ge(route_got, 2)
            then(dve.tensor_scalar(p0, p1, 1.0, None, ALU.add))
            then(dve.reciprocal(p0, p0))
            then(dve.tensor_tensor(p0, p0, ga, ALU.mult))
            then(dve.tensor_tensor(p1, p1, p0, ALU.mult))
            bank = get(("rank", 0))
            then(dve.memset(rk, 0.0))
            dve.tensor_copy(rk[:, 0:NP, :], bank[:, 0:32 * NP].rearrange("p (t n) -> p t n", t=NP))
            dve.tensor_copy(rk[0:NS, NP, :], bank[0:NS, 32 * NP:32 * NT])
            kept(dve.tensor_reduce(counts[:, 0:1], bank[:, 160:192], AX, ALU.max), ("rank", 0))
            then(dve.tensor_copy(idx_cnt, counts[:, 0:1]))
            then(dve.memset(over_gate, 0.0))
            for k, (e, m, rr, oo, p, w) in enumerate(((e0, m0, r0, o0, p0, w0), (e1, m1, r1, o1, p1, w1_))):
                then(dve.tensor_tensor(em, m, rk, ALU.mult))
                then(dve.tensor_reduce(rr, em, AX, ALU.add))
                then(dve.tensor_scalar(oo, rr, float(CAP), None, ALU.is_ge))
                then(dve.tensor_tensor(gb, p, oo, ALU.mult))
                then(dve.tensor_tensor(em, m, inner(gb, NE), ALU.mult))
                then(dve.tensor_tensor(over_gate, over_gate, em, ALU.add))
                then(dve.tensor_tensor(w, p, gb, ALU.subtract))
                then(dve.tensor_scalar(tq, rr, float(CAP - 1), None, ALU.min))
                then(dve.scalar_tensor_tensor(tq, e, float(CAP), tq, ALU.mult, ALU.add))
                then(dve.tensor_copy(idx_ga[:, NT * k:NT * k + NT], tq))
                then(dve.tensor_tensor(gi, const("spare")[:, NT * k:NT * k + NT], tq, ALU.subtract))
                then(dve.tensor_tensor(gi, gi, oo, ALU.mult))
                then(dve.tensor_tensor(tq, tq, gi, ALU.add))
                ins = dve.tensor_copy(idx_sc[:, NT * k:NT * k + NT], tq)
                if k == 0:
                    then(ins)
                else:
                    ins.then_inc(index_ready, 1)

        @block.vector
        def _(dve):
            steps, roots, asks = [0], [0], [0]

            def then(ins):
                steps[0] += 1
                ins.then_inc(vec_step, 1)
                dve.wait_ge(vec_step, steps[0])

            def get(label):
                dve.wait_ge(vec_filled, V_AT[label] + 1)
                return v_bank(V_AT[label])

            def kept(ins, label=None):
                ins.then_inc(vec_drained, 1)
                if label is not None:
                    dve.wait_ge(vec_drained, V_AT[label] + 1)

            def inv_root(ap):
                roots[0] += 1
                dve.reciprocal(ap, ap).then_inc(root_asked, 1)
                dve.wait_ge(root_ready, roots[0])

            def norm_scale():
                then(dve.tensor_scalar(rstd, ssq, 1.0 / D, EPS, ALU.mult, ALU.add))
                inv_root(rstd)

            dve.memset(small[:, :], 1.0).then_inc(small_set, 1)
            dve.memset(zeros, 0.0).then_inc(zeros_ready, 1)
            dve.wait_ge(small_set, 1)
            dve.wait_ge(consts_loaded, 16)
            dve.wait_ge(x_loaded, 32)
            groups = ((128, slice(0, NP), NP), (NS, slice(NP, NT), 1))
            with dve.Fori(0, DEPTH) as L:
                dve.wait_ge(squares_ready, NT)
                norm_scale()
                dve.wait_ge(params_loaded, 16 * 6)

                def normal(t):
                    r = ROWS[t]
                    dve.tensor_scalar(hst[t % 2][0:r], x[0:r, t, :], rstd[0:r, t:t + 1], None, ALU.mult).then_inc(rows_ready, 1)

                def gained(label, t, h, gain):
                    bank = get(label)
                    kept(dve.tensor_tensor(hT[:, 4 * h:4 * h + 4, 128 * t:128 * t + ROWS[t]],
                                           bank[:, 0:4 * ROWS[t]].rearrange("p (k n) -> p k n", k=4),
                                           inner(gain[:, 4 * h:4 * h + 4], ROWS[t]), ALU.mult))
                normal(0)
                for t in range(NT):
                    if t + 1 < NT:
                        normal(t + 1)
                    for h in range(2):
                        gained(("norm1", t, h), t, h, g1)
                for c in cin:
                    dve.memset(c[:, 0:3], 0.0).then_inc(vec_step, 1)
                steps[0] += 2
                dve.wait_ge(vec_step, steps[0])
                n = XW - 3
                for i in range(NCT + 2):
                    if i < NCT:
                        c, a = cin[i % 2], acc[i % 2]
                        if i >= 2:
                            dve.wait_ge(silu_done, i - 1)
                        dve.wait_ge(conv_in, i + 1)
                        then(dve.tensor_scalar(a[:, 0:n], c[:, 0:n], taps[:, i, 24:25], None, ALU.mult))
                        for j in range(1, 4):
                            ins = dve.scalar_tensor_tensor(a[:, 0:n], c[:, j:j + n], taps[:, i, 24 + j:25 + j], a[:, 0:n], ALU.mult, ALU.add)
                            if j < 3:
                                then(ins)
                            else:
                                ins.then_inc(conv_done, 1)
                    if i >= 2:
                        j = i - 2
                        bank = get(("qkvP", j))
                        kept(dve.tensor_copy(qkv[:, 0:NP, 128 * j:128 * j + 128], bank[:, :].rearrange("p (t n) -> p t n", t=NP)))
                        bank = get(("qkvS", j))
                        kept(dve.tensor_copy(qkv[0:NS, NP, 128 * j:128 * j + 128], bank[0:NS, 0:128]))
                for i in range(3):
                    bank = get(("tail", i))
                    kept(dve.tensor_copy(tail_rows[:, 384 * i:384 * i + 384], bank[0:27, 0:384]))
                dve.wait_ge(act_drained, A_AT[("A", NT - 1, 1)] + 1)
                dve.wait_ge(mlp_params, 48)
                for r, ts, n in groups:
                    v = proj[0:r, ts, AV:AV + AW]
                    mean, var, sq = ln_mean[0:r, ts], ln_var[0:r, ts], ln_sq[0:r, 0:n, :]
                    then(dve.tensor_reduce(mean, v, AX, ALU.add))
                    then(dve.tensor_scalar(mean, mean, 1.0 / AW, None, ALU.mult))
                    then(dve.tensor_tensor(v, v, inner(mean, AW), ALU.subtract))
                    then(dve.tensor_tensor(sq, v, v, ALU.mult))
                    then(dve.tensor_reduce(var, sq, AX, ALU.add))
                then(dve.tensor_scalar(ln_var, ln_var, 1.0 / AW, EPS, ALU.mult, ALU.add))
                inv_root(ln_var)
                for r, ts, n in groups:
                    v = proj[0:r, ts, AV:AV + AW]
                    then(dve.tensor_tensor(v, v, inner(ln_var[0:r, ts], AW), ALU.mult))
                    ins = dve.tensor_tensor(v, v, mid(v_gain[0:r, :], n), ALU.mult)
                    if r == 128:
                        then(ins)
                    else:
                        ins.then_inc(vn_ready, 1)
                bank = get(("wsT",))
                kept(dve.tensor_tensor(wsT, bank[:, :].rearrange("p (h n) -> p h n", h=AH), mid(const("upto"), AH), ALU.mult))
                bank = get(("rep",))
                kept(dve.tensor_copy(rep_w, bank[0:DS, 0:AH * NS]))
                bank = get(("ws4",))
                then(dve.tensor_tensor(ws4, bank[0:NS, 0:AH * NS].rearrange("p (h n) -> p h n", h=AH), mid(const("same4"), AH), ALU.mult))
                kept(dve.tensor_copy(bias_s[0:NS, :], bank[0:NS, 128:128 + AH]), ("ws4",))
                for t in range(NT):
                    bank = get(("gate", t))
                    r = ROWS[t]
                    bias = bias_p if t < NP else bias_s
                    for h in range(AH):
                        u = proj[0:r, t, AU + 64 * h:AU + 64 * h + 64]
                        ins = dve.scalar_tensor_tensor(u, bank[0:r, 64 * h:64 * h + 64], bias[0:r, h:h + 1], u, ALU.add, ALU.mult)
                    kept(ins)
                dve.wait_ge(act_drained, A_AT[("C", NT - 1, 1)] + 1)
                for r, ts, n in groups:
                    for t in range(ts.start, ts.stop):
                        heads = proj[0:r, t, BQ:BQ + 2 * BW].rearrange("p (h n) -> p h n", h=2 * BH)
                        x1, x2 = heads[:, :, 0:8], heads[:, :, 8:16]
                        cos = mid(const("cos")[0:r, 8 * t:8 * t + 8], 2 * BH)
                        sin = mid(const("sin")[0:r, 8 * t:8 * t + 8], 2 * BH)
                        tt = [b[0:r, 96 * (t % NP):96 * (t % NP) + 96].rearrange("p (h n) -> p h n", h=2 * BH) for b in rope_t]
                        dve.tensor_tensor(tt[0], x1, cos, ALU.mult)
                        dve.tensor_tensor(tt[1], x2, sin, ALU.mult)
                        dve.tensor_tensor(tt[2], x2, cos, ALU.mult)
                        then(dve.tensor_tensor(tt[3], x1, sin, ALU.mult))
                        dve.tensor_tensor(x1, tt[0], tt[1], ALU.subtract)
                        ins = dve.tensor_tensor(x2, tt[2], tt[3], ALU.add)
                        if t < NT - 1:
                            then(ins)
                        else:
                            ins.then_inc(rope_done, 1)
                dve.tensor_copy(gates[:, 0:NP, :], proj[:, 0:NP, CB:CB + 12])
                dve.tensor_copy(gates[0:NS, NP, :], proj[0:NS, NP, CB:CB + 12]).then_inc(gate_asked, 1)
                dve.wait_ge(gate_asked, 1)
                dve.wait_ge(gate_got, 1)
                then(dve.tensor_scalar(beta, beta, 1.0, None, ALU.add))
                then(dve.reciprocal(beta, beta))
                then(dve.tensor_tensor(soft, gates[:, :, CH:2 * CH], mid(dt_bias, NT), ALU.add))
                dve.scalar_tensor_tensor(decay, soft, -1.0, soft, ALU.mult, ALU.max).then_inc(gate_asked, 1)
                dve.wait_ge(gate_got, 2)
                then(dve.scalar_tensor_tensor(soft, soft, 0.0, decay, ALU.max, ALU.add))
                then(dve.scalar_tensor_tensor(decay, soft, -1.0, mid(a_log, NT), ALU.mult, ALU.mult))
                for t in range(NT):
                    r = ROWS[t]
                    qk = qkv[0:r, t, 0:2 * CW]
                    sq = work[0:r, 0:2 * CW]
                    then(dve.tensor_tensor(sq, qk, qk, ALU.mult))
                    then(dve.tensor_reduce(l2[0:r, t, :], hd(sq, 12), AX, ALU.add))
                then(dve.tensor_scalar(l2, l2, EPS, None, ALU.add))
                inv_root(l2)
                then(dve.tensor_scalar(l2[:, :, 0:CH], l2[:, :, 0:CH], SCALE, None, ALU.mult))
                dve.memset(state, 0.0)
                then(dve.memset(KZ_, 0.0))
                for t in range(NT):
                    delta_vec(dve, t, then, get, kept, inv_root)
                n = BH * NP
                for i in range(n + 2):
                    if i < n:
                        t = i % NP
                        keys = 128 * (t + 1)
                        if i >= 2:
                            dve.wait_ge(act_filled, A_AT[("P", i - 2)] + 1)
                        bank = get(("S", i))
                        kept(dve.tensor_tensor_reduce(prob[i % 2][:, 0:keys], bank[:, 0:keys], const("pmask")[:, 384 - 128 * t:512],
                                                      SCALE, -3e38, ALU.add, ALU.max, a_max[:, i:i + 1]), ("S", i))
                        dve.tensor_scalar(a_max[:, i:i + 1], a_max[:, i:i + 1], -1.0, None, ALU.mult).then_inc(probs_asked, 1)
                    if i >= 2:
                        j = i - 2
                        h, t = divmod(j, NP)
                        bank = get(("O", j))
                        dve.wait_ge(probs_ready, j + 1)
                        then(dve.reciprocal(a_sum[:, j:j + 1], a_sum[:, j:j + 1]))
                        kept(dve.tensor_scalar(proj[:, t, BQ + 64 * h:BQ + 64 * h + 64], bank[:, 0:64], a_sum[:, j:j + 1], None, ALU.mult))
                for G in range(2):
                    if G == 0:
                        then(dve.memset(qblk, 0.0))
                        dve.wait_ge(act_drained, A_AT[("bks", 2)] + 1)
                        for h in range(BH):
                            p = 64 * (h % 2)
                            ins = dve.tensor_copy(qblk[p:p + 64, :, h // 2, DS * h:DS * h + DS],
                                                  qTb[h // 2][p:p + 64, SEQ:NTOK].rearrange("p (b s) -> p b s", b=DB))
                        ins.then_inc(qblk_ready, 1)
                    for i, (name, c, cols) in enumerate((("sd", 0, 384), ("sr", 384, 512), ("sn", 896, 32))):
                        bank = get((name, G))
                        mask = const("smask")[:, c:c + cols] if i < 2 else const("smask")[:, 896 + 32 * G:928 + 32 * G]
                        kept(dve.tensor_tensor_reduce(sprob[:, c:c + cols], bank[:, 0:cols], mask, SCALE, -3e38, ALU.add, ALU.max,
                                                      s_max[:, i:i + 1]), (name, G))
                    then(dve.tensor_reduce(s_max[:, 3:4], s_max[:, 0:3], AX, ALU.max))
                    dve.tensor_scalar(s_max[:, 4:5], s_max[:, 3:4], -1.0, None, ALU.mult).then_inc(sprob_asked, 1)
                    dve.wait_ge(sprob_got, G + 1)
                    then(dve.reciprocal(s_sum[:, 1:2], s_sum[:, 0:1]))
                    dve.tensor_scalar(sprob, sprob, s_sum[:, 1:2], None, ALU.mult).then_inc(sprob_ready, 1)
                    for name, dst, rr, cols in (("pd", spd, NDIL, 512), ("pr", spr, 128, 512), ("pn", spn, NS, 128)):
                        bank = get((name, G))
                        kept(dve.tensor_copy(dst[0:rr, 0:cols], bank[0:rr, 0:cols]))
                    for b in range(4):
                        bank = get(("ov", G, b))
                        at = DS * (4 * G + b)
                        for hh in range(2):
                            p = 64 * hh
                            ins = dve.tensor_copy(o4T[p:p + 64, :, at:at + DS],
                                                  bank[p:p + 64, 0:24].rearrange("p (g n) -> p g n", g=3)[:, :, DS * hh:DS * hh + DS])
                        kept(ins)
                dve.wait_ge(vec_drained, V_AT[("ov", 1, 3)] + 1)
                dve.tensor_copy(hT[:, 2:5, SEQ:NTOK], o4T).then_inc(mix_ready, 1)
                for c in range(2):
                    for t in range(NT):
                        bank = get(("out", c, t))
                        xs = x[0:ROWS[t], t, 512 * c:512 * c + 512]
                        kept(dve.tensor_tensor(xs, xs, bank[0:ROWS[t], :], ALU.add))
                dve.wait_ge(squares_ready, 2 * NT)
                norm_scale()
                dve.wait_ge(pool_stored, (L + 1) * (16 * STORES))
                dve.sem_inc(aside, 1)
                for t in range(NT):
                    r = ROWS[t]
                    dve.tensor_scalar(h2[0:r, t, :], x[0:r, t, :], rstd[0:r, t:t + 1], None, ALU.mult).then_inc(rows_ready, 1)
                for t in range(NT):
                    for h in range(2):
                        gained(("norm2", t, h), t, h, g2)
                route(dve, then, get, kept)

                def expert(k, rnd):
                    jobs = rnd * (2 * EUN)
                    dve.wait_ge(vec_filled, jobs + (V0 + 2 * k + 1))
                    dve.tensor_tensor(rowsT[k % 2].rearrange("p (k n) -> p k n", k=KT),
                                      v_bank(V0 + 2 * k)[:, :].rearrange("p (k n) -> p k n", k=KT), inner(g2, CAP), ALU.mult).then_inc(vec_drained, 1)
                    dve.wait_ge(act_gated, rnd * EUN + (k + 1))
                    dve.tensor_tensor(hid[k % 2], gate_act[k % 2], v_bank(V0 + 2 * k + 1)[:, 128:256], ALU.mult).then_inc(vec_drained, 1)
                with dve.Fori(0, NE // EUN) as rnd:
                    for k in range(EUN):
                        expert(k, rnd)
                for k in range(NE - ELOOP):
                    expert(k, NE // EUN)
                per = ((NT + 1) // 2 * 16, NT // 2 * 16)
                for t in range(NT):
                    r = ROWS[t]
                    for k in range(2):
                        j = (t % 2) * 2 + k
                        dve.wait_ge(gathered[j], L * per[t % 2] + 16 * (t // 2 + 1))
                        w = (w0, w1_)[k][0:r, t:t + 1]
                        ins = dve.scalar_tensor_tensor(x[0:r, t, :], got[j][0:r, :], w, x[0:r, t, :], ALU.mult, ALU.add)
                        if k == 0:
                            then(ins)
                        elif t < NT - 1:
                            ins.then_inc(got_used, 1)
                        else:
                            ins.then_inc(moe_done, 1)
                dve.wait_ge(moe_done, 1)
                over = dve.value_load(idx_cnt[0:1, 0:1], min_val=0, max_val=NTOK)
                with dve.If(over > CAP):
                    dve.sem_inc(fb_added, 1)
                    with dve.Fori(0, NE) as e:
                        for f in range(2):
                            dve.wait_ge(fb_silu, e * 2 + (f + 1))
                            dve.tensor_tensor(fb_hid[:, f, 0:SEQ], fb_act[:, f, 0:SEQ], psum[2 * f + 1][:, :], ALU.mult)
                            dve.tensor_tensor(fb_hid[:, f, SEQ:NTOK], fb_act[:, f, SEQ:NTOK], psum[4 + f][:, 64:64 + NS],
                                              ALU.mult).then_inc(fb_prod, 1)
                        for t in range(NT):
                            r = ROWS[t]
                            dve.wait_ge(fb_down, e * NT + (t + 1))
                            for c in range(2):
                                xs = x[0:r, t, 512 * c:512 * c + 512]
                                ins = dve.scalar_tensor_tensor(xs, psum[6 + c][0:r, :], over_gate[0:r, t, bass.ds(e, 1)], xs, ALU.mult, ALU.add)
                            ins.then_inc(fb_added, 1)
                leave_layer(dve, L)
            dve.wait_ge(fin_step, NT)
            dve.tensor_scalar(rstd, ssq, 1.0 / D, EPS, ALU.mult, ALU.add).then_inc(small_set, 1)
            dve.wait_ge(small_set, 2)
            dve.reciprocal(rstd, rstd).then_inc(fin_step, 1)
            dve.wait_ge(fin_step, NT + 2)
            dve.wait_ge(fin_gain, 16)
            for t in range(NT):
                r = ROWS[t]
                dve.scalar_tensor_tensor(x[0:r, t, :], x[0:r, t, :], rstd[0:r, t:t + 1], g_final[0:r, :], ALU.mult, ALU.mult).then_inc(fin_row, 1)


_IN = ["x_prompt", "x_sample", "cache_win_k", "cache_win_v", "state_conv", "state_delta", "norm1_g", "w_in", "a_vnorm_g",
       "a_ws", "a_bs", "c_conv_w", "c_a_log", "c_dt_bias", "c_norm_g", "w_out", "norm2_g", "w_group", "w_router", "w1", "w3",
       "w2", "final_g"]
_OUT = [("y_prompt", (1, SEQ, D)), ("y_sample", (DB, DS, D)), ("win_k_prompt", (DEPTH, 1, SEQ, BH, HD)),
        ("win_v_prompt", (DEPTH, 1, SEQ, BH, HD)), ("conv_prompt", (DEPTH, 1, 3, CCH)), ("delta_prompt", (DEPTH, 1, CH, HD, HD)),
        ("win_k_sample", (DEPTH, DB, DS, BH, HD)), ("win_v_sample", (DEPTH, DB, DS, BH, HD)), ("chunk_v_sample", (DEPTH, DB, DS, AW)),
        ("conv_sample", (DEPTH, DB, 3, CCH)), ("delta_sample", (DEPTH, DB, CH, HD, HD))]


def kernel(**inputs):
    import concourse.bacc as bacc
    from concourse.bass_utils import run_bass_kernel_spmd as run

    nc = bacc.Bacc("TRN2", target_bir_lowering=False, num_devices=1)
    table, at = constants()
    arrays = {"in_" + k: np.ascontiguousarray(inputs[k]) for k in _IN}
    arrays["in_consts"] = table
    ins = {k[3:]: nc.dram_tensor(k, a.shape, F32, kind="ExternalInput").ap() for k, a in arrays.items()}
    outs = {k: nc.dram_tensor("out_" + k, shape, F32, kind="ExternalOutput").ap() for k, shape in _OUT}
    x_lists = nc.dram_tensor("x_lists", (NE * CAP + 2 * 128 * NT, D), F32, kind="Internal").ap()
    y_lists = nc.dram_tensor("y_lists", (NE * CAP, D), F32, kind="Internal").ap()
    build(nc, ins, outs, at, x_lists, y_lists)
    r = run(nc, [arrays], core_ids=[0])
    return tuple(r.results[0]["out_" + k] for k, _ in _OUT)
```

```python
from contextlib import ExitStack

import numpy as np
import concourse.bass as bass
from concourse import mybir

F32 = mybir.dt.float32
U32 = mybir.dt.uint32
I32 = mybir.dt.int32
ALU = mybir.AluOpType
ACT = mybir.ActivationFunctionType
AX = mybir.AxisListType.X

DEPTH, D, SEQ, DB, DS, PAST = 2, 1024, 512, 8, 4, 2048
NP, KT = SEQ // 128, D // 128
NT = NP + 1
NS = DB * DS
NTOK = SEQ + NS
HD, AH, BH, CH = 64, 4, 6, 6
AW, BW, CW = AH * HD, BH * HD, CH * HD
PROJ = 2 * AW + 3 * BW + 4 * CW + 2 * CH
CONV0 = 2 * AW + 3 * BW
CCH = 3 * CW
NCT = CCH // 128
NE, NG, DE, CAP = 32, 4, 256, 64
EPS = 1e-6
NEG = -1e30
SCALE = HD ** -0.5
ROWS = [128] * NP + [NS]
AU, AV, BQ, BK, BV, CZ, CB = 0, AW, 2 * AW, 2 * AW + BW, 2 * AW + 2 * BW, 2 * AW + 3 * BW, 2 * AW + 3 * BW + CW
PW = CB + 2 * CH
MIXCOL = [AU, AU + 128, BQ, BQ + 128, BQ + 256, CZ, CZ + 128, CZ + 256]
SLOT = 6144
WIN = 2048
NDIL = (WIN - 512) // 16


def constants():
    t = {}
    i = np.arange(128)
    blk, loc, col = i // 64, i % 64, np.arange(64)
    f = np.float32
    same = blk[:, None] == blk[None, :]
    t["ident"] = np.eye(128)
    t["le"] = same & (i[:, None] <= i[None, :])
    t["gt"] = same & (i[:, None] > i[None, :])
    t["ch0"] = np.broadcast_to((blk == 0)[:, None], (128, 128))
    t["ch1"] = np.broadcast_to((blk == 1)[:, None], (128, 128))
    t["gtc"] = loc[:, None] > col[None, :]
    t["lec"] = loc[:, None] <= col[None, :]
    t["idc"] = loc[:, None] == col[None, :]
    b16 = loc[:, None] // 16 == col[None, :] // 16
    b32 = loc[:, None] // 32 == col[None, :] // 32
    t["nlow16"] = -1.0 * (t["gtc"] & b16)
    t["nup16"] = -1.0 * ((loc[:, None] < col[None, :]) & b16)
    t["low32"] = t["gtc"] & b32 & ~b16
    t["low64"] = t["gtc"] & ~b32
    j = np.arange(NS)
    sb = j[:, None] // DS == j[None, :] // DS
    t["le4"] = sb & (j[:, None] <= j[None, :])
    t["gt4"] = sb & (j[:, None] > j[None, :])
    t["nlow4"] = -1.0 * t["gt4"]
    t["nup4"] = -1.0 * (sb & (j[:, None] < j[None, :]))
    t["same4"] = sb
    t["rowseq"] = (np.arange(64)[:, None] % NS) // DS == np.arange(DB)[None, :]
    t["rep4"] = np.arange(DS)[:, None] == j[None, :] % DS
    t["ones"] = np.ones((128, 128))
    t["before"] = i[:, None] < i[None, :]
    t["upto"] = i[:, None] <= i[None, :]
    t["expert"] = np.broadcast_to(np.arange(NE), (128, NE))
    t["group"] = np.broadcast_to(np.arange(NE) // 8, (128, NE))
    t["spare"] = NE * CAP + i[:, None] + 128 * np.arange(2 * NT)[None, :]

    def logmult(delta, scale):
        m = ((delta >= 0) & (delta <= 128)) * 1
        m = m + ((delta >= 0) & (delta <= 512) & (delta % 4 == 0)) + ((delta >= 0) & (delta <= 2048) & (delta % 16 == 0))
        return np.where(m > 0, np.log(np.maximum(m, 1)) / scale, NEG)

    t["pmask"] = logmult(i[:, None] + 384 - np.arange(512)[None, :], SCALE)
    r = i % 32
    s = r % DS
    kd = np.concatenate([16 * np.arange(NDIL) + a for a in range(4)])
    kr = np.concatenate([WIN - 512 + 4 * np.arange(128) + a for a in range(4)])
    sm = logmult(WIN + s[:, None] - np.concatenate([kd, kr])[None, :], SCALE)
    new = []
    for g in range(2):
        own = (4 * g + i // 32)[:, None] == (j // DS)[None, :]
        m = np.where(own, logmult(s[:, None] - (j % DS)[None, :], SCALE), NEG)
        new.append(m)
    sm = np.concatenate([sm] + new, 1)
    sm[r >= BH * DS] = 0.0
    t["smask"] = sm
    t["ownhead"] = (r // DS)[:, None] == np.arange(BH)[None, :]
    t["token16"] = (i // 32)[:, None] * DS + s[:, None] == np.arange(4 * DS)[None, :]
    inv = np.power(f(500000.0), (-np.arange(0, 16, 2, dtype=f) / f(16))).astype(f)
    pos = np.zeros((128, NT), f)
    for q in range(NP):
        pos[:, q] = 128 * q + i
    pos[:NS, NP] = PAST + j % DS
    ang = (pos[:, :, None] * inv[None, None, :]).astype(f)
    t["cos"] = np.cos(ang.astype(np.float64)).reshape(128, -1)
    t["sin"] = np.sin(ang.astype(np.float64)).reshape(128, -1)
    at, parts, n = {}, [], 0
    for k, v in t.items():
        v = np.asarray(v, f)
        at[k] = (n, v.shape[0], v.shape[1])
        full = np.zeros((128, v.shape[1]), f)
        full[: v.shape[0]] = v
        parts.append(full)
        n += v.shape[1]
    return np.ascontiguousarray(np.concatenate(parts, 1)), at


STEPS = BH * NP
SIDE_POINTS = tuple(range(15))
NSIDE = 6 + STEPS + 3


def beside(t, point):
    if point not in SIDE_POINTS:
        return []
    n = len(SIDE_POINTS) * t + SIDE_POINTS.index(point)
    if t == NP - 1 and point == SIDE_POINTS[-1]:
        return list(range(n, NSIDE))
    return [n] if n < NSIDE else []


def side_jobs(n):
    if n < 6:
        name, g = ("bq", "bk")[n % 2], n // 2
        return [(name, g), (name + "s", g)], []
    i = n - 6
    a = [("P", i - 2)] if 0 <= i - 2 < STEPS else []
    v = [("O", i - 3)] if 0 <= i - 3 < STEPS else []
    return a, v + ([("S", i)] if i < STEPS else [])


def schedule():
    a, v = [], []
    a.append(("tapsT",))
    for t in range(NT):
        v += [("norm1", t, 0), ("norm1", t, 1)]
    for i in range(NCT + 2):
        if i < NCT:
            a += ([("convR", i // 3)] if i % 3 == 0 else []) + [("convP", i), ("convS", i)]
        if i >= 2:
            v += [("qkvP", i - 2), ("qkvS", i - 2)]
    v += [("tail", i) for i in range(3)]
    for piece in "ABC":
        for t in range(NT):
            a += [(piece, t, 0), (piece, t, 1)]
    v += [("wsT",), ("rep",), ("ws4",)]
    v += [("gate", t) for t in range(NT)]
    for t in range(NT):
        def side(point, t=t):
            for n in beside(t, point):
                jobs = side_jobs(n)
                a.extend(jobs[0])
                v.extend(jobs[1])
        a += [("cg", t), ("D", t), ("DT", t)]
        v += [("qT", t), ("kT", t), ("bT", t)]
        if t < NP:
            side(0)
        v += [("AA", t), ("AT0", t), ("AT1", t)]
        if t < NP:
            side(1)
        a += [("N2", t)]
        v += [("N2T", t)]
        if t < NP:
            side(2)
            a += [("N4", t)]
            v += [("N4T", t)]
        v += [("M1", t)]
        if t < NP:
            side(3)
            a += [("N8", t)]
            v += [("M2", t)]
            side(4)
            v += [("M3", t)]
            side(5)
            for m, b in enumerate((32, 64)):
                a += [("T", t, b), ("Y", t, b)]
                side(6 + 2 * m)
                v += [("X", t, b)]
                side(7 + 2 * m)
        v += [("u", t)]
        a += [("wT", t, c) for c in range(2 if t < NP else 1)]
        v += [("qdT", t)]
        if t < NP:
            side(10)
            for c in range(2):
                v += [("wS", t, c)]
                side(11 + 2 * c)
                v += [("o", t, c), ("S", t, c)]
                side(12 + 2 * c)
        else:
            v += [("wS4", h) for h in range(CH)] + [("oShift",), ("o4",)] + [("S4", h) for h in range(CH)]
    for G in range(2):
        for b in range(4):
            for g in range(3):
                a += [("kd", G, b, g), ("kr", G, b, g)]
        v += [("sd", G), ("sr", G), ("sn", G)]
        v += [("pd", G), ("pr", G), ("pn", G)]
        v += [("ov", G), ("oT", G)]
    for t in range(NT):
        a += [("mixT", t, 0), ("mixT", t, 1)]
    for c in range(2):
        for t in range(NT):
            v += [("out", c, t)]
    for t in range(NT):
        v += [("norm2", t, 0), ("norm2", t, 1)]
    v += [("logit", 0), ("rank", 0)]
    return a, v


def build(nc, ins, outs, consts_at, x_lists, y_lists):
    c_dram = ins["consts"]
    ctx = ExitStack()
    with ctx:
        def sb(name, cols, dt=F32, rows=128):
            return ctx.enter_context(nc.sbuf_tensor(name, [rows, cols], dt))

        NCONST = c_dram.shape[1]
        consts = sb("consts", NCONST)
        x = sb("x", NT * D)[:, :].rearrange("p (t d) -> p t d", t=NT)
        hT_raw = sb("hT_raw", KT * NTOK)
        proj_raw = sb("proj_raw", NT * PW)
        ring = sb("ring", 3 * SLOT)
        qkv_raw = sb("qkv_raw", NT * CCH)
        work = sb("work", 12 * CW)
        small = sb("small", 600)
        state = sb("state", CW)[:, :]
        idx = sb("idx", 8 * NT + 4 * NT + 1, U32)
        idx_top, idx_sc, idx_ga = idx[:, 0:40], idx[:, 40:50], idx[:, 50:60]
        idx_cnt = idx[:, 60:61].bitcast(I32)

        hT = hT_raw[:, :].rearrange("p (k n) -> p k n", k=KT)
        proj = proj_raw[:, :].rearrange("p (t n) -> p t n", t=NT)
        qkv = qkv_raw[:, :].rearrange("p (t n) -> p t n", t=NT)

        def const(name):
            n, r, c = consts_at[name]
            return consts[0:r, n:n + c]

        ident = const("ident")

        class Cut:
            def __init__(self, tensor, at=0):
                self.tensor, self.at = tensor, at

            def __call__(self, cols, rows=128):
                self.at += cols
                assert self.at <= self.tensor.shape[1], (self.at, self.tensor.shape)
                return self.tensor[0:rows, self.at - cols:self.at]

        cut = Cut(small)
        g1, g2 = cut(KT), cut(KT)
        c_gain = cut(HD)
        a_log, dt_bias = cut(CH), cut(CH)
        bias_p = cut(AH)
        bias_s = cut(AH)
        w_ba = cut(KT * 12).rearrange("p (k n) -> p k n", k=KT)
        ssq, rstd = cut(NT), cut(NT)
        ln_mean, ln_var = cut(NT), cut(NT)
        gates = cut(NT * 12).rearrange("p (t n) -> p t n", t=NT)
        beta, decay = (cut(NT * CH).rearrange("p (t n) -> p t n", t=NT) for _ in range(2))
        soft = cut(NT * CH).rearrange("p (t n) -> p t n", t=NT)
        ex_cg = cut(60)
        l2 = cut(NT * 12).rearrange("p (t n) -> p t n", t=NT)
        o_ss = cut(CH)
        s_max, s_sum = cut(8), cut(8)

        hst = [qkv_raw[:, D * i:D * i + D] for i in range(2)]
        cut = Cut(work)
        XW = 3 + SEQ + 7 * DB
        cin = [cut(XW + 1)[:, 0:XW] for _ in range(2)]
        acc = [cut(XW) for _ in range(2)]
        sil = [cut(NTOK) for _ in range(2)]
        taps = cut(NCT * 28).rearrange("p (c n) -> p c n", c=NCT)
        tail = cut(NCT * 27).rearrange("p (c n) -> p c n", c=NCT)
        tail_rows = proj_raw[0:27, NP * PW + BK:NP * PW + BK + CCH]
        state_rows = proj_raw[0:28, 0:CCH]
        zeros = proj_raw[:, 5 * D:6 * D]
        conv_rows = proj_raw[0:NS, CCH:2 * CCH]
        g_final = proj_raw[:, 0:D]
        cut = Cut(work)
        ln_sq = cut(NP * AW).rearrange("p (t n) -> p t n", t=NP)
        ws_raw = cut(AH * 128).rearrange("p (h n) -> p h n", h=AH)
        wsT = cut(AH * 128).rearrange("p (h n) -> p h n", h=AH)
        rep_w = cut(AH * NS, DS)
        ws4 = cut(AH * NS, NS).rearrange("p (h n) -> p h n", h=AH)
        v_gain = cut(AW)
        rope_t = [cut(NP * 96) for _ in range(4)]
        c1, c2 = Cut(work), Cut(ring, 2 * SLOT)
        N_, NT_, U_, T_, Y_, aT_, kb_, rw_, qd_, kd_, N2_, N2T_ = (c1(CW) for _ in range(12))
        Sp_ = state
        BIG_ = work[:, 3 * CW:3 * CW + DB * HD]
        A32_, A64_, N4_, N4T_ = (c2(CW) for _ in range(4))
        S4_ = ring[:, 2 * SLOT:2 * SLOT + 3 * DB * HD]
        E_, ET_ = (c2(CW) for _ in range(2))
        KZ_ = c2(CH * 128).rearrange("p (h n) -> p h n", h=CH)
        KQ_ = c2(2 * CW)
        Sg_ = c2(CW)
        gt4_ = c2(CH * DB)
        probT = [c2(SEQ) for _ in range(2)]
        a_max, a_sum = c2(STEPS), c2(STEPS)
        O_ = c2(CW)
        cut = Cut(hT_raw)
        qTb = [cut(NTOK) for _ in range(3)]
        kTb = [cut(NTOK) for _ in range(3)]
        prob = [cut(SEQ) for _ in range(2)]
        cut = Cut(qkv_raw)
        keysT = [cut(896) for _ in range(2)]
        cut = Cut(work)
        sprob = cut(928)
        spd, spr, spn = cut(512), cut(512), cut(128)
        own = spd[:, 0:BW]
        qblk = cut(DB * 3 * 32).rearrange("p (b g n) -> p b g n", b=DB, g=3)
        o4T = cut(3 * NS).rearrange("p (g n) -> p g n", g=3)
        cut = Cut(proj_raw)
        h2 = cut(NT * D).rearrange("p (t d) -> p t d", t=NT)
        rows_in = [proj_raw[0:CAP, D * i:D * i + D] for i in range(3)]
        rows_out = [cut(D // 2) for _ in range(3)]
        hidT = [cut(128) for _ in range(2)]
        rowsT = [cut(KT * CAP) for _ in range(2)]
        got = [proj_raw[:, D * i:D * i + D] for i in range(4)]
        w_route = qkv_raw[:, 3840:3840 + KT * 36].rearrange("p (k n) -> p k n", k=KT)
        junk1, junk2 = qkv_raw[:, 2 * D:3 * D], qkv_raw[:, 2 * D:3 * D]
        cut = Cut(qkv_raw)
        hid = [cut(128) for _ in range(2)]
        gate_act = [cut(128) for _ in range(2)]
        logit = cut(NT * 36).rearrange("p (t n) -> p t n", t=NT)
        glog = cut(NT * 8).rearrange("p (t n) -> p t n", t=NT)
        top = cut(NT * 8).rearrange("p (t n) -> p t n", t=NT)
        el, em, rk, m0, m1, msum = (cut(NT * NE).rearrange("p (t n) -> p t n", t=NT) for _ in range(6))
        over_gate = cut(NT * NE).rearrange("p (t n) -> p t n", t=NT)
        gi, ga, gb, e0, e1, r0, r1, o0, o1, p0, p1, w0, w1_, tq = (cut(NT) for _ in range(14))
        counts = cut(NE + 2)
        assert cut.at <= 2 * D
        fb_w = proj_raw[:, 0:SLOT]
        fb_hid = proj_raw[:, SLOT:SLOT + 2 * NTOK].rearrange("p (f n) -> p f n", f=2)
        fb_act = proj_raw[:, SLOT + 2 * NTOK:SLOT + 4 * NTOK].rearrange("p (f n) -> p f n", f=2)

        psum = [ctx.enter_context(nc.psum_tensor(f"bank{i}", [128, 512], F32)) for i in range(8)]

        keep = {}

        def lasting(name):
            keep[name] = ctx.enter_context(nc.semaphore(name))
            return keep[name]

        consts_loaded = lasting("consts_loaded")
        x_loaded = lasting("x_loaded")
        zeros_ready = lasting("zeros_ready")
        slot_full = [lasting(f"slot_full{i}") for i in range(3)]
        small_set = lasting("small_set")
        pool_stored = lasting("pool_stored")
        scattered = lasting("scattered")
        gathered = [lasting(f"gathered{i}") for i in range(4)]
        rows_loaded = [lasting(f"rows_loaded{i}") for i in range(3)]
        rows_stored = [lasting(f"rows_stored{i}") for i in range(3)]
        per_buffer = [len(range(i, NE, 3)) for i in range(3)]
        layer_left = lasting("layer_left")
        layer_cleared = lasting("layer_cleared")
        aside = lasting("aside")
        y_stored = lasting("y_stored")
        fin_row = lasting("fin_row")
        fin_step = lasting("fin_step")
        fin_gain = lasting("fin_gain")
        first_squares = lasting("first_squares")
        cleared = []

        def signal(name):
            cleared.append(ctx.enter_context(nc.semaphore(name)))
            return cleared[-1]

        act_filled, act_drained = signal("act_filled"), signal("act_drained")
        vec_filled, vec_drained = signal("vec_filled"), signal("vec_drained")
        vec_step, act_step = signal("vec_step"), signal("act_step")
        params_loaded = signal("params_loaded")
        taps_loaded = signal("taps_loaded")
        squares_ready = signal("squares_ready")
        root_asked = signal("root_asked")
        root_ready = signal("root_ready")
        rows_ready = signal("rows_ready")
        conv_in = signal("conv_in")
        conv_done = signal("conv_done")
        silu_done = signal("silu_done")
        tail_copied = signal("tail_copied")
        tail_stored = signal("tail_stored")
        mlp_params = signal("mlp_params")
        vn_ready = signal("vn_ready")
        rope_done = signal("rope_done")
        z_ready = signal("z_ready")
        gate_asked, gate_got = signal("gate_asked"), signal("gate_got")
        delta_in = signal("delta_in")
        delta_w = signal("delta_w")
        delta_state = signal("delta_state")
        state_loaded = signal("state_loaded")
        state_stored = signal("state_stored")
        expand_ready = signal("expand_ready")
        keys_used = signal("keys_used")
        sprob_asked, sprob_got = signal("sprob_asked"), signal("sprob_got")
        mix_ready = signal("mix_ready")
        probs_asked, probs_ready = signal("probs_asked"), signal("probs_ready")
        qblk_ready = signal("qblk_ready")
        sprob_ready = signal("sprob_ready")
        norms_done = signal("norms_done")
        route_loaded = signal("route_loaded")
        route_asked, route_got = signal("route_asked"), signal("route_got")
        masks_ready = signal("masks_ready")
        index_ready = signal("index_ready")
        act_gated, hid_ready = signal("act_gated"), signal("hid_ready")
        got_used = signal("got_used")
        moe_done = signal("moe_done")
        fb_loaded, fb_up, fb_silu, fb_prod, fb_down, fb_added = (
            signal(n) for n in ("fb_loaded", "fb_up", "fb_silu", "fb_prod", "fb_down", "fb_added"))
        clear_range = range(min(s.num for s in cleared), max(s.num for s in cleared) + 1)
        assert not any(s.num in clear_range for s in keep.values())

        a_jobs, v_jobs = schedule()
        A_AT = {k: i for i, k in enumerate(a_jobs)}
        V_AT = {k: i for i, k in enumerate(v_jobs)}
        assert len(A_AT) == len(a_jobs) and len(V_AT) == len(v_jobs)
        A0, V0 = len(a_jobs), len(v_jobs)
        STORES = 7
        EUN = 6
        ELOOP = NE // EUN * EUN

        def a_bank(n):
            return psum[n % 4]

        def v_bank(n):
            return psum[4 + n % 4]

        def hd(ap, n=CH):
            return ap.rearrange("p (h n) -> p h n", h=n)

        def mid(ap, n):
            return ap[:, None, :].broadcast_to([ap.shape[0], n, ap.shape[1]])

        def inner(ap, n):
            return ap[:, :, None].broadcast_to([ap.shape[0], ap.shape[1], n])

        w_in, w_out = ins["w_in"], ins["w_out"]

        def layer_of(ap, L):
            names = "abcdefg"[:len(ap.shape) - 1]
            pat = " ".join(names)
            return ap[bass.ds(L, 1)].rearrange(f"o {pat} -> (o {names[0]}) {pat[2:]}" if len(names) > 1 else "o a -> (o a)")

        def win_cols(L, slot, at, c0, n):
            src = layer_of(w_in, L).rearrange("(p k) n -> p k n", k=KT)[:, :, c0:c0 + n]
            dst = ring[:, slot * SLOT + at:slot * SLOT + at + KT * n].rearrange("p (k n) -> p k n", k=KT)
            return dst, src

        def load_list():
            out = []
            for i in range(3):
                out.append(lambda L, s, i=i: [win_cols(L, s, 0, CONV0 + 384 * i, 384)])
            out.append(lambda L, s: [win_cols(L, s, 0, 0, 512)])
            out.append(lambda L, s: [win_cols(L, s, 0, BQ, 768)])
            out.append(lambda L, s: [win_cols(L, s, 0, BV, 384), win_cols(L, s, KT * 384, CONV0 + CCH, 384)])

            def cache(which, b0):
                def go(L, s):
                    r = []
                    for i in range(2):
                        src = layer_of(ins[which], L)[b0 + i].rearrange("n h d -> n (h d)")
                        base = s * SLOT + i * 3072
                        r.append((ring[0:NDIL, base:base + 1536],
                                  src[0:WIN - 512].rearrange("(p j) n -> p (j n)", j=16)[:, 0:1536]))
                        r.append((ring[:, base + 1536:base + 3072],
                                  src[WIN - 512:WIN].rearrange("(p j) n -> p (j n)", j=4)))
                    return r
                return go
            for G in range(2):
                for which in ("cache_win_k", "cache_win_v"):
                    for i in range(2):
                        out.append(cache(which, 4 * G + 2 * i))
            for c in range(2):
                def go(L, s, c=c):
                    src = layer_of(w_out, L).rearrange("(k p) n -> p k n", p=128)[:, :, 512 * c:512 * c + 512]
                    return [(ring[:, s * SLOT:s * SLOT + 4096].rearrange("p (k n) -> p k n", k=KT), src)]
                out.append(go)
            return out

        loads = load_list()
        E_AT = len(loads)
        NLOAD = E_AT + NE
        assert NLOAD % 3 == 0 and E_AT % 3 + 0 == 1
        ndma = [1, 1, 1, 1, 1, 2] + [4] * 8 + [1, 1] + [3] * NE
        full_at = []
        per = [0, 0, 0]
        for n in range(NLOAD):
            per[n % 3] += 16 * ndma[n]
            full_at.append(per[n % 3])
        SLOT_TOTAL = per

        def expert_src(L, e):
            w1 = layer_of(ins["w1"], L)[bass.ds(e, 1)].rearrange("o (p k) f -> (o p) (k f)", k=KT)
            w3 = layer_of(ins["w3"], L)[bass.ds(e, 1)].rearrange("o (p k) f -> (o p) (k f)", k=KT)
            w2 = layer_of(ins["w2"], L)[bass.ds(e, 1)].rearrange("o (p f) d -> (o p) (f d)", f=2)
            return w1, w3, w2

        def leave_layer(eng, L, clears=False):
            eng.drain().then_inc(layer_left, 1)
            eng.wait_ge(layer_left, (L + 1) * 5)
            eng.sem_inc(aside, 1)
            if clears:
                eng.sem_clear(clear_range)
                eng.sem_inc(layer_cleared, 1)
            eng.wait_ge(layer_cleared, L + 1)
            eng.sem_inc(aside, 1)

        def state_tile(g):
            return S4_[:, DB * HD * g:DB * HD * (g + 1)].rearrange("p (b v) -> p b v", b=DB)

        def mix_tiles(t, h):
            if t < NP:
                return list(range(4 * h, 4 * h + 4))
            return [0, 1] if h == 0 else [5, 6, 7]

        def dense_loads(sp, L):
            sp.wait_ge(moe_done, 1)
            over = sp.value_load(idx_cnt[0:1, 0:1], min_val=0, max_val=NTOK)
            with sp.If(over > CAP):
                with sp.Fori(0, NE) as e:
                    sp.wait_ge(fb_added, e * NT + 1)
                    sp.sem_inc(aside, 1)
                    for i, src in enumerate(expert_src(L, e)):
                        sp.dma_start(fb_w[:, 2048 * i:2048 * (i + 1)], src).then_inc(fb_loaded, 16)
            sp.sem_inc(aside, 1)

        block = ctx.enter_context(nc.Block())

        @block.sync
        def _(sp):
            sp.wait_ge(small_set, 1)
            sp.dma_start(x[:, 0:NP, :], ins["x_prompt"].rearrange("b (t p) d -> p (b t) d", p=128)).then_inc(x_loaded, 16)
            sp.dma_start(x[0:NS, NP, :], ins["x_sample"].rearrange("b s d -> (b s) d")).then_inc(x_loaded, 16)
            sp.dma_start(consts[:, :], c_dram).then_inc(consts_loaded, 16)

            def used_up(n):
                if n < 3:
                    return act_filled, A_AT[("convS", 3 * n + 2)] + 1
                if n < 6:
                    return act_filled, A_AT[("ABC"[n - 3], NT - 1, 1)] + 1
                if n < 14:
                    G, m = (n - 6) // 4, (n - 6) % 4
                    if m < 2:
                        return act_filled, A_AT[("kr", G, 2 * m + 1, 2)] + 1
                    return vec_filled, V_AT[("ov", G)] + 1
                if n < 16:
                    return vec_filled, V_AT[("out", n - 14, NT - 1)] + 1
                return act_filled, A0 + 2 * (n - 16) + 2

            def stream(L, n, dmas):
                if n >= 3 and n != 8:
                    sp.wait_ge(*used_up(n - 3))
                for dst, src in dmas:
                    sp.dma_start(dst, src).then_inc(slot_full[n % 3], 16)

            with sp.Fori(0, DEPTH) as L:
                lay = {k: layer_of(ins[k], L) for k in ("norm1_g", "norm2_g", "c_norm_g", "c_a_log", "c_dt_bias",
                                                        "state_conv", "c_conv_w", "a_bs", "w_in")}
                for dst, src in ((g1, lay["norm1_g"].rearrange("(p k) -> p k", k=KT)),
                                 (g2, lay["norm2_g"].rearrange("(p k) -> p k", k=KT)),
                                 (c_gain, lay["c_norm_g"][None, :].broadcast_to([128, HD])),
                                 (a_log, lay["c_a_log"][None, :].broadcast_to([128, CH])),
                                 (dt_bias, lay["c_dt_bias"][None, :].broadcast_to([128, CH])),
                                 (w_ba, lay["w_in"].rearrange("(p k) n -> p k n", k=KT)[:, :, PROJ - 12:PROJ])):
                    sp.dma_start(dst, src).then_inc(params_loaded, 16)
                sp.dma_start(state_rows[0:24, :], lay["state_conv"].rearrange("b r c -> (b r) c")).then_inc(taps_loaded, 16)
                sp.dma_start(state_rows[24:28, :], lay["c_conv_w"]).then_inc(taps_loaded, 16)
                for n in range(4):
                    stream(L, n, loads[n](L, n % 3))
                sp.wait_ge(vec_drained, V_AT[("tail", 2)] + 1)
                sp.dma_start(layer_of(outs["conv_prompt"], L).rearrange("b r c -> (b r) c"), tail_rows[0:3, :]).then_inc(tail_stored, 16)
                sp.dma_start(layer_of(outs["conv_sample"], L).rearrange("b r c -> (b r) c"), tail_rows[3:27, :]).then_inc(tail_stored, 16)
                sp.wait_ge(tail_stored, 32)
                sp.dma_start(ws_raw, layer_of(ins["a_ws"], L).rearrange("h p q -> p h q")).then_inc(mlp_params, 16)
                sp.dma_start(v_gain, layer_of(ins["a_vnorm_g"], L)[None, :].broadcast_to([128, AW])).then_inc(mlp_params, 16)
                sp.dma_start(bias_p, lay["a_bs"].rearrange("h p -> p h"), allow_slow_non_contiguous=True).then_inc(mlp_params, 16)
                for n in range(4, 8):
                    stream(L, n, loads[n](L, n % 3))
                sp.wait_ge(vec_drained, V_AT[("X", NP - 1, 64)] + 1)
                for g in range(3):
                    sp.dma_start(state_tile(g), layer_of(ins["state_delta"], L)[:, 2 * g:2 * g + 2].rearrange("b h k v -> (h k) b v")).then_inc(state_loaded, 16)
                sp.wait_ge(vec_drained, V_AT[("S4", CH - 1)] + 1)
                sp.dma_start(w_route[:, :, 0:NG], layer_of(ins["w_group"], L).rearrange("(p k) n -> p k n", k=KT)).then_inc(route_loaded, 16)
                sp.dma_start(w_route[:, :, NG:36], layer_of(ins["w_router"], L).rearrange("(p k) n -> p k n", k=KT)).then_inc(route_loaded, 16)
                sp.wait_ge(state_stored, 48)
                sp.wait_ge(norms_done, 1)
                for n in range(8, E_AT):
                    stream(L, n, loads[n](L, n % 3))

                def expert_load(e, slot):
                    base = slot * SLOT
                    for i, src in enumerate(expert_src(L, e)):
                        sp.dma_start(ring[:, base + 2048 * i:base + 2048 * (i + 1)], src).then_inc(slot_full[slot], 16)
                for e in range(3):
                    sp.wait_ge(*used_up(E_AT + e - 3))
                    expert_load(e, (E_AT + e) % 3)
                with sp.Fori(0, (NE - 3) // 3) as i:
                    for k in range(3):
                        sp.wait_ge(act_filled, i * 6 + (A0 + 2 * k + 2))
                        sp.sem_inc(aside, 1)
                        expert_load(i * 3 + (3 + k), (E_AT + k) % 3)
                for e in range(3 + (NE - 3) // 3 * 3, NE):
                    sp.wait_ge(*used_up(E_AT + e - 3))
                    expert_load(e, (E_AT + e) % 3)
                dense_loads(sp, L)
                leave_layer(sp, L)
            sp.dma_start(g_final, ins["final_g"][None, :].broadcast_to([128, D])).then_inc(fin_gain, 16)
            sp.wait_ge(fin_row, NT)
            sp.dma_start(outs["y_prompt"].rearrange("b (t p) d -> p (b t) d", p=128), x[:, 0:NP, :]).then_inc(y_stored, 16)
            sp.dma_start(outs["y_sample"].rearrange("b s d -> (b s) d"), x[0:NS, NP, :]).then_inc(y_stored, 16)
            sp.wait_ge(y_stored, 32)

        @block.gpsimd
        def _(pool):
            pool.wait_ge(zeros_ready, 1)
            pool.wait_ge(slot_full[0], 16)
            for i in range(3):
                blocks = 6 if i < 2 else 4
                pool.dma_start(x_lists[768 * i:768 * i + 128 * blocks, :].rearrange("(n p) d -> p n d", p=128),
                               mid(zeros, blocks)).then_inc(rows_stored[i], 16)
            with pool.Fori(0, DEPTH) as L:
                for ct in range(NCT):
                    pool.wait_ge(conv_in, ct + 1)
                    pool.tensor_copy(tail[:, ct, 0:3], cin[ct % 2][:, SEQ:SEQ + 3])
                    src = cin[ct % 2][:, 3 + SEQ:XW].rearrange("p (b n) -> p b n", b=DB)
                    pool.tensor_copy(tail[:, ct, 3:27].rearrange("p (b n) -> p b n", b=DB), src[:, :, 4:7]).then_inc(tail_copied, 1)
                pool.wait_ge(vn_ready, 1)
                pool.dma_start(layer_of(outs["chunk_v_sample"], L).rearrange("b s c -> (b s) c"),
                               proj[0:NS, NP, AV:AV + AW]).then_inc(pool_stored, 16)
                pool.wait_ge(rope_done, 1)
                pool.wait_ge(z_ready, 2)
                for name, c in (("win_k", BK), ("win_v", BV)):
                    pool.dma_start(layer_of(outs[name + "_prompt"], L).rearrange("b (t p) h d -> p (b t) (h d)", p=128),
                                   proj[:, 0:NP, c:c + BW]).then_inc(pool_stored, 16)
                    pool.dma_start(layer_of(outs[name + "_sample"], L).rearrange("b s h d -> (b s) (h d)"),
                                   proj[0:NS, NP, c:c + BW]).then_inc(pool_stored, 16)
                pool.wait_ge(vec_drained, V_AT[("S", NP - 1, 1)] + 1)
                for hh in range(2):
                    pool.dma_start(layer_of(outs["delta_prompt"], L).rearrange("b (g h) k v -> h k (b g) v", h=2)[hh],
                                   hd(state[64 * hh:64 * hh + 64, :])[:, hh::2, :]).then_inc(pool_stored, 16)
                for i in range(3):
                    pool.wait_ge(rows_stored[i], 16)
                for k in range(2):
                    pool.wait_ge(index_ready, k + 1)
                    for t in range(NT):
                        pool.indirect_dma_start(x_lists[:, :], bass.IndirectOffsetOnAxis(idx_sc[0:ROWS[t], NT * k + t:NT * k + t + 1], 0),
                                                h2[0:ROWS[t], t, :], None).then_inc(scattered, 16)
                pool.wait_ge(scattered, (L + 1) * (32 * NT))
                pool.sem_inc(aside, 1)

                def load_rows(e, k):
                    pool.dma_start(rows_in[k], x_lists[bass.ds(e * CAP, CAP), :]).then_inc(rows_loaded[k], 16)

                def store_rows(e, k):
                    for c in range(2):
                        pool.dma_start(y_lists[bass.ds(e * CAP, CAP), 512 * c:512 * c + 512],
                                       rows_out[k][CAP * c:CAP * c + CAP, :]).then_inc(rows_stored[k], 16)
                for e in range(3):
                    load_rows(e, e)
                for e in range(2):
                    pool.wait_ge(vec_filled, V0 + 2 * e + 1)
                    load_rows(e + 3, e)
                with pool.Fori(0, (NE - 5) // 3) as i:
                    for k in range(3):
                        pool.wait_ge(vec_filled, i * 6 + (V0 + 2 * (k + 2) + 1))
                        pool.sem_inc(aside, 1)
                        load_rows(i * 3 + (5 + k), (k + 2) % 3)
                        pool.wait_ge(act_drained, i * 6 + (A0 + 2 * k + 2))
                        pool.sem_inc(aside, 1)
                        store_rows(i * 3 + k, k)
                for e in range(NE - 5, NE):
                    pool.wait_ge(act_drained, A0 + 2 * e + 2)
                    store_rows(e, e % 3)
                for k in range(3):
                    pool.wait_ge(rows_stored[k], L * (32 * per_buffer[k]) + (32 * per_buffer[k] + 16))
                pool.sem_inc(aside, 1)
                for t in range(NT):
                    if t >= 2:
                        pool.wait_ge(got_used, t - 1)
                    for k in range(2):
                        j = (t % 2) * 2 + k
                        pool.indirect_dma_start(got[j][0:ROWS[t], :], None, y_lists[:, :],
                                                bass.IndirectOffsetOnAxis(idx_ga[0:ROWS[t], NT * k + t:NT * k + t + 1], 0)).then_inc(gathered[j], 16)
                pool.wait_ge(pool_stored, (L + 1) * (16 * STORES))
                pool.sem_inc(aside, 1)
                leave_layer(pool, L, clears=True)

        @block.scalar
        def _(act):
            steps = [0]
            roots, asked = [0], [0]

            def get(label):
                act.wait_ge(act_filled, A_AT[label] + 1)
                return a_bank(A_AT[label])

            def root(ap):
                roots[0] += 1
                act.wait_ge(root_asked, roots[0])
                act.activation(ap, ap, ACT.Sqrt).then_inc(root_ready, 1)

            act.wait_ge(x_loaded, 32)

            def squares(t, before, done):
                if before:
                    act.wait_ge(done, before)
                act.activation(junk1[0:ROWS[t]], x[0:ROWS[t], t, :], ACT.Square, accum_out=ssq[0:ROWS[t], t:t + 1]).then_inc(done, 1)
            for t in range(NT):
                squares(t, t, first_squares)
            with act.Fori(0, DEPTH) as L:
                root(rstd)
                bank = get(("tapsT",))
                act.activation(taps, bank[:, 0:NCT * 28].rearrange("p (c n) -> p c n", c=NCT), ACT.Copy).then_inc(act_drained, 1)
                for i in range(NCT + 1):
                    if i < NCT:
                        c = cin[i % 2]
                        seqs = c[:, 3 + SEQ:XW].rearrange("p (b n) -> p b n", b=DB)
                        if i >= 2:
                            act.wait_ge(conv_done, i - 1)
                            act.wait_ge(tail_copied, i - 1)
                        if i % 3 == 0:
                            bank = get(("convR", i // 3))
                            for q in range(4):
                                at = 384 * (i // 3) + 96 * q
                                out = act.activation(conv_rows[:, at:at + 96], bank[NS * q:NS * q + NS, 0:96], ACT.Copy)
                            out.then_inc(act_drained, 1)
                        bank = get(("convP", i))
                        act.activation(c[:, 3:3 + SEQ], bank[:, 0:SEQ], ACT.Copy).then_inc(act_drained, 1)
                        bank = get(("convS", i))
                        act.activation(seqs[:, :, 3:7], bank[:, 0:NS].rearrange("p (b n) -> p b n", b=DB), ACT.Copy).then_inc(act_drained, 1)
                        if i == 0:
                            act.wait_ge(act_drained, A_AT[("tapsT",)] + 1)
                        act.activation(seqs[:, :, 0:3], taps[:, i, 0:24].rearrange("p (b n) -> p b n", b=DB), ACT.Copy).then_inc(conv_in, 1)
                    if i >= 1:
                        j = i - 1
                        act.wait_ge(conv_done, j + 1)
                        if j >= 2:
                            act.wait_ge(vec_filled, V_AT[("qkvS", j - 2)] + 1)
                        a = acc[j % 2]
                        act.activation(sil[j % 2][:, 0:SEQ], a[:, 0:SEQ], ACT.Silu)
                        src = a[:, 3 + SEQ:XW].rearrange("p (b n) -> p b n", b=DB)[:, :, 0:DS]
                        act.activation(sil[j % 2][:, SEQ:NTOK].rearrange("p (b n) -> p b n", b=DB), src, ACT.Silu).then_inc(silu_done, 1)
                act.wait_ge(rows_stored[0], 16)
                act.wait_ge(rows_stored[1], 16)
                act.wait_ge(rows_stored[2], 16)
                where = {"A": ((AU, 512), (CB, 12)), "B": ((BQ, BW), (BK, BW)), "C": ((BV, BW), (CZ, CW))}

                def delta_gates():
                    root(l2)
                    act.wait_ge(gate_asked, 1)
                    act.activation(beta, gates[:, :, 0:CH], ACT.Exp, scale=-1.0)
                    act.wait_ge(params_loaded, 16 * 6)
                    act.activation(a_log, a_log, ACT.Exp).then_inc(gate_got, 1)
                    act.wait_ge(gate_asked, 2)
                    act.activation(decay, decay, ACT.Exp, scale=-1.0).then_inc(act_step, 1)
                    act.wait_ge(act_step, 1)
                    act.activation(decay, decay, ACT.Ln, bias=1.0).then_inc(gate_got, 1)
                    root(ln_var)
                for piece in "ABC":
                    for t in range(NT):
                        for j, (c, n) in enumerate(where[piece]):
                            if (piece, t, j) == ("B", NP, 0):
                                act.wait_ge(tail_stored, 32)
                            bank = get((piece, t, j))
                            if t == NP and n > 12:
                                for q in range(4):
                                    out = act.activation(proj[0:NS, NP, c + n // 4 * q:c + n // 4 * (q + 1)],
                                                         bank[NS * q:NS * q + NS, 0:n // 4], ACT.Copy)
                                out.then_inc(act_drained, 1)
                                continue
                            act.activation(proj[0:ROWS[t], t, c:c + n], bank[0:ROWS[t], 0:n], ACT.Copy).then_inc(act_drained, 1)
                    if piece == "A":
                        delta_gates()
                act.wait_ge(act_drained, A_AT[("C", NT - 1, 1)] + 1)
                act.activation(proj[:, 0:NP, CZ:CZ + CW], proj[:, 0:NP, CZ:CZ + CW], ACT.Silu).then_inc(z_ready, 1)
                act.activation(proj[0:NS, NP, CZ:CZ + CW], proj[0:NS, NP, CZ:CZ + CW], ACT.Silu).then_inc(z_ready, 1)
                def side(t, point):
                    for n in beside(t, point):
                        if n < 6:
                            name, g = ("bq", "bk")[n % 2], n // 2
                            dst = (qTb, kTb)[n % 2][g]
                            bank = get((name, g))
                            act.activation(dst[:, 0:SEQ], bank[:, 0:SEQ], ACT.Copy).then_inc(act_drained, 1)
                            bank = get((name + "s", g))
                            act.activation(dst[:, SEQ:NTOK], bank[:, 0:NS], ACT.Copy).then_inc(act_drained, 1)
                            continue
                        j = n - 7
                        if 0 <= j < STEPS:
                            keys = 128 * (j % NP + 1)
                            act.wait_ge(probs_asked, j + 1)
                            act.activation(prob[j % 2][:, 0:keys], prob[j % 2][:, 0:keys], ACT.Exp, bias=a_max[:, j:j + 1],
                                           accum_out=a_sum[:, j:j + 1]).then_inc(probs_ready, 1)
                        j = n - 8
                        if 0 <= j < STEPS:
                            keys = 128 * (j % NP + 1)
                            bank = get(("P", j))
                            if j >= 2:
                                act.wait_ge(vec_filled, V_AT[("O", j - 2)] + 1)
                            act.activation(probT[j % 2][:, 0:keys], bank[:, 0:keys], ACT.Copy).then_inc(act_drained, 1)
                for t in range(NT):
                    r, w = ROWS[t], (64 if t < NP else NS)
                    bank = get(("cg", t))
                    if t < NP:
                        act.activation(ex_cg[:, 0:24], bank[:, 0:24], ACT.Exp).then_inc(act_drained, 1)
                    else:
                        act.activation(ex_cg[0:r, 0:12], bank[0:r, 0:12], ACT.Exp)
                        act.activation(ex_cg[:, 12:60], bank[:, 12:60], ACT.Exp).then_inc(act_drained, 1)
                    for label, dst in (("D", E_), ("DT", ET_)):
                        bank = get((label, t))
                        act.activation(dst[0:r, 0:CH * w], bank[0:r, 0:CH * w], ACT.Exp).then_inc(act_drained, 1)

                    def out(label, dst, n=CW, rr=r):
                        bank = get(label)
                        act.activation(dst[0:rr, 0:n], bank[0:rr, 0:n], ACT.Copy).then_inc(act_drained, 1)
                    if t < NP:
                        side(t, 0)
                        side(t, 1)
                    out(("N2", t), N2_, CH * w)
                    if t < NP:
                        side(t, 2)
                        out(("N4", t), N4_)
                        side(t, 3)
                        out(("N8", t), N2_)
                        side(t, 4)
                        if t:
                            root(o_ss)
                        side(t, 5)
                        for m, b in enumerate((32, 64)):
                            out(("T", t, b), T_)
                            out(("Y", t, b), Y_)
                            side(t, 6 + 2 * m)
                            side(t, 7 + 2 * m)
                        for c in range(2):
                            bank = get(("wT", t, c))
                            act.activation(hd(ET_, 3)[:, :, 64 * c:64 * c + 64], hd(bank[:, 0:3 * 64], 3), ACT.Copy).then_inc(act_drained, 1)
                        for point in range(10, 15):
                            side(t, point)
                    else:
                        bank = get(("wT", t, 0))
                        root(o_ss)
                        act.activation(ET_[:, 0:192].rearrange("p (g n) -> p g n", g=3)[:, :, 0:NS],
                                       bank[:, 0:3 * NS].rearrange("p (g n) -> p g n", g=3), ACT.Copy).then_inc(act_drained, 1)
                act.wait_ge(vec_drained, V_AT[("S4", CH - 1)] + 1)
                for g in range(3):
                    act.dma_start(layer_of(outs["delta_sample"], L)[:, 2 * g:2 * g + 2].rearrange("b h k v -> (h k) b v"), state_tile(g)).then_inc(state_stored, 16)
                for G in range(2):
                    for q in range(12):
                        qq = 12 * G + q
                        if q >= 2:
                            act.wait_ge(keys_used, 11 * G + q - 1)
                        bank = get(("kd", G, q // 3, q % 3))
                        act.activation(keysT[qq % 2][:, 0:384], bank[:, 0:384], ACT.Copy).then_inc(act_drained, 1)
                        bank = get(("kr", G, q // 3, q % 3))
                        act.activation(keysT[qq % 2][:, 384:896], bank[:, :], ACT.Copy).then_inc(act_drained, 1)
                        if qq == 1:
                            root(o_ss)
                    act.wait_ge(sprob_asked, G + 1)
                    act.activation(sprob, sprob, ACT.Exp, bias=s_max[:, 4:5], accum_out=s_sum[:, 0:1]).then_inc(sprob_got, 1)
                for t in range(NT):
                    for h in range(2):
                        bank = get(("mixT", t, h))
                        ks = mix_tiles(t, h)
                        act.activation(hT[:, ks[0]:ks[0] + len(ks), 128 * t:128 * t + ROWS[t]],
                                       bank[:, 0:len(ks) * ROWS[t]].rearrange("p (k n) -> p k n", k=len(ks)), ACT.Copy).then_inc(act_drained, 1)
                for t in range(NT):
                    r = ROWS[t]
                    act.wait_ge(vec_drained, V_AT[("out", 1, t)] + 1)
                    if t:
                        act.wait_ge(squares_ready, t)
                    act.activation(junk2[0:r], x[0:r, t, :], ACT.Square, accum_out=ssq[0:r, t:t + 1]).then_inc(squares_ready, 1)
                root(rstd)
                act.wait_ge(route_asked, 1)
                act.activation(top[:, :, 0:NG], top[:, :, 0:NG], ACT.Exp).then_inc(route_got, 1)
                act.wait_ge(route_asked, 2)
                act.activation(p1, p1, ACT.Exp).then_inc(route_got, 1)

                def silu(k, rnd):
                    act.wait_ge(vec_filled, rnd * (2 * EUN) + (V0 + 2 * k + 2))
                    act.activation(gate_act[k % 2], v_bank(V0 + 2 * k + 1)[:, 0:128], ACT.Silu).then_inc(act_gated, 1)

                def hidden_out(k, rnd):
                    act.wait_ge(act_filled, rnd * (2 * EUN) + (A0 + 2 * k + 1))
                    act.activation(hidT[k % 2], a_bank(A0 + 2 * k)[:, 0:128], ACT.Copy).then_inc(act_drained, 1)

                def result_out(k, rnd):
                    act.wait_ge(act_filled, rnd * (2 * EUN) + (A0 + 2 * k + 2))
                    act.wait_ge(rows_stored[k % 3], L * (32 * per_buffer[k % 3]) + rnd * (32 * EUN // 3) + 32 * (k // 3) + 16)
                    act.activation(rows_out[k % 3], a_bank(A0 + 2 * k + 1)[:, :], ACT.Copy).then_inc(act_drained, 1)
                silu(0, 0)
                hidden_out(0, 0)
                with act.Fori(0, ELOOP // EUN) as rnd:
                    for k in range(EUN):
                        silu(k + 1, rnd)
                        result_out(k, rnd)
                        hidden_out(k + 1, rnd)
                for k in range(NE - ELOOP):
                    if k + 1 < NE - ELOOP:
                        silu(k + 1, ELOOP // EUN)
                    result_out(k, ELOOP // EUN)
                    if k + 1 < NE - ELOOP:
                        hidden_out(k + 1, ELOOP // EUN)
                for t in range(NT):
                    if t < NT - 1:
                        act.wait_ge(got_used, t + 1)
                    else:
                        act.wait_ge(moe_done, 1)
                    squares(t, NT + t, squares_ready)
                over = act.value_load(idx_cnt[0:1, 0:1], min_val=0, max_val=NTOK)
                with act.If(over > CAP):
                    with act.Fori(0, NE) as e:
                        for f in range(2):
                            act.wait_ge(fb_up, e * 2 + (f + 1))
                            act.activation(fb_act[:, f, 0:SEQ], psum[2 * f][:, :], ACT.Silu)
                            act.activation(fb_act[:, f, SEQ:NTOK], psum[4 + f][:, 0:NS], ACT.Silu).then_inc(fb_silu, 1)
                    act.wait_ge(fb_added, NE * NT + 1)
                    for t in range(NT):
                        squares(t, 2 * NT + t, squares_ready)
                leave_layer(act, L)
            act.wait_ge(fin_step, 1)
            act.activation(rstd, rstd, ACT.Sqrt).then_inc(fin_step, 1)

        def delta_tile(pe, L, t, job, after, tr, side):
            r, w = ROWS[t], (64 if t < NP else NS)
            chunks = [0, 64] if t < NP else [0]
            prompt = t < NP
            LE, GT = (const("le"), const("gt")) if prompt else (const("le4"), const("gt4"))

            def each(label, lhs, rhs, n=w, of_heads=range(CH)):
                bank, done = job(label)
                for h in of_heads:
                    for c in chunks:
                        mm = pe.matmul(bank[c:c + w, n * h:n * h + n], lhs(h, c), rhs(h, c), start=True, stop=True)
                mm.then_inc(done, 1)

            def of(buf):
                return lambda h, c: buf[c:c + w, w * h:w * h + w]

            pe.wait_ge(delta_in, 3 * t + 3)
            bank, done = job(("cg", t))
            g = decay[0:r, t, :]
            mm = pe.matmul(bank[0:r, 0:CH], LE, g, start=True, stop=True)
            pe.matmul(bank[0:r, CH:2 * CH], GT, g, start=True, stop=True)
            if prompt:
                for c in range(2):
                    mm = pe.matmul(bank[:, 12 + 6 * c:18 + 6 * c], const(f"ch{c}"), g, start=True, stop=True)
            else:
                mm = pe.matmul(bank[:, 12:60], const("ones")[0:r, :], gt4_[0:r, :], start=True, stop=True)
            mm.then_inc(done, 1)
            bank, done = job(("D", t))
            pe.matmul(bank[0:r, 0:CH * w], LE, N2_[0:r, 0:CH * w], start=True, stop=True).then_inc(done, 1)
            bank, done = job(("DT", t))
            pe.matmul(bank[0:r, 0:CH * w], GT, N2T_[0:r, 0:CH * w], start=True, stop=True).then_inc(done, 1)
            for label, src in (("qT", qkv[0:r, t, 0:CW]), ("kT", qkv[0:r, t, CW:2 * CW]), ("bT", kb_[0:r])):
                bank, done = job((label, t))
                for gg in range(3):
                    mm = tr(bank[:, r * gg:r * gg + r], src[:, 128 * gg:128 * gg + 128])
                mm.then_inc(done, 1)
            side(0)
            after(("bT", t))
            kq = KQ_[:, 0:6 * r].rearrange("p (g m n) -> p g m n", g=3, m=2)

            def kTc(h, c):
                return KZ_[:, h, c:c + w]

            def kqc(h, c, m):
                return kq[:, h // 2, m, c:c + w]
            each(("AA", t), lambda h, c: kqc(h, c, 0), kTc)
            for i, hs in enumerate((range(0, 4), range(4, 6))):
                bank, done = job((f"AT{i}", t))
                for h in hs:
                    for c in chunks:
                        mm = pe.matmul(bank[c:c + w, 2 * w * (h - hs[0]):2 * w * (h - hs[0] + 1)].rearrange("p (m n) -> p m n", m=2),
                                       kTc(h, c), kqc(h, c, slice(0, 2)), start=True, stop=True)
                mm.then_inc(done, 1)
            side(1)
            pe.wait_ge(delta_w, 2 * t + 2)
            each(("N2", t), of(NT_), of(N_))
            each(("N2T", t), of(N_), of(NT_))
            side(2)
            after(("N2", t))
            after(("N2T", t))
            if prompt:
                each(("N4", t), of(N2T_), of(N2_))
                each(("N4T", t), of(N2_), of(N2T_))
            each(("M1", t), of(N2_), of(U_))
            side(3)
            after(("M1", t))
            if prompt:
                after(("N4", t))
                each(("N8", t), of(N4T_), of(N4_))
                each(("M2", t), of(N4_), of(U_))
                side(4)
                after(("M2", t))
                after(("N8", t))
                each(("M3", t), of(N2_), of(U_))
                side(5)
                after(("M3", t))
                for s, A in ((32, A32_), (64, A64_)):
                    each(("T", t, s), of(U_), lambda h, c: ident[c:c + w, c:c + w])
                    each(("Y", t, s), of(A), of(U_))
                    side(s // 16 + 4)
                    after(("Y", t, s))
                    each(("X", t, s), of(T_), of(Y_))
                    side(s // 16 + 5)
                    after(("X", t, s))
            pe.wait_ge(delta_w, 2 * t + 2)
            each(("u", t), of(U_), lambda h, c: qkv[c:c + w, t, 2 * CW + 64 * h:2 * CW + 64 * h + 64], n=64)
            for ci, c in enumerate(chunks):
                bank, done = job(("wT", t, ci))
                for h in range(CH):
                    mm = pe.matmul(bank[64 * (h % 2):64 * (h % 2) + 64, w * (h // 2):w * (h // 2) + w],
                                   rw_[c:c + w, 64 * h:64 * h + 64], U_[c:c + w, w * h:w * h + w], start=True, stop=True)
                mm.then_inc(done, 1)
            bank, done = job(("qdT", t))
            for gg in range(3):
                mm = tr(bank[:, r * gg:r * gg + r], qd_[0:r, 128 * gg:128 * gg + 128])
            mm.then_inc(done, 1)
            side(10)
            after(("qdT", t))
            after(("wT", t, len(chunks) - 1))
            if prompt:
                for ci, c in enumerate(chunks):
                    def state_of(h):
                        return state[:, 64 * h:64 * h + 64]
                    bank, done = job(("wS", t, ci))
                    for h in range(CH):
                        mm = pe.matmul(bank[c:c + 64, 64 * h:64 * h + 64],
                                       ET_[:, 128 * (h // 2) + c:128 * (h // 2) + c + 64],
                                       state_of(h), start=True, stop=True)
                    mm.then_inc(done, 1)
                    side(11 + 2 * ci)
                    after(("wS", t, ci))
                    bank, done = job(("o", t, ci))
                    for h in range(CH):
                        dst = bank[c:c + 64, 64 * h:64 * h + 64]
                        pe.matmul(dst, KQ_[:, 128 * (h // 2) + c:128 * (h // 2) + c + 64],
                                  state_of(h), start=True, stop=False)
                        mm = pe.matmul(dst, aT_[c:c + 64, 64 * h:64 * h + 64], N_[c:c + 64, 64 * h:64 * h + 64], start=False, stop=True)
                    mm.then_inc(done, 1)
                    bank, done = job(("S", t, ci))
                    for h in range(CH):
                        mm = pe.matmul(bank[64 * (h % 2):64 * (h % 2) + 64, 64 * h:64 * h + 64],
                                       kd_[c:c + 64, 64 * h:64 * h + 64], N_[c:c + 64, 64 * h:64 * h + 64], start=True, stop=True)
                    mm.then_inc(done, 1)
                    side(12 + 2 * ci)
                    after(("S", t, ci))
                return
            pe.wait_ge(state_loaded, 48)
            for h in range(CH):
                p = 64 * (h % 2)
                bank, done = job(("wS4", h))
                pe.matmul(bank[0:64, :], ET_[p:p + 64, 64 * (h // 2):64 * (h // 2) + 64], S4_[p:p + 64, 512 * (h // 2):512 * (h // 2) + 512],
                          start=True, stop=True).then_inc(done, 1)
            pe.wait_ge(delta_state, 1)
            bank, done = job(("oShift",))
            pe.matmul(bank[0:NS, 0:CW], ident[NS:2 * NS, NS:2 * NS], KQ_[NS:2 * NS, 0:CW], start=True, stop=True).then_inc(done, 1)
            bank, done = job(("o4",))
            for h in range(CH):
                mm = pe.matmul(bank[0:NS, 64 * h:64 * h + 64], aT_[0:NS, NS * h:NS * h + NS], N_[0:NS, 64 * h:64 * h + 64], start=True, stop=True)
            mm.then_inc(done, 1)
            for h in range(CH):
                pe.wait_ge(expand_ready, h + 1)
                bank, done = job(("S4", h))
                pe.matmul(bank[64 * (h % 2):64 * (h % 2) + 64, :], kd_[0:NS, 64 * h:64 * h + 64], BIG_[0:NS, :], start=True, stop=True).then_inc(done, 1)

        @block.tensor
        def _(pe):
            def job(label):
                if label in A_AT:
                    n = A_AT[label]
                    if n >= 4:
                        pe.wait_ge(act_drained, n - 3)
                    return a_bank(n), act_filled
                n = V_AT[label]
                if n >= 4:
                    pe.wait_ge(vec_drained, n - 3)
                return v_bank(n), vec_filled

            def after(label):
                if label in A_AT:
                    pe.wait_ge(act_drained, A_AT[label] + 1)
                else:
                    pe.wait_ge(vec_drained, V_AT[label] + 1)

            def arrived(L, n):
                pe.wait_ge(slot_full[n % 3], L * SLOT_TOTAL[n % 3] + full_at[n])
                pe.sem_inc(aside, 1)

            def tr(out, in_, start=True):
                r = in_.shape[0]
                return pe.transpose(out, in_, ident[0:r, 0:r])

            def ringv(n, at, cols, k=KT):
                base = (n % 3) * SLOT + at
                return ring[:, base:base + k * cols].rearrange("p (k n) -> p k n", k=k)

            pe.wait_ge(consts_loaded, 16)
            with pe.Fori(0, DEPTH) as L:
                pe.wait_ge(taps_loaded, 32)
                bank, done = job(("tapsT",))
                for c in range(NCT):
                    mm = tr(bank[:, 28 * c:28 * c + 28], state_rows[:, 128 * c:128 * c + 128])
                mm.then_inc(done, 1)
                for t in range(NT):
                    pe.wait_ge(rows_ready, t + 1)
                    r = ROWS[t]
                    for h in range(2):
                        bank, done = job(("norm1", t, h))
                        for k in range(4):
                            mm = tr(bank[:, k * r:k * r + r], hst[t % 2][0:r, 4 * h + k::KT])
                        mm.then_inc(done, 1)
                after(("norm1", NT - 1, 1))
                def sample_rows(bank, w):
                    n4 = w.shape[2] // 4
                    for k in range(KT):
                        for q in range(4):
                            mm = pe.matmul(bank[NS * q:NS * q + NS, 0:n4], hT[:, k, SEQ:NTOK], w[:, k, n4 * q:n4 * q + n4],
                                           start=k == 0, stop=k == KT - 1)
                    return mm

                for i in range(NCT + 2):
                    if i < NCT:
                        n = i // 3
                        if i % 3 == 0:
                            arrived(L, n)
                            bank, done = job(("convR", n))
                            sample_rows(bank, ringv(n, 0, 384)).then_inc(done, 1)
                        w = ringv(n, 0, 384)[:, :, 128 * (i % 3):128 * (i % 3) + 128]
                        bank, done = job(("convP", i))
                        for k in range(KT):
                            mm = pe.matmul(bank[:, 0:SEQ], w[:, k, :], hT[:, k, 0:SEQ], start=k == 0, stop=k == KT - 1)
                        mm.then_inc(done, 1)
                        if i % 3 == 0:
                            after(("convR", n))
                        bank, done = job(("convS", i))
                        tr(bank[:, 0:NS], conv_rows[:, 128 * i:128 * i + 128]).then_inc(done, 1)
                    if i >= 2:
                        j = i - 2
                        pe.wait_ge(silu_done, j + 1)
                        bank, done = job(("qkvP", j))
                        for t in range(NP):
                            mm = tr(bank[:, 128 * t:128 * t + 128], sil[j % 2][:, 128 * t:128 * t + 128])
                        mm.then_inc(done, 1)
                        bank, done = job(("qkvS", j))
                        tr(bank[0:NS, 0:128], sil[j % 2][:, SEQ:NTOK]).then_inc(done, 1)
                pe.wait_ge(tail_copied, NCT)
                for i in range(3):
                    bank, done = job(("tail", i))
                    for c in range(3):
                        mm = tr(bank[0:27, 128 * c:128 * c + 128], tail[:, 3 * i + c, :])
                    mm.then_inc(done, 1)
                def spatial_gating():
                    pe.wait_ge(mlp_params, 48)
                    bank, done = job(("wsT",))
                    for h in range(AH):
                        mm = tr(bank[:, 128 * h:128 * h + 128], ws_raw[:, h, :])
                    mm.then_inc(done, 1)
                    after(("wsT",))
                    bank, done = job(("rep",))
                    for h in range(AH):
                        mm = pe.matmul(bank[0:DS, NS * h:NS * h + NS], wsT[0:DS, h, 0:DS], const("rep4"), start=True, stop=True)
                    mm.then_inc(done, 1)
                    after(("rep",))
                    bank, done = job(("ws4",))
                    for h in range(AH):
                        pe.matmul(bank[0:NS, NS * h:NS * h + NS], rep_w[:, NS * h:NS * h + NS], const("rep4"), start=True, stop=True)
                    pe.matmul(bank[0:NS, 128:128 + AH], const("rep4"), bias_p[0:DS, :], start=True, stop=True).then_inc(done, 1)
                    after(("ws4",))
                    pe.wait_ge(vn_ready, 1)
                    for t in range(NT):
                        bank, done = job(("gate", t))
                        for h in range(AH):
                            w = wsT[:, h, :] if t < NP else ws4[:, h, :]
                            mm = pe.matmul(bank[0:ROWS[t], 64 * h:64 * h + 64], w, proj[0:ROWS[t], t, AV + 64 * h:AV + 64 * h + 64],
                                           start=True, stop=True)
                        mm.then_inc(done, 1)
                pe.wait_ge(params_loaded, 16 * 6)
                for p, piece in enumerate("ABC"):
                    n = 3 + p
                    if piece == "C":
                        spatial_gating()
                    arrived(L, n)
                    parts = {"A": (ringv(n, 0, 512), w_ba), "B": (ringv(n, 0, 768)[:, :, 0:384], ringv(n, 0, 768)[:, :, 384:768]),
                             "C": (ringv(n, 0, 384), ringv(n, KT * 384, 384))}[piece]
                    for t in range(NT):
                        for j, w in enumerate(parts):
                            bank, done = job((piece, t, j))
                            if t == NP and w.shape[2] > 12:
                                sample_rows(bank, w).then_inc(done, 1)
                                continue
                            for k in range(KT):
                                mm = pe.matmul(bank[0:ROWS[t], 0:w.shape[2]], hT[:, k, 128 * t:128 * t + ROWS[t]], w[:, k, :],
                                               start=k == 0, stop=k == KT - 1)
                            mm.then_inc(done, 1)
                pe.wait_ge(rope_done, 1)

                def side(t, point):
                    for n in beside(t, point):
                        if n < 6:
                            name, g, c = ("bq", "bk")[n % 2], n // 2, (BQ, BK)[n % 2]
                            bank, done = job((name, g))
                            for u in range(NP):
                                mm = tr(bank[:, 128 * u:128 * u + 128], proj[:, u, c + 128 * g:c + 128 * g + 128])
                            mm.then_inc(done, 1)
                            bank, done = job((name + "s", g))
                            tr(bank[:, 0:NS], proj[0:NS, NP, c + 128 * g:c + 128 * g + 128]).then_inc(done, 1)
                            continue
                        j = n - 8
                        if 0 <= j < STEPS:
                            pe.wait_ge(probs_ready, j + 1)
                            bank, done = job(("P", j))
                            for b in range(j % NP + 1):
                                mm = tr(bank[:, 128 * b:128 * b + 128], prob[j % 2][:, 128 * b:128 * b + 128])
                            mm.then_inc(done, 1)
                        j = n - 9
                        if 0 <= j < STEPS:
                            h, u = divmod(j, NP)
                            after(("P", j))
                            bank, done = job(("O", j))
                            for b in range(u + 1):
                                mm = pe.matmul(bank[:, 0:64], probT[j % 2][:, 128 * b:128 * b + 128],
                                               proj[:, b, BV + 64 * h:BV + 64 * h + 64], start=b == 0, stop=b == u)
                            mm.then_inc(done, 1)
                        j = n - 6
                        if j < STEPS:
                            h, u = divmod(j, NP)
                            p0_, g = 64 * (h % 2), h // 2
                            if j == 0:
                                after(("bks", 2))
                            bank, done = job(("S", j))
                            pe.matmul(bank[:, 0:128 * (u + 1)], qTb[g][p0_:p0_ + 64, 128 * u:128 * u + 128],
                                      kTb[g][p0_:p0_ + 64, 0:128 * (u + 1)], start=True, stop=True).then_inc(done, 1)
                for t in range(NT):
                    delta_tile(pe, L, t, job, after, tr, lambda point, t=t: side(t, point) if t < NP else None)
                for G in range(2):
                    score = {}
                    for q in range(13):
                        if q < 12:
                            b, g = divmod(q, 3)
                            n = 6 + 4 * G + b // 2
                            if q % 6 == 0:
                                arrived(L, n)
                            kk = ring[:, (n % 3) * SLOT + 3072 * (b % 2):(n % 3) * SLOT + 3072 * (b % 2) + 3072].rearrange("p (j n) -> p j n", j=8)
                            bank, done = job(("kd", G, b, g))
                            for j in range(4):
                                mm = tr(bank[:, NDIL * j:NDIL * j + NDIL], kk[0:NDIL, j, 128 * g:128 * g + 128])
                            mm.then_inc(done, 1)
                            bank, done = job(("kr", G, b, g))
                            for j in range(4):
                                mm = tr(bank[:, 128 * j:128 * j + 128], kk[:, 4 + j, 128 * g:128 * g + 128])
                            mm.then_inc(done, 1)
                        if q >= 1:
                            b, g = divmod(q - 1, 3)
                            after(("kr", G, b, g))
                            if q == 1:
                                pe.wait_ge(qblk_ready, 1)
                                for name in ("sd", "sr", "sn"):
                                    score[name] = job((name, G))
                            kt = keysT[(12 * G + q - 1) % 2]
                            qb = qblk[:, 4 * G + b, g, :]
                            for name, rhs in (("sd", kt[:, 0:384]), ("sr", kt[:, 384:896]), ("sn", kTb[g][:, SEQ:NTOK])):
                                bank = score[name][0]
                                mm = pe.matmul(bank[32 * b:32 * b + 32, 0:rhs.shape[1]], qb, rhs, start=g == 0, stop=g == 2)
                                if q == 12:
                                    mm.then_inc(vec_filled, 1)
                                elif name == "sn":
                                    mm.then_inc(keys_used, 1)
                    pe.wait_ge(sprob_ready, G + 1)
                    bank, done = job(("pd", G))
                    for j in range(4):
                        mm = tr(bank[0:NDIL, 128 * j:128 * j + 128], sprob[:, NDIL * j:NDIL * j + NDIL])
                    mm.then_inc(done, 1)
                    bank, done = job(("pr", G))
                    for j in range(4):
                        mm = tr(bank[:, 128 * j:128 * j + 128], sprob[:, 384 + 128 * j:384 + 128 * j + 128])
                    mm.then_inc(done, 1)
                    bank, done = job(("pn", G))
                    tr(bank[0:NS, 0:128], sprob[:, 896:928]).then_inc(done, 1)
                    after(("pn", G))
                    arrived(L, 8 + 4 * G)
                    arrived(L, 9 + 4 * G)
                    vv = []
                    for b in range(4):
                        n = 8 + 4 * G + b // 2
                        base = (n % 3) * SLOT + 3072 * (b % 2)
                        vv.append(ring[:, base:base + 3072].rearrange("p (j n) -> p j n", j=8))
                    bank, done = job(("ov", G))
                    for j in range(9):
                        for b in range(4):
                            dst = bank[32 * b:32 * b + 32, 0:BW]
                            col = 128 * (j % 4) + 32 * b
                            if j < 4:
                                pe.matmul(dst, spd[0:NDIL, col:col + 32], vv[b][0:NDIL, j, :], start=j == 0, stop=False)
                            elif j < 8:
                                pe.matmul(dst, spr[:, col:col + 32], vv[b][:, j, :], start=False, stop=False)
                            else:
                                mm = pe.matmul(dst, spn[0:NS, 32 * b:32 * b + 32], proj[0:NS, NP, BV:BV + BW], start=False, stop=True)
                    mm.then_inc(done, 1)
                    after(("ov", G))
                    bank, done = job(("oT", G))
                    for g in range(3):
                        mm = pe.matmul(bank[:, 16 * g:16 * g + 16], own[:, 128 * g:128 * g + 128], const("token16"), start=True, stop=True)
                    mm.then_inc(done, 1)
                pe.wait_ge(mix_ready, 1)
                for t in range(NT):
                    r = ROWS[t]
                    for h in range(2):
                        bank, done = job(("mixT", t, h))
                        for j, k in enumerate(mix_tiles(t, h)):
                            mm = tr(bank[:, j * r:j * r + r], proj[0:r, t, MIXCOL[k]:MIXCOL[k] + 128])
                        mm.then_inc(done, 1)
                after(("mixT", NT - 1, 1))
                for c in range(2):
                    arrived(L, 14 + c)
                    w = ringv(14 + c, 0, 512)
                    for t in range(NT):
                        bank, done = job(("out", c, t))
                        if t == NP:
                            sample_rows(bank, w).then_inc(done, 1)
                            continue
                        for k in range(KT):
                            mm = pe.matmul(bank[0:ROWS[t], :], hT[:, k, 128 * t:128 * t + ROWS[t]], w[:, k, :], start=k == 0, stop=k == KT - 1)
                        mm.then_inc(done, 1)
                for t in range(NT):
                    r = ROWS[t]
                    pe.wait_ge(rows_ready, NT + t + 1)
                    for h in range(2):
                        bank, done = job(("norm2", t, h))
                        for k in range(4):
                            mm = tr(bank[:, k * r:k * r + r], h2[0:r, t, 4 * h + k::KT])
                        mm.then_inc(done, 1)
                after(("norm2", NT - 1, 1))
                pe.wait_ge(route_loaded, 32)
                bank, done = job(("logit", 0))
                for t in range(NT):
                    for k in range(KT):
                        mm = pe.matmul(bank[0:ROWS[t], 36 * t:36 * t + 36], hT[:, k, 128 * t:128 * t + ROWS[t]], w_route[:, k, :],
                                       start=k == 0, stop=k == KT - 1)
                mm.then_inc(done, 1)
                pe.wait_ge(masks_ready, 1)
                bank, done = job(("rank", 0))
                for t in range(NT + 1):
                    dst = bank[0:ROWS[t], 32 * t:32 * t + 32] if t < NT else bank[:, 160:192]
                    for u in range(min(t + 1, NT)):
                        m = const("before") if u == t else const("ones")
                        mm = pe.matmul(dst, m[0:ROWS[u], 0:dst.shape[0]], msum[0:ROWS[u], u, :], start=u == 0, stop=u == min(t, NT - 1))
                mm.then_inc(done, 1)

                def rows_across(k, rnd):
                    pe.wait_ge(rows_loaded[k % 3], L * (16 * per_buffer[k % 3]) + rnd * (16 * EUN // 3) + 16 * (k // 3 + 1))
                    pe.wait_ge(vec_drained, rnd * (2 * EUN) + (V0 + 2 * k - 3))
                    pe.sem_inc(aside, 1)
                    bank = v_bank(V0 + 2 * k)
                    for c in range(KT):
                        mm = pe.transpose(bank[:, CAP * c:CAP * c + CAP], rows_in[k % 3][:, c::KT], ident[0:CAP, 0:CAP])
                    mm.then_inc(vec_filled, 1)

                def up(k, rnd):
                    slot = (E_AT + k) % 3
                    w13 = ring[:, slot * SLOT:slot * SLOT + 4096].rearrange("p (w k f j) -> p w k f j", w=2, k=KT, j=2)
                    pe.wait_ge(slot_full[slot], L * SLOT_TOTAL[slot] + rnd * (48 * EUN // 3) + full_at[E_AT + k])
                    pe.wait_ge(vec_drained, rnd * (2 * EUN) + (V0 + 2 * k + 1))
                    pe.sem_inc(aside, 1)
                    bank = v_bank(V0 + 2 * k + 1)
                    for c in range(KT):
                        for j in range(2):
                            mm = pe.matmul(bank[CAP * j:CAP * j + CAP, 0:256].rearrange("p (w f) -> p w f", w=2),
                                           rowsT[k % 2][:, CAP * c:CAP * c + CAP], w13[:, :, c, :, j], start=c == 0, stop=c == KT - 1)
                    mm.then_inc(vec_filled, 1)

                def hidden_across(k, rnd):
                    pe.wait_ge(vec_drained, rnd * (2 * EUN) + (V0 + 2 * k + 2))
                    pe.wait_ge(act_drained, rnd * (2 * EUN) + (A0 + 2 * k - 3))
                    pe.sem_inc(aside, 1)
                    pe.transpose(a_bank(A0 + 2 * k)[:, 0:128], hid[k % 2], ident).then_inc(act_filled, 1)

                def down(k, rnd):
                    slot = (E_AT + k) % 3
                    w2 = ring[:, slot * SLOT + 4096:slot * SLOT + 6144].rearrange("p (j d) -> p j d", j=2)
                    pe.wait_ge(act_drained, rnd * (2 * EUN) + (A0 + 2 * k + 1))
                    pe.sem_inc(aside, 1)
                    bank = a_bank(A0 + 2 * k + 1)
                    for j in range(2):
                        for c in range(2):
                            mm = pe.matmul(bank[CAP * c:CAP * c + CAP, :], hidT[k % 2][:, CAP * j:CAP * j + CAP], w2[:, j, 512 * c:512 * c + 512],
                                           start=j == 0, stop=j == 1)
                    mm.then_inc(act_filled, 1)
                rows_across(0, 0)
                up(0, 0)
                rows_across(1, 0)
                hidden_across(0, 0)
                with pe.Fori(0, ELOOP // EUN) as rnd:
                    for k in range(EUN):
                        up(k + 1, rnd)
                        rows_across(k + 2, rnd)
                        down(k, rnd)
                        hidden_across(k + 1, rnd)
                for k in range(NE - ELOOP):
                    if k + 1 < NE - ELOOP:
                        up(k + 1, ELOOP // EUN)
                    down(k, ELOOP // EUN)
                    if k + 1 < NE - ELOOP:
                        hidden_across(k + 1, ELOOP // EUN)
                pe.wait_ge(moe_done, 1)
                over = pe.value_load(idx_cnt[0:1, 0:1], min_val=0, max_val=NTOK)
                with pe.If(over > CAP):
                    fw = [fb_w[:, 2048 * i:2048 * i + 2048].rearrange("p (k f) -> p k f", k=KT) for i in range(2)]
                    fw2 = fb_w[:, 4096:6144].rearrange("p (j d) -> p j d", j=2)
                    with pe.Fori(0, NE) as e:
                        pe.wait_ge(fb_loaded, e * 48 + 48)
                        pe.sem_inc(aside, 1)
                        for f in range(2):
                            for i in range(2):
                                for dst, c0, c1_ in ((psum[2 * f + i][:, :], 0, SEQ), (psum[4 + f][:, 64 * i:64 * i + NS], SEQ, NTOK)):
                                    for c in range(KT):
                                        mm = pe.matmul(dst, fw[i][:, c, f::2], hT[:, c, c0:c1_], start=c == 0, stop=c == KT - 1)
                            mm.then_inc(fb_up, 1)
                        pe.wait_ge(fb_prod, e * 2 + 2)
                        pe.sem_inc(aside, 1)
                        for t in range(NT):
                            r = ROWS[t]
                            pe.wait_ge(fb_added, e * NT + (t + 1))
                            pe.sem_inc(aside, 1)
                            for c in range(2):
                                for j in range(2):
                                    mm = pe.matmul(psum[6 + c][0:r, :], fb_hid[:, j, 128 * t:128 * t + r], fw2[:, j, 512 * c:512 * c + 512],
                                                   start=j == 0, stop=j == 1)
                            mm.then_inc(fb_down, 1)
                leave_layer(pe, L)

        def delta_names(t):
            r, w = ROWS[t], (64 if t < NP else NS)
            prompt = t < NP
            m = ("gtc", "lec", "idc", "nlow16", "nup16") if prompt else ("gt4", "le4", "ident", "nlow4", "nup4")
            q, k, v = (qkv[0:r, t, CW * i:CW * i + CW] for i in range(3))
            return r, w, prompt, [const(n)[0:r, 0:w] for n in m], q, k, v, CH * w

        def delta_prepare(dve, t, then):
            r, w, prompt, (gtc, lec, idc, nlow, nup), q, k, v, ew = delta_names(t)
            then(dve.tensor_tensor(hd(qkv[0:r, t, 0:2 * CW], 12), hd(qkv[0:r, t, 0:2 * CW], 12), inner(l2[0:r, t, :], 64), ALU.mult))
            bt = inner(beta[0:r, t, :], 64)
            if not prompt:
                then(dve.tensor_tensor(gt4_[0:r, :].rearrange("p (h b) -> p h b", h=CH), mid(const("rowseq")[0:r, :], CH),
                                       inner(decay[0:r, t, :], DB), ALU.mult))
            dve.tensor_tensor(hd(kb_[0:r]), hd(k), bt, ALU.mult).then_inc(delta_in, 1)
            gb = inner(decay[0:r, t, :], w)
            dve.tensor_tensor(hd(N2_[0:r, 0:ew]), mid(gtc, CH), gb, ALU.mult).then_inc(delta_in, 1)
            dve.tensor_tensor(hd(N2T_[0:r, 0:ew]), mid(lec, CH), gb, ALU.mult).then_inc(delta_in, 1)
            dve.tensor_tensor(hd(v), hd(v), bt, ALU.mult)

        def delta_norm(dve, t, then, inv_root):
            r = ROWS[t]
            dve.wait_ge(z_ready, 2)
            o = O_[0:r, :]
            then(dve.tensor_tensor(Sg_[0:r, :], o, o, ALU.mult))
            then(dve.tensor_reduce(o_ss[0:r, :], hd(Sg_[0:r, :]), AX, ALU.add))
            then(dve.tensor_scalar(o_ss, o_ss, 1.0 / HD, EPS, ALU.mult, ALU.add))
            inv_root(o_ss)
            then(dve.tensor_tensor(hd(o), hd(o), inner(o_ss[0:r, :], HD), ALU.mult))
            then(dve.tensor_tensor(hd(o), hd(o), mid(c_gain[0:r, :], CH), ALU.mult))
            z = proj[0:r, t, CZ:CZ + CW]
            ins = dve.tensor_tensor(z, z, o, ALU.mult)
            if t < NP:
                then(ins)
            else:
                ins.then_inc(norms_done, 1)

        def delta_vec(dve, t, then, get, kept, inv_root, side):
            r, w, prompt, (gtc, lec, idc, nlow, nup), q, k, v, ew = delta_names(t)
            dve.wait_ge(delta_in, 3 * t + 3)
            dve.wait_ge(act_drained, A_AT[("cg", t)] + 1)
            dve.tensor_tensor(hd(rw_[0:r]), hd(kb_[0:r]), inner(ex_cg[0:r, 0:CH], 64), ALU.mult)
            dve.tensor_tensor(hd(qd_[0:r]), hd(q), inner(ex_cg[0:r, 0:CH], 64), ALU.mult)
            dve.tensor_tensor(hd(kd_[0:r]), hd(k), inner(ex_cg[0:r, CH:2 * CH], 64), ALU.mult).then_inc(delta_w, 1)
            kq = KQ_[:, 0:6 * r].rearrange("p (g m n) -> p g m n", g=3, m=2)
            bank = get(("qT", t))
            kept(dve.tensor_copy(kq[:, :, 1, :], hd(bank[:, 0:3 * r], 3)))
            bank = get(("kT", t))
            for hh in range(2):
                p = slice(64 * hh, 64 * hh + 64)
                ins = dve.tensor_copy(KZ_[p, hh::2, 0:r], hd(bank[p, 0:3 * r], 3))
            kept(ins)
            bank = get(("bT", t))
            kept(dve.tensor_copy(kq[:, :, 0, :], hd(bank[:, 0:3 * r], 3)))
            side(0)
            dve.wait_ge(act_drained, A_AT[("DT", t)] + 1)
            bank = get(("AA", t))
            kept(dve.tensor_tensor(T_[0:r, 0:ew], bank[0:r, 0:ew], E_[0:r, 0:ew], ALU.mult), ("AA", t))
            A = hd(T_[0:r, 0:ew])
            dve.tensor_tensor(hd(N_[0:r, 0:ew]), A, mid(nlow, CH), ALU.mult)
            if prompt:
                dve.tensor_tensor(hd(A32_), A, mid(const("low32"), CH), ALU.mult)
                dve.tensor_tensor(hd(A64_), A, mid(const("low64"), CH), ALU.mult)
            for i, (h0, h1) in enumerate(((0, 4), (4, 6))):
                bank = get((f"AT{i}", t))
                pair = bank[0:r, 0:2 * w * (h1 - h0)].rearrange("p (h m n) -> p h m n", h=h1 - h0, m=2)
                e = hd(ET_[0:r, 0:ew])[:, h0:h1, :]
                dve.tensor_tensor(hd(NT_[0:r, 0:ew])[:, h0:h1, :], pair[:, :, 0, :], e, ALU.mult)
                kept(dve.tensor_tensor(hd(aT_[0:r, 0:ew])[:, h0:h1, :], pair[:, :, 1, :], e, ALU.mult), (f"AT{i}", t))
            then(dve.tensor_tensor(hd(NT_[0:r, 0:ew]), hd(NT_[0:r, 0:ew]), mid(nup, CH), ALU.mult))
            dve.tensor_tensor(hd(aT_[0:r, 0:ew]), hd(aT_[0:r, 0:ew]), mid(lec, CH), ALU.mult)
            dve.tensor_tensor(hd(U_[0:r, 0:ew]), hd(NT_[0:r, 0:ew]), mid(idc, CH), ALU.add).then_inc(delta_w, 1)
            dve.wait_ge(delta_w, 2 * t + 2)
            side(1)

            def copy(label, dst):
                bank = get(label)
                kept(dve.tensor_copy(dst, bank[0:dst.shape[0], 0:dst.shape[1]]), label)

            def more(label, op=ALU.add):
                bank = get(label)
                kept(dve.tensor_tensor(U_[0:r, 0:ew], U_[0:r, 0:ew], bank[0:r, 0:ew], op), label)
            copy(("N2T", t), N2T_[0:r, 0:ew])
            side(2)
            if prompt:
                copy(("N4T", t), N4T_)
            more(("M1", t))
            side(3)
            if prompt:
                more(("M2", t))
                side(4)
                if t:
                    delta_norm(dve, t - 1, then, inv_root)
                more(("M3", t))
                side(5)
                for m, b in enumerate((32, 64)):
                    side(6 + 2 * m)
                    more(("X", t, b), ALU.subtract)
                    side(7 + 2 * m)
                delta_prepare(dve, t + 1, then)
            else:
                delta_norm(dve, t - 1, then, inv_root)
            copy(("u", t), E_[0:r])
            if prompt:
                copy(("qdT", t), KQ_[:, 0:CW])
                side(10)
                for ci in range(2):
                    c = slice(64 * ci, 64 * ci + 64)
                    bank = get(("wS", t, ci))
                    kept(dve.tensor_tensor(N_[c, :], E_[c, :], bank[c, 0:CW], ALU.subtract))
                    then(dve.tensor_tensor(hd(Sg_), hd(state), inner(ex_cg[:, 12 + 6 * ci:18 + 6 * ci], 64), ALU.mult))
                    side(11 + 2 * ci)
                    bank = get(("o", t, ci))
                    kept(dve.tensor_copy(O_[c, :], bank[c, 0:CW]))
                    bank = get(("S", t, ci))
                    for hh in range(2):
                        p = slice(64 * hh, 64 * hh + 64)
                        ins = dve.tensor_tensor(hd(state[p, :])[:, hh::2, :], hd(Sg_[p, :])[:, hh::2, :], hd(bank[p, 0:CW])[:, hh::2, :], ALU.add)
                    kept(ins, ("S", t, ci))
                    side(12 + 2 * ci)
            else:
                bank = get(("qdT", t))
                kept(dve.tensor_copy(ET_[:, 0:192].rearrange("p (g n) -> p g n", g=3)[:, :, NS:2 * NS],
                                     bank[:, 0:3 * NS].rearrange("p (g n) -> p g n", g=3)))
                for h in range(CH):
                    bank = get(("wS4", h))
                    big = BIG_[0:64, :].rearrange("p (b v) -> p b v", b=DB)
                    kept(dve.tensor_tensor(big, bank[0:64, :].rearrange("p (b v) -> p b v", b=DB), inner(const("rowseq"), HD), ALU.mult), ("wS4", h))
                    then(dve.tensor_reduce(KQ_[0:64, 64 * h:64 * h + 64], BIG_[0:64, :].rearrange("p (b v) -> p v b", b=DB), AX, ALU.add))
                dve.tensor_tensor(N_[0:r, :], E_[0:r, :], KQ_[0:r, 0:CW], ALU.subtract).then_inc(delta_state, 1)
                dve.wait_ge(delta_state, 1)
                copy(("oShift",), O_[0:r, :])
                bank = get(("o4",))
                kept(dve.tensor_tensor(O_[0:r, :], O_[0:r, :], bank[0:r, 0:CW], ALU.add))
                for h in range(CH):
                    p = slice(64 * (h % 2), 64 * (h % 2) + 64)
                    dve.tensor_tensor(BIG_[0:r, :].rearrange("p (b v) -> p b v", b=DB), mid(N_[0:r, 64 * h:64 * h + 64], DB),
                                      inner(const("rowseq")[0:r, :], HD), ALU.mult).then_inc(expand_ready, 1)
                    s4 = S4_[p, 512 * (h // 2):512 * (h // 2) + 512]
                    s4v = s4.rearrange("p (b v) -> p b v", b=DB)
                    then(dve.tensor_tensor(s4v, s4v, inner(ex_cg[p, 12 + DB * h:12 + DB * h + DB], HD), ALU.mult))
                    bank = get(("S4", h))
                    kept(dve.tensor_tensor(s4, s4, bank[p, :], ALU.add))
                dve.wait_ge(vec_drained, V_AT[("S4", CH - 1)] + 1)

        def route(dve, then, get, kept):
            bank = get(("logit", 0))
            then(dve.memset(logit, 0.0))
            then(dve.memset(glog, -3e38))
            dve.tensor_copy(logit[:, 0:NP, :], bank[:, 0:36 * NP].rearrange("p (t n) -> p t n", t=NP))
            kept(dve.tensor_copy(logit[0:NS, NP, :], bank[0:NS, 36 * NP:36 * NT]), ("logit", 0))
            then(dve.tensor_copy(glog[:, :, 0:NG], logit[:, :, 0:NG]))

            def eight(src):
                for t in range(NT):
                    ins = dve.max(top[:, t, :], src[:, t, :])
                then(ins)
                for t in range(NT):
                    ins = dve.max_index(idx_top[:, 8 * t:8 * t + 8], top[:, t, :], src[:, t, :])
                then(ins)
            it = idx_top.rearrange("p (t n) -> p t n", t=NT)
            eight(glog)
            dve.tensor_copy(gi, it[:, :, 0])
            then(dve.tensor_copy(ga, top[:, :, 0]))
            dve.tensor_tensor(top[:, :, 0:NG], logit[:, :, 0:NG], inner(ga, NG), ALU.subtract).then_inc(route_asked, 1)
            then(dve.tensor_tensor(em, mid(const("group"), NT), inner(gi, NE), ALU.is_equal))
            then(dve.tensor_tensor(el, logit[:, :, NG:36], em, ALU.mult))
            then(dve.tensor_scalar(em, em, -NEG, NEG, ALU.mult, ALU.add))
            then(dve.tensor_tensor(el, el, em, ALU.add))
            dve.wait_ge(route_got, 1)
            then(dve.tensor_reduce(ga, top[:, :, 0:NG], AX, ALU.add))
            then(dve.reciprocal(ga, ga))
            eight(el)
            dve.tensor_copy(e0, it[:, :, 0])
            then(dve.tensor_copy(e1, it[:, :, 1]))
            dve.tensor_tensor(p1, top[:, :, 1], top[:, :, 0], ALU.subtract).then_inc(route_asked, 1)
            for e, m in ((e0, m0), (e1, m1)):
                then(dve.tensor_tensor(m, mid(const("expert"), NT), inner(e, NE), ALU.is_equal))
            dve.tensor_tensor(msum, m0, m1, ALU.add).then_inc(masks_ready, 1)
            dve.wait_ge(route_got, 2)
            then(dve.tensor_scalar(p0, p1, 1.0, None, ALU.add))
            then(dve.reciprocal(p0, p0))
            then(dve.tensor_tensor(p0, p0, ga, ALU.mult))
            then(dve.tensor_tensor(p1, p1, p0, ALU.mult))
            bank = get(("rank", 0))
            then(dve.memset(rk, 0.0))
            dve.tensor_copy(rk[:, 0:NP, :], bank[:, 0:32 * NP].rearrange("p (t n) -> p t n", t=NP))
            dve.tensor_copy(rk[0:NS, NP, :], bank[0:NS, 32 * NP:32 * NT])
            kept(dve.tensor_reduce(counts[:, 0:1], bank[:, 160:192], AX, ALU.max), ("rank", 0))
            then(dve.tensor_copy(idx_cnt, counts[:, 0:1]))
            then(dve.memset(over_gate, 0.0))
            for k, (e, m, rr, oo, p, w) in enumerate(((e0, m0, r0, o0, p0, w0), (e1, m1, r1, o1, p1, w1_))):
                then(dve.tensor_tensor(em, m, rk, ALU.mult))
                then(dve.tensor_reduce(rr, em, AX, ALU.add))
                then(dve.tensor_scalar(oo, rr, float(CAP), None, ALU.is_ge))
                then(dve.tensor_tensor(gb, p, oo, ALU.mult))
                then(dve.tensor_tensor(em, m, inner(gb, NE), ALU.mult))
                then(dve.tensor_tensor(over_gate, over_gate, em, ALU.add))
                then(dve.tensor_tensor(w, p, gb, ALU.subtract))
                then(dve.tensor_scalar(tq, rr, float(CAP - 1), None, ALU.min))
                then(dve.scalar_tensor_tensor(tq, e, float(CAP), tq, ALU.mult, ALU.add))
                then(dve.tensor_copy(idx_ga[:, NT * k:NT * k + NT], tq))
                then(dve.tensor_tensor(gi, const("spare")[:, NT * k:NT * k + NT], tq, ALU.subtract))
                then(dve.tensor_tensor(gi, gi, oo, ALU.mult))
                then(dve.tensor_tensor(tq, tq, gi, ALU.add))
                ins = dve.tensor_copy(idx_sc[:, NT * k:NT * k + NT], tq)
                ins.then_inc(index_ready, 1)
                if k == 0:
                    dve.wait_ge(index_ready, 1)

        @block.vector
        def _(dve):
            steps, roots, asks = [0], [0], [0]

            def then(ins):
                steps[0] += 1
                ins.then_inc(vec_step, 1)
                dve.wait_ge(vec_step, steps[0])

            def get(label):
                dve.wait_ge(vec_filled, V_AT[label] + 1)
                return v_bank(V_AT[label])

            def kept(ins, label=None):
                ins.then_inc(vec_drained, 1)
                if label is not None:
                    dve.wait_ge(vec_drained, V_AT[label] + 1)

            def inv_root(ap):
                roots[0] += 1
                dve.reciprocal(ap, ap).then_inc(root_asked, 1)
                dve.wait_ge(root_ready, roots[0])

            def norm_scale():
                then(dve.tensor_scalar(rstd, ssq, 1.0 / D, EPS, ALU.mult, ALU.add))
                inv_root(rstd)

            dve.memset(small[:, :], 1.0).then_inc(small_set, 1)
            dve.memset(zeros, 0.0).then_inc(zeros_ready, 1)
            dve.wait_ge(small_set, 1)
            dve.wait_ge(consts_loaded, 16)
            dve.wait_ge(x_loaded, 32)
            groups = ((128, slice(0, NP), NP), (NS, slice(NP, NT), 1))
            with dve.Fori(0, DEPTH) as L:
                dve.wait_ge(first_squares, NT)
                norm_scale()
                dve.wait_ge(params_loaded, 16 * 6)

                def normal(t):
                    r = ROWS[t]
                    dve.tensor_scalar(hst[t % 2][0:r], x[0:r, t, :], rstd[0:r, t:t + 1], None, ALU.mult).then_inc(rows_ready, 1)

                def gained(label, t, h, gain):
                    bank = get(label)
                    kept(dve.tensor_tensor(hT[:, 4 * h:4 * h + 4, 128 * t:128 * t + ROWS[t]],
                                           bank[:, 0:4 * ROWS[t]].rearrange("p (k n) -> p k n", k=4),
                                           inner(gain[:, 4 * h:4 * h + 4], ROWS[t]), ALU.mult))
                normal(0)
                for t in range(NT):
                    if t + 1 < NT:
                        normal(t + 1)
                    for h in range(2):
                        gained(("norm1", t, h), t, h, g1)
                for c in cin:
                    dve.memset(c[:, 0:3], 0.0).then_inc(vec_step, 1)
                steps[0] += 2
                dve.wait_ge(vec_step, steps[0])
                n = XW - 3
                for i in range(NCT + 2):
                    if i < NCT:
                        c, a = cin[i % 2], acc[i % 2]
                        if i >= 2:
                            dve.wait_ge(silu_done, i - 1)
                        dve.wait_ge(conv_in, i + 1)
                        then(dve.tensor_scalar(a[:, 0:n], c[:, 0:n], taps[:, i, 24:25], None, ALU.mult))
                        for j in range(1, 4):
                            ins = dve.scalar_tensor_tensor(a[:, 0:n], c[:, j:j + n], taps[:, i, 24 + j:25 + j], a[:, 0:n], ALU.mult, ALU.add)
                            if j < 3:
                                then(ins)
                            else:
                                ins.then_inc(conv_done, 1)
                    if i >= 2:
                        j = i - 2
                        bank = get(("qkvP", j))
                        kept(dve.tensor_copy(qkv[:, 0:NP, 128 * j:128 * j + 128], bank[:, :].rearrange("p (t n) -> p t n", t=NP)))
                        bank = get(("qkvS", j))
                        kept(dve.tensor_copy(qkv[0:NS, NP, 128 * j:128 * j + 128], bank[0:NS, 0:128]))
                for i in range(3):
                    bank = get(("tail", i))
                    kept(dve.tensor_copy(tail_rows[:, 384 * i:384 * i + 384], bank[0:27, 0:384]))
                dve.wait_ge(tail_copied, NCT)
                for t in range(NT):
                    r = ROWS[t]
                    qk = qkv[0:r, t, 0:2 * CW]
                    sq = work[0:r, 0:2 * CW]
                    then(dve.tensor_tensor(sq, qk, qk, ALU.mult))
                    then(dve.tensor_reduce(l2[0:r, t, :], hd(sq, 12), AX, ALU.add))
                then(dve.tensor_scalar(l2, l2, EPS, None, ALU.add))
                inv_root(l2)
                then(dve.tensor_scalar(l2[:, :, 0:CH], l2[:, :, 0:CH], SCALE, None, ALU.mult))
                dve.wait_ge(act_drained, A_AT[("A", NT - 1, 1)] + 1)
                dve.tensor_copy(gates[:, 0:NP, :], proj[:, 0:NP, CB:CB + 12])
                dve.tensor_copy(gates[0:NS, NP, :], proj[0:NS, NP, CB:CB + 12]).then_inc(gate_asked, 1)
                dve.wait_ge(gate_asked, 1)
                dve.wait_ge(gate_got, 1)
                then(dve.tensor_scalar(beta, beta, 1.0, None, ALU.add))
                then(dve.reciprocal(beta, beta))
                then(dve.tensor_tensor(soft, gates[:, :, CH:2 * CH], mid(dt_bias, NT), ALU.add))
                dve.scalar_tensor_tensor(decay, soft, -1.0, soft, ALU.mult, ALU.max).then_inc(gate_asked, 1)
                dve.wait_ge(gate_got, 2)
                then(dve.scalar_tensor_tensor(soft, soft, 0.0, decay, ALU.max, ALU.add))
                then(dve.scalar_tensor_tensor(decay, soft, -1.0, mid(a_log, NT), ALU.mult, ALU.mult))
                dve.wait_ge(mlp_params, 48)
                for r, ts, n in groups:
                    v = proj[0:r, ts, AV:AV + AW]
                    mean, var, sq = ln_mean[0:r, ts], ln_var[0:r, ts], ln_sq[0:r, 0:n, :]
                    then(dve.tensor_reduce(mean, v, AX, ALU.add))
                    then(dve.tensor_scalar(mean, mean, 1.0 / AW, None, ALU.mult))
                    then(dve.tensor_tensor(v, v, inner(mean, AW), ALU.subtract))
                    then(dve.tensor_tensor(sq, v, v, ALU.mult))
                    then(dve.tensor_reduce(var, sq, AX, ALU.add))
                then(dve.tensor_scalar(ln_var, ln_var, 1.0 / AW, EPS, ALU.mult, ALU.add))
                inv_root(ln_var)
                for r, ts, n in groups:
                    v = proj[0:r, ts, AV:AV + AW]
                    then(dve.tensor_tensor(v, v, inner(ln_var[0:r, ts], AW), ALU.mult))
                    ins = dve.tensor_tensor(v, v, mid(v_gain[0:r, :], n), ALU.mult)
                    if r == 128:
                        then(ins)
                    else:
                        ins.then_inc(vn_ready, 1)
                bank = get(("wsT",))
                kept(dve.tensor_tensor(wsT, bank[:, :].rearrange("p (h n) -> p h n", h=AH), mid(const("upto"), AH), ALU.mult))
                bank = get(("rep",))
                kept(dve.tensor_copy(rep_w, bank[0:DS, 0:AH * NS]))
                bank = get(("ws4",))
                then(dve.tensor_tensor(ws4, bank[0:NS, 0:AH * NS].rearrange("p (h n) -> p h n", h=AH), mid(const("same4"), AH), ALU.mult))
                kept(dve.tensor_copy(bias_s[0:NS, :], bank[0:NS, 128:128 + AH]), ("ws4",))
                for t in range(NT):
                    bank = get(("gate", t))
                    r = ROWS[t]
                    bias = bias_p if t < NP else bias_s
                    for h in range(AH):
                        u = proj[0:r, t, AU + 64 * h:AU + 64 * h + 64]
                        ins = dve.scalar_tensor_tensor(u, bank[0:r, 64 * h:64 * h + 64], bias[0:r, h:h + 1], u, ALU.add, ALU.mult)
                    kept(ins)
                dve.wait_ge(act_drained, A_AT[("B", NT - 1, 1)] + 1)
                for r, ts, n in groups:
                    for t in range(ts.start, ts.stop):
                        heads = proj[0:r, t, BQ:BQ + 2 * BW].rearrange("p (h n) -> p h n", h=2 * BH)
                        x1, x2 = heads[:, :, 0:8], heads[:, :, 8:16]
                        cos = mid(const("cos")[0:r, 8 * t:8 * t + 8], 2 * BH)
                        sin = mid(const("sin")[0:r, 8 * t:8 * t + 8], 2 * BH)
                        tt = [b[0:r, 96 * (t % NP):96 * (t % NP) + 96].rearrange("p (h n) -> p h n", h=2 * BH) for b in rope_t]
                        dve.tensor_tensor(tt[0], x1, cos, ALU.mult)
                        dve.tensor_tensor(tt[1], x2, sin, ALU.mult)
                        dve.tensor_tensor(tt[2], x2, cos, ALU.mult)
                        then(dve.tensor_tensor(tt[3], x1, sin, ALU.mult))
                        dve.tensor_tensor(x1, tt[0], tt[1], ALU.subtract)
                        ins = dve.tensor_tensor(x2, tt[2], tt[3], ALU.add)
                        if t < NT - 1:
                            then(ins)
                        else:
                            ins.then_inc(rope_done, 1)
                dve.memset(state, 0.0)
                dve.wait_ge(act_drained, A_AT[("C", NT - 1, 1)] + 1)
                then(dve.memset(KZ_, 0.0))
                def side(t, point):
                    for n in beside(t, point):
                        j = n - 9
                        if 0 <= j < STEPS:
                            h, u = divmod(j, NP)
                            bank = get(("O", j))
                            dve.wait_ge(probs_ready, j + 1)
                            then(dve.reciprocal(a_sum[:, j:j + 1], a_sum[:, j:j + 1]))
                            kept(dve.tensor_scalar(proj[:, u, BQ + 64 * h:BQ + 64 * h + 64], bank[:, 0:64], a_sum[:, j:j + 1], None, ALU.mult))
                        j = n - 6
                        if 0 <= j < STEPS:
                            u = j % NP
                            keys = 128 * (u + 1)
                            if j >= 2:
                                dve.wait_ge(act_filled, A_AT[("P", j - 2)] + 1)
                            bank = get(("S", j))
                            kept(dve.tensor_tensor_reduce(prob[j % 2][:, 0:keys], bank[:, 0:keys], const("pmask")[:, 384 - 128 * u:512],
                                                          SCALE, -3e38, ALU.add, ALU.max, a_max[:, j:j + 1]), ("S", j))
                            dve.tensor_scalar(a_max[:, j:j + 1], a_max[:, j:j + 1], -1.0, None, ALU.mult).then_inc(probs_asked, 1)
                delta_prepare(dve, 0, then)
                for t in range(NT):
                    delta_vec(dve, t, then, get, kept, inv_root, lambda point, t=t: side(t, point) if t < NP else None)
                for G in range(2):
                    if G == 0:
                        then(dve.memset(qblk, 0.0))
                        dve.wait_ge(act_drained, A_AT[("bks", 2)] + 1)
                        for h in range(BH):
                            p = 64 * (h % 2)
                            ins = dve.tensor_copy(qblk[p:p + 64, :, h // 2, DS * h:DS * h + DS],
                                                  qTb[h // 2][p:p + 64, SEQ:NTOK].rearrange("p (b s) -> p b s", b=DB))
                        ins.then_inc(qblk_ready, 1)
                        delta_norm(dve, NP, then, inv_root)
                    for i, (name, c, cols) in enumerate((("sd", 0, 384), ("sr", 384, 512), ("sn", 896, 32))):
                        bank = get((name, G))
                        mask = const("smask")[:, c:c + cols] if i < 2 else const("smask")[:, 896 + 32 * G:928 + 32 * G]
                        kept(dve.tensor_tensor_reduce(sprob[:, c:c + cols], bank[:, 0:cols], mask, SCALE, -3e38, ALU.add, ALU.max,
                                                      s_max[:, i:i + 1]), (name, G))
                    then(dve.tensor_reduce(s_max[:, 3:4], s_max[:, 0:3], AX, ALU.max))
                    dve.tensor_scalar(s_max[:, 4:5], s_max[:, 3:4], -1.0, None, ALU.mult).then_inc(sprob_asked, 1)
                    dve.wait_ge(sprob_got, G + 1)
                    then(dve.reciprocal(s_sum[:, 1:2], s_sum[:, 0:1]))
                    dve.tensor_scalar(sprob, sprob, s_sum[:, 1:2], None, ALU.mult).then_inc(sprob_ready, 1)
                    for name, dst, rr, cols in (("pd", spd, NDIL, 512), ("pr", spr, 128, 512), ("pn", spn, NS, 128)):
                        bank = get((name, G))
                        kept(dve.tensor_copy(dst[0:rr, 0:cols], bank[0:rr, 0:cols]))
                    bank = get(("ov", G))
                    kept(dve.tensor_tensor(hd(own), hd(bank[:, 0:BW]), inner(const("ownhead"), HD), ALU.mult))
                    bank = get(("oT", G))
                    kept(dve.tensor_copy(o4T[:, :, 16 * G:16 * G + 16], bank[:, 0:48].rearrange("p (g n) -> p g n", g=3)))
                dve.wait_ge(vec_drained, V_AT[("oT", 1)] + 1)
                dve.tensor_copy(hT[:, 2:5, SEQ:NTOK], o4T).then_inc(mix_ready, 1)
                for c in range(2):
                    for t in range(NT):
                        bank = get(("out", c, t))
                        if t == NP:
                            for q in range(4):
                                xs = x[0:NS, NP, 512 * c + 128 * q:512 * c + 128 * q + 128]
                                ins = dve.tensor_tensor(xs, xs, bank[NS * q:NS * q + NS, 0:128], ALU.add)
                            kept(ins)
                            continue
                        xs = x[0:ROWS[t], t, 512 * c:512 * c + 512]
                        kept(dve.tensor_tensor(xs, xs, bank[0:ROWS[t], :], ALU.add))
                dve.wait_ge(squares_ready, NT)
                norm_scale()
                dve.wait_ge(pool_stored, (L + 1) * (16 * STORES))
                dve.sem_inc(aside, 1)
                for t in range(NT):
                    r = ROWS[t]
                    dve.tensor_scalar(h2[0:r, t, :], x[0:r, t, :], rstd[0:r, t:t + 1], None, ALU.mult).then_inc(rows_ready, 1)
                for t in range(NT):
                    for h in range(2):
                        gained(("norm2", t, h), t, h, g2)
                route(dve, then, get, kept)

                def expert(k, rnd):
                    jobs = rnd * (2 * EUN)
                    dve.wait_ge(vec_filled, jobs + (V0 + 2 * k + 1))
                    dve.tensor_tensor(rowsT[k % 2].rearrange("p (k n) -> p k n", k=KT),
                                      v_bank(V0 + 2 * k)[:, :].rearrange("p (k n) -> p k n", k=KT), inner(g2, CAP), ALU.mult).then_inc(vec_drained, 1)
                    dve.wait_ge(act_gated, rnd * EUN + (k + 1))
                    dve.tensor_tensor(hid[k % 2], gate_act[k % 2], v_bank(V0 + 2 * k + 1)[:, 128:256], ALU.mult).then_inc(vec_drained, 1)
                with dve.Fori(0, NE // EUN) as rnd:
                    for k in range(EUN):
                        expert(k, rnd)
                for k in range(NE - ELOOP):
                    expert(k, NE // EUN)
                per = ((NT + 1) // 2 * 16, NT // 2 * 16)
                for t in range(NT):
                    r = ROWS[t]
                    for k in range(2):
                        j = (t % 2) * 2 + k
                        dve.wait_ge(gathered[j], L * per[t % 2] + 16 * (t // 2 + 1))
                        w = (w0, w1_)[k][0:r, t:t + 1]
                        ins = dve.scalar_tensor_tensor(x[0:r, t, :], got[j][0:r, :], w, x[0:r, t, :], ALU.mult, ALU.add)
                        if k == 0:
                            then(ins)
                        elif t < NT - 1:
                            ins.then_inc(got_used, 1)
                        else:
                            ins.then_inc(moe_done, 1)
                dve.wait_ge(moe_done, 1)
                over = dve.value_load(idx_cnt[0:1, 0:1], min_val=0, max_val=NTOK)
                with dve.If(over > CAP):
                    dve.sem_inc(fb_added, 1)
                    with dve.Fori(0, NE) as e:
                        for f in range(2):
                            dve.wait_ge(fb_silu, e * 2 + (f + 1))
                            dve.tensor_tensor(fb_hid[:, f, 0:SEQ], fb_act[:, f, 0:SEQ], psum[2 * f + 1][:, :], ALU.mult)
                            dve.tensor_tensor(fb_hid[:, f, SEQ:NTOK], fb_act[:, f, SEQ:NTOK], psum[4 + f][:, 64:64 + NS],
                                              ALU.mult).then_inc(fb_prod, 1)
                        for t in range(NT):
                            r = ROWS[t]
                            dve.wait_ge(fb_down, e * NT + (t + 1))
                            for c in range(2):
                                xs = x[0:r, t, 512 * c:512 * c + 512]
                                ins = dve.scalar_tensor_tensor(xs, psum[6 + c][0:r, :], over_gate[0:r, t, bass.ds(e, 1)], xs, ALU.mult, ALU.add)
                            ins.then_inc(fb_added, 1)
                leave_layer(dve, L)
            dve.tensor_scalar(rstd, ssq, 1.0 / D, EPS, ALU.mult, ALU.add).then_inc(small_set, 1)
            dve.wait_ge(small_set, 2)
            dve.reciprocal(rstd, rstd).then_inc(fin_step, 1)
            dve.wait_ge(fin_step, 2)
            dve.wait_ge(fin_gain, 16)
            for t in range(NT):
                r = ROWS[t]
                dve.scalar_tensor_tensor(x[0:r, t, :], x[0:r, t, :], rstd[0:r, t:t + 1], g_final[0:r, :], ALU.mult, ALU.mult).then_inc(fin_row, 1)


_IN = ["x_prompt", "x_sample", "cache_win_k", "cache_win_v", "state_conv", "state_delta", "norm1_g", "w_in", "a_vnorm_g",
       "a_ws", "a_bs", "c_conv_w", "c_a_log", "c_dt_bias", "c_norm_g", "w_out", "norm2_g", "w_group", "w_router", "w1", "w3",
       "w2", "final_g"]
_OUT = [("y_prompt", (1, SEQ, D)), ("y_sample", (DB, DS, D)), ("win_k_prompt", (DEPTH, 1, SEQ, BH, HD)),
        ("win_v_prompt", (DEPTH, 1, SEQ, BH, HD)), ("conv_prompt", (DEPTH, 1, 3, CCH)), ("delta_prompt", (DEPTH, 1, CH, HD, HD)),
        ("win_k_sample", (DEPTH, DB, DS, BH, HD)), ("win_v_sample", (DEPTH, DB, DS, BH, HD)), ("chunk_v_sample", (DEPTH, DB, DS, AW)),
        ("conv_sample", (DEPTH, DB, 3, CCH)), ("delta_sample", (DEPTH, DB, CH, HD, HD))]


def kernel(**inputs):
    import concourse.bacc as bacc
    from concourse.bass_utils import run_bass_kernel_spmd as run

    nc = bacc.Bacc("TRN2", target_bir_lowering=False, num_devices=1)
    table, at = constants()
    arrays = {"in_" + k: np.ascontiguousarray(inputs[k]) for k in _IN}
    arrays["in_consts"] = table
    ins = {k[3:]: nc.dram_tensor(k, a.shape, F32, kind="ExternalInput").ap() for k, a in arrays.items()}
    outs = {k: nc.dram_tensor("out_" + k, shape, F32, kind="ExternalOutput").ap() for k, shape in _OUT}
    x_lists = nc.dram_tensor("x_lists", (NE * CAP + 2 * 128 * NT, D), F32, kind="Internal").ap()
    y_lists = nc.dram_tensor("y_lists", (NE * CAP, D), F32, kind="Internal").ap()
    build(nc, ins, outs, at, x_lists, y_lists)
    r = run(nc, [arrays], core_ids=[0])
    return tuple(r.results[0]["out_" + k] for k, _ in _OUT)
```
